# Optimizing a Trainium2 kernel written in Bass

```python
import jax, jax.numpy as jnp
from jax import lax
import numpy as np
import math

D_MODEL = 1024
BATCH = 1
SEQ = 256
DEPTH = 2

HEAD_DIM = 64
N_HEADS = 4
BRANCH_WIDTH = N_HEADS * HEAD_DIM
N_BRANCHES = 4
Q_BLOCK = 128
RMS_EPS = 1e-6

DSW_PATTERNS = ((128, 1), (512, 4), (2048, 16))

MLA_Q_RANK = 192
MLA_KV_RANK = 128
MLA_NOPE_DIM = 64
MLA_ROPE_DIM = 32
MLA_V_DIM = 64
ROPE_THETA = 10000.0

NSA_CMP_BLOCK = 32
NSA_CMP_STRIDE = 16
NSA_CMP_HIDDEN = 128
NSA_SEL_BLOCK = 64
NSA_TOP_N = 16
NSA_WINDOW = 512
NSA_KV_DIM = 64
NSA_FORCE_SCORE = 1e9

N_ALIBI_HEADS = 8

IN_SPLITS = (
    ("a_q", BRANCH_WIDTH), ("a_k", BRANCH_WIDTH), ("a_v", BRANCH_WIDTH), ("a_gate", BRANCH_WIDTH),
    ("b_cq", MLA_Q_RANK), ("b_ckv", MLA_KV_RANK), ("b_kpe", MLA_ROPE_DIM), ("b_gate", BRANCH_WIDTH),
    ("c_q", BRANCH_WIDTH), ("c_kc", NSA_KV_DIM), ("c_vc", NSA_KV_DIM), ("c_ks", NSA_KV_DIM),
    ("c_vs", NSA_KV_DIM), ("c_kw", NSA_KV_DIM), ("c_vw", NSA_KV_DIM), ("c_g", 3 * N_HEADS),
    ("c_gate", BRANCH_WIDTH),
    ("d_q", BRANCH_WIDTH), ("d_k", BRANCH_WIDTH), ("d_v", BRANCH_WIDTH), ("d_gate", BRANCH_WIDTH),
)
D_IN = sum(w for _, w in IN_SPLITS)


def rmsnorm(x, g):
    xf = x.astype(jnp.float32)
    y = xf * lax.rsqrt(jnp.mean(xf * xf, axis=-1, keepdims=True) + RMS_EPS)
    return (y * g.astype(jnp.float32)).astype(x.dtype)

def split_columns(p):
    out, off = {}, 0
    for name, w in IN_SPLITS:
        out[name] = p[..., off:off + w]
        off += w
    return out

def alibi_slopes():
    s = 2.0 ** (-8.0 * (np.arange(N_ALIBI_HEADS) + 1) / N_ALIBI_HEADS)
    s = jnp.asarray(s, jnp.float32)
    return s[0::2], s[1::2]

def masked_softmax(s, mask):
    s = jnp.where(mask, s, -jnp.inf)
    m = jnp.max(s, axis=-1, keepdims=True)
    m = jnp.where(jnp.isfinite(m), m, 0.0)
    e = jnp.exp(s - m)
    return e / jnp.maximum(jnp.sum(e, axis=-1, keepdims=True), 1e-30)

def sweep_query_blocks(block_fn, seq):
    out = lax.map(block_fn, jnp.arange(seq // Q_BLOCK))
    nq, b, tq, h, d = out.shape
    return jnp.swapaxes(out, 0, 1).reshape(b, nq * tq, h, d)

def rope(x, pos):
    half = x.shape[-1] // 2
    inv = ROPE_THETA ** (-jnp.arange(half, dtype=jnp.float32) / half)
    ang = pos.astype(jnp.float32)[:, None] * inv[None, :]
    cos, sin = jnp.cos(ang)[:, None, :], jnp.sin(ang)[:, None, :]
    xf = x.astype(jnp.float32)
    x1, x2 = xf[..., :half], xf[..., half:]
    return jnp.concatenate([x1 * cos - x2 * sin, x1 * sin + x2 * cos], axis=-1).astype(x.dtype)

def dilated_window_attention(q, k, v, slopes):
    B, S, H, Dh = q.shape
    scale = Dh ** -0.5

    def block(qb):
        t0 = qb * Q_BLOCK
        t = t0 + jnp.arange(Q_BLOCK)
        qblk = lax.dynamic_slice_in_dim(q, t0, Q_BLOCK, axis=1)
        outs, lses = [], []
        for window, dil in DSW_PATTERNS:
            dist = dil * jnp.arange(window // dil + 1)
            idx = t[:, None] - dist[None, :]
            valid = idx >= 0
            idxc = jnp.maximum(idx, 0)
            kg, vg = k[:, idxc], v[:, idxc]
            s = jnp.einsum('bqhd,bqjhd->bhqj', qblk, kg).astype(jnp.float32) * scale
            s = s - slopes[:, None, None] * dist.astype(jnp.float32)
            s = jnp.where(valid[None, None], s, -jnp.inf)
            lse = jax.nn.logsumexp(s, axis=-1)
            p = jnp.exp(s - lse[..., None])
            outs.append(jnp.einsum('bhqj,bqjhd->bqhd', p.astype(v.dtype), vg))
            lses.append(lse)
        w = jax.nn.softmax(jnp.stack(lses, axis=0), axis=0)
        o = 0.0
        for i in range(len(DSW_PATTERNS)):
            o = o + jnp.transpose(w[i], (0, 2, 1))[..., None].astype(v.dtype) * outs[i]
        return o

    return sweep_query_blocks(block, S)

def blocked_causal_softmax(q, k, v, scale):
    B, S, H, _ = q.shape
    kpos = jnp.arange(S)

    def block(qb):
        t0 = qb * Q_BLOCK
        t = t0 + jnp.arange(Q_BLOCK)
        qblk = lax.dynamic_slice_in_dim(q, t0, Q_BLOCK, axis=1)
        s = jnp.einsum('bqhd,bkhd->bhqk', qblk, k).astype(jnp.float32) * scale
        s = jnp.where(kpos[None, :] <= t[:, None], s, -jnp.inf)
        p = jax.nn.softmax(s, axis=-1)
        return jnp.einsum('bhqk,bkhd->bqhd', p.astype(v.dtype), v)

    return sweep_query_blocks(block, S)

def mla_attention(cq, ckv, kpe, q_norm_g, w_uq, kv_norm_g, w_ukv):
    B, S, _ = cq.shape
    pos = jnp.arange(S)
    q = (rmsnorm(cq, q_norm_g) @ w_uq).reshape(B, S, N_HEADS, MLA_NOPE_DIM + MLA_ROPE_DIM)
    q = jnp.concatenate([q[..., :MLA_NOPE_DIM], rope(q[..., MLA_NOPE_DIM:], pos)], axis=-1)
    kv = (rmsnorm(ckv, kv_norm_g) @ w_ukv).reshape(B, S, N_HEADS, MLA_NOPE_DIM + MLA_V_DIM)
    k_nope, v = kv[..., :MLA_NOPE_DIM], kv[..., MLA_NOPE_DIM:]
    k_pe = rope(kpe[:, :, None, :], pos)
    k = jnp.concatenate([k_nope, jnp.broadcast_to(k_pe, (B, S, N_HEADS, MLA_ROPE_DIM))], axis=-1)
    return blocked_causal_softmax(q, k, v, (MLA_NOPE_DIM + MLA_ROPE_DIM) ** -0.5)

def compress_blocks(tok, pos_emb, w1, b1, w2, b2):
    B, S, Dk = tok.shape
    n_cmp = (S - NSA_CMP_BLOCK) // NSA_CMP_STRIDE + 1
    idx = np.arange(n_cmp)[:, None] * NSA_CMP_STRIDE + np.arange(NSA_CMP_BLOCK)[None, :]
    blocks = tok[:, idx] + pos_emb
    hid = jax.nn.gelu(blocks.reshape(B, n_cmp, NSA_CMP_BLOCK * Dk) @ w1 + b1)
    return hid @ w2 + b2

def nsa_attention(q, kc, vc, ks, vs, kw, vw, gates, pos_emb, w1, b1, w2, b2, slopes):
    B, S, H, Dh = q.shape
    scale = Dh ** -0.5
    k_cmp = compress_blocks(kc, pos_emb[0], w1[0], b1[0], w2[0], b2[0])
    v_cmp = compress_blocks(vc, pos_emb[1], w1[1], b1[1], w2[1], b2[1])
    n_cmp = k_cmp.shape[1]
    cmp_end = jnp.arange(n_cmp) * NSA_CMP_STRIDE + NSA_CMP_BLOCK - 1
    n_sel = S // NSA_SEL_BLOCK
    top_n = min(NSA_TOP_N, n_sel)
    r_sel, r_cmp = NSA_SEL_BLOCK // NSA_CMP_STRIDE, NSA_CMP_BLOCK // NSA_CMP_STRIDE
    src = (jnp.arange(n_sel)[:, None, None] * r_sel - jnp.arange(r_sel)[None, :, None]
           - jnp.arange(r_cmp)[None, None, :]).reshape(n_sel, -1)
    sel_map = jnp.sum(src[..., None] == jnp.arange(n_cmp), axis=1).astype(jnp.float32)
    kw_pad = jnp.pad(kw, ((0, 0), (NSA_WINDOW, 0), (0, 0)))
    vw_pad = jnp.pad(vw, ((0, 0), (NSA_WINDOW, 0), (0, 0)))
    blk = jnp.arange(n_sel)
    sel_off = jnp.arange(NSA_SEL_BLOCK)

    def block(qb):
        t0 = qb * Q_BLOCK
        t = t0 + jnp.arange(Q_BLOCK)
        qblk = lax.dynamic_slice_in_dim(q, t0, Q_BLOCK, axis=1)
        gblk = lax.dynamic_slice_in_dim(gates, t0, Q_BLOCK, axis=1)
        dist_c = (t[:, None] - cmp_end[None, :]).astype(jnp.float32)
        s = jnp.einsum('bqhd,bnd->bhqn', qblk, k_cmp).astype(jnp.float32) * scale
        p_cmp = masked_softmax(s - slopes[:, None, None] * dist_c, dist_c >= 0)
        o_cmp = jnp.einsum('bhqn,bnd->bqhd', p_cmp.astype(v_cmp.dtype), v_cmp)
        p_sel = jnp.einsum('bhqn,jn->bqj', p_cmp, sel_map)
        cur = t // NSA_SEL_BLOCK
        valid = blk[None, :] * NSA_SEL_BLOCK <= t[:, None]
        forced = (blk[None, :] == 0) | (blk[None, :] == cur[:, None]) | (blk[None, :] == cur[:, None] - 1)
        score = jnp.where(valid, jnp.where(forced, NSA_FORCE_SCORE, p_sel), -jnp.inf)
        _, sel = lax.top_k(score, top_n)
        tok = (sel[..., None] * NSA_SEL_BLOCK + sel_off).reshape(B, Q_BLOCK, top_n * NSA_SEL_BLOCK)
        ks_g = jax.vmap(lambda a, i: a[i])(ks, tok)
        vs_g = jax.vmap(lambda a, i: a[i])(vs, tok)
        dist_s = (t[None, :, None] - tok).astype(jnp.float32)
        s = jnp.einsum('bqhd,bqkd->bhqk', qblk, ks_g).astype(jnp.float32) * scale
        s = s - slopes[None, :, None, None] * dist_s[:, None]
        p = masked_softmax(s, (dist_s >= 0)[:, None])
        o_slc = jnp.einsum('bhqk,bqkd->bqhd', p.astype(vs_g.dtype), vs_g)
        kwin = lax.dynamic_slice_in_dim(kw_pad, t0, Q_BLOCK + NSA_WINDOW, axis=1)
        vwin = lax.dynamic_slice_in_dim(vw_pad, t0, Q_BLOCK + NSA_WINDOW, axis=1)
        spos = t0 - NSA_WINDOW + jnp.arange(Q_BLOCK + NSA_WINDOW)
        dist_w = t[:, None] - spos[None, :]
        mask_w = (dist_w >= 0) & (dist_w < NSA_WINDOW) & (spos[None, :] >= 0)
        s = jnp.einsum('bqhd,bkd->bhqk', qblk, kwin).astype(jnp.float32) * scale
        p = masked_softmax(s - slopes[:, None, None] * dist_w.astype(jnp.float32), mask_w)
        o_win = jnp.einsum('bhqk,bkd->bqhd', p.astype(vwin.dtype), vwin)
        return gblk[..., 0:1] * o_cmp + gblk[..., 1:2] * o_slc + gblk[..., 2:3] * o_win

    return sweep_query_blocks(block, S)

def stick_breaking_attention(q, k, v):
    B, S, H, Dh = q.shape
    scale = Dh ** -0.5
    kpos = jnp.arange(S)

    def block(qb):
        t0 = qb * Q_BLOCK
        t = t0 + jnp.arange(Q_BLOCK)
        qblk = lax.dynamic_slice_in_dim(q, t0, Q_BLOCK, axis=1)
        z = jnp.einsum('bqhd,bkhd->bhqk', qblk, k).astype(jnp.float32) * scale
        mask = kpos[None, :] < t[:, None]
        log1m = jnp.where(mask, jax.nn.log_sigmoid(-z), 0.0)
        after = lax.cumsum(log1m, axis=3, reverse=True) - log1m
        a = jnp.where(mask, jnp.exp(jax.nn.log_sigmoid(z) + after), 0.0)
        return jnp.einsum('bhqk,bkhd->bqhd', a.astype(v.dtype), v)

    return sweep_query_blocks(block, S)

def first_inputs(seed: int = 0) -> dict:
    key = jax.random.key(seed)
    ks = jax.random.split(key, 18)
    f32 = jnp.float32

    def nrm(k, shape, fan_in):
        return jax.random.normal(k, shape, f32) * (fan_in ** -0.5)

    def gain(k, shape):
        return 1.0 + 0.05 * jax.random.normal(k, shape, f32)

    return {
        "x": jax.random.normal(ks[0], (BATCH, SEQ, D_MODEL), f32),
        "norm_g": gain(ks[1], (DEPTH, D_MODEL)),
        "w_in": nrm(ks[2], (DEPTH, D_MODEL, D_IN), D_MODEL),
        "mla_q_norm": gain(ks[3], (DEPTH, MLA_Q_RANK)),
        "mla_w_uq": nrm(ks[4], (DEPTH, MLA_Q_RANK, N_HEADS * (MLA_NOPE_DIM + MLA_ROPE_DIM)), MLA_Q_RANK),
        "mla_kv_norm": gain(ks[5], (DEPTH, MLA_KV_RANK)),
        "mla_w_ukv": nrm(ks[6], (DEPTH, MLA_KV_RANK, N_HEADS * (MLA_NOPE_DIM + MLA_V_DIM)), MLA_KV_RANK),
        "nsa_pos": 0.1 * jax.random.normal(ks[7], (DEPTH, 2, NSA_CMP_BLOCK, NSA_KV_DIM), f32),
        "nsa_w1": nrm(ks[8], (DEPTH, 2, NSA_CMP_BLOCK * NSA_KV_DIM, NSA_CMP_HIDDEN), NSA_CMP_BLOCK * NSA_KV_DIM),
        "nsa_b1": 0.02 * jax.random.normal(ks[9], (DEPTH, 2, NSA_CMP_HIDDEN), f32),
        "nsa_w2": nrm(ks[10], (DEPTH, 2, NSA_CMP_HIDDEN, NSA_KV_DIM), NSA_CMP_HIDDEN),
        "nsa_b2": 0.02 * jax.random.normal(ks[11], (DEPTH, 2, NSA_KV_DIM), f32),
        "w_branch": nrm(ks[12], (DEPTH, N_BRANCHES, BRANCH_WIDTH, D_MODEL), BRANCH_WIDTH),
        "w_merge": nrm(ks[13], (DEPTH, N_BRANCHES, D_MODEL, D_MODEL), D_MODEL),
        "b_merge": 0.02 * jax.random.normal(ks[14], (DEPTH, N_BRANCHES, D_MODEL), f32),
        "w_out": nrm(ks[15], (DEPTH, D_MODEL, D_MODEL), D_MODEL),
        "final_norm_g": gain(ks[16], (D_MODEL,)),
    }

def first_block(x, norm_g, w_in, mla_q_norm, mla_w_uq, mla_kv_norm, mla_w_ukv, nsa_pos, nsa_w1,
              nsa_b1, nsa_w2, nsa_b2, w_branch, w_merge, b_merge, w_out, final_norm_g):
    B, S, D = x.shape
    slopes_a, slopes_c = alibi_slopes()
    for l in range(DEPTH):
        h = rmsnorm(x, norm_g[l])
        c = split_columns(h @ w_in[l])
        heads = lambda a: a.reshape(B, S, N_HEADS, HEAD_DIM)
        flat = lambda a: a.reshape(B, S, BRANCH_WIDTH)
        y_a = flat(dilated_window_attention(heads(c["a_q"]), heads(c["a_k"]), heads(c["a_v"]), slopes_a))
        y_a = y_a * jax.nn.silu(c["a_gate"])
        y_b = flat(mla_attention(c["b_cq"], c["b_ckv"], c["b_kpe"], mla_q_norm[l], mla_w_uq[l],
                                 mla_kv_norm[l], mla_w_ukv[l]))
        y_b = y_b * jax.nn.silu(c["b_gate"])
        g_c = jax.nn.sigmoid(c["c_g"]).reshape(B, S, N_HEADS, 3)
        y_c = flat(nsa_attention(heads(c["c_q"]), c["c_kc"], c["c_vc"], c["c_ks"], c["c_vs"],
                                 c["c_kw"], c["c_vw"], g_c, nsa_pos[l], nsa_w1[l], nsa_b1[l],
                                 nsa_w2[l], nsa_b2[l], slopes_c))
        y_c = y_c * jax.nn.silu(c["c_gate"])
        y_d = flat(stick_breaking_attention(heads(c["d_q"]), heads(c["d_k"]), heads(c["d_v"])))
        y_d = y_d * jax.nn.silu(c["d_gate"])
        merged = 0.0
        for i, y in enumerate((y_a, y_b, y_c, y_d)):
            gate = jax.nn.sigmoid(h @ w_merge[l, i] + b_merge[l, i])
            merged = merged + gate * (y @ w_branch[l, i])
        x = x + merged @ w_out[l]
    return rmsnorm(x, final_norm_g)


N_MIXERS = 2
N_ATTN_LAYERS = (DEPTH + 1) // 2
N_RWKV_LAYERS = DEPTH // 2
DA_HEADS = 8
DA_HEAD_DIM = D_MODEL // (2 * DA_HEADS)
DA_QBLOCK = 128
RMS_EPS_2 = 1e-5
RW_HEAD = 64
RW_HEADS = D_MODEL // RW_HEAD
RW_DECAY_LORA = max(32, int(round(1.8 * D_MODEL ** 0.5 / 32)) * 32)
RW_AAA_LORA = max(32, int(round(1.8 * D_MODEL ** 0.5 / 32)) * 32)
RW_MV_LORA = max(32, int(round(1.3 * D_MODEL ** 0.5 / 32)) * 32)
RW_GATE_LORA = max(32, int(round(0.6 * D_MODEL ** 0.8 / 32)) * 32)
RW_GN_EPS = 64e-5
MOE_GROUPS = 4
MOE_EPG = 8
MOE_EXPERTS = MOE_GROUPS * MOE_EPG
MOE_TOPK = 2
MOE_HIDDEN = D_MODEL // 2
MOE_BLOCK = 128
DEEPNORM_ALPHA = (2 * DEPTH) ** 0.25
DEEPNORM_BETA = (8 * DEPTH) ** -0.25
LN_EPS = 1e-5


def layer_norm(x, g, b):
    xf = x.astype(jnp.float32)
    mu = jnp.mean(xf, -1, keepdims=True)
    var = jnp.mean(jnp.square(xf - mu), -1, keepdims=True)
    return ((xf - mu) * lax.rsqrt(var + LN_EPS) * g + b).astype(x.dtype)

def diff_attention(x, w_qkv, w_o, lam, subln_g, lambda_init):
    B, S, _ = x.shape
    q, k, v = jnp.split(x @ w_qkv, 3, axis=-1)
    q = q.reshape(B, S, DA_HEADS, 2, DA_HEAD_DIM)
    k = k.reshape(B, S, DA_HEADS, 2, DA_HEAD_DIM)
    v = v.reshape(B, S, DA_HEADS, 2 * DA_HEAD_DIM)
    lamf = lam.astype(jnp.float32)
    lam_full = jnp.exp(jnp.sum(lamf[0] * lamf[1])) - jnp.exp(jnp.sum(lamf[2] * lamf[3])) + lambda_init
    n_blk = S // DA_QBLOCK
    q_blocks = jnp.moveaxis(q.reshape(B, n_blk, DA_QBLOCK, DA_HEADS, 2, DA_HEAD_DIM), 1, 0)
    k_pos = jnp.arange(S)
    scale = DA_HEAD_DIM ** -0.5

    def one_block(args):
        q_blk, blk = args
        s = jnp.einsum('bqhcd,bkhcd->bhcqk', q_blk, k).astype(jnp.float32) * scale
        q_pos = blk * DA_QBLOCK + jnp.arange(DA_QBLOCK)
        causal = k_pos[None, :] <= q_pos[:, None]
        p = jax.nn.softmax(jnp.where(causal, s, -jnp.inf), axis=-1)
        attn = p[:, :, 0] - lam_full * p[:, :, 1]
        return jnp.einsum('bhqk,bkhe->bqhe', attn.astype(v.dtype), v)

    o = lax.map(one_block, (q_blocks, jnp.arange(n_blk)))
    o = jnp.moveaxis(o, 0, 1).reshape(B, S, DA_HEADS, 2 * DA_HEAD_DIM).astype(jnp.float32)
    o = o * lax.rsqrt(jnp.mean(o * o, -1, keepdims=True) + RMS_EPS_2) * subln_g * (1.0 - lambda_init)
    return o.reshape(B, S, D_MODEL).astype(x.dtype) @ w_o

def wkv7_scan(r, decay, k, v, a_vec, b_vec):
    B, S, H, N = r.shape

    def step(state, inp):
        r_t, w_t, k_t, v_t, a_t, b_t = inp
        sa = jnp.einsum('bhij,bhj->bhi', state, a_t)
        state = (state * w_t[:, :, None, :] + sa[..., None] * b_t[:, :, None, :]
                 + v_t[..., None] * k_t[:, :, None, :])
        return state, jnp.einsum('bhij,bhj->bhi', state, r_t)

    xs = tuple(jnp.moveaxis(t, 1, 0) for t in (r, decay, k, v, a_vec, b_vec))
    _, ys = lax.scan(step, jnp.zeros((B, H, N, N), jnp.float32), xs)
    return jnp.moveaxis(ys, 0, 1)

def rwkv7_time_mix(x, mu, w_rkv, w_o, w0, w1, w2, a0, a1, a2, g1, g2, k_k, k_a, r_k,
                   lnx_g, lnx_b, v_first, value_mix):
    B, S, D = x.shape
    H, N = RW_HEADS, RW_HEAD
    xx = jnp.pad(x, ((0, 0), (1, 0), (0, 0)))[:, :-1] - x
    xm = x[None] + xx[None] * mu[:, None, None, :]
    r, k, v = jnp.einsum('nbsd,nde->nbse', xm[:3], w_rkv)
    xv, xw, xa, xg = xm[2], xm[3], xm[4], xm[5]
    w = -jax.nn.softplus(-(w0 + jnp.tanh(xw @ w1) @ w2)) - 0.5
    if value_mix is None:
        v_first = v
    else:
        v0, v1, v2 = value_mix
        v = v + (v_first - v) * jax.nn.sigmoid(v0 + (xv @ v1) @ v2)
    a = jax.nn.sigmoid(a0 + (xa @ a1) @ a2)
    g = jax.nn.sigmoid(xg @ g1) @ g2
    kk = (k * k_k).reshape(B, S, H, N).astype(jnp.float32)
    kk = kk / jnp.maximum(jnp.sqrt(jnp.sum(kk * kk, -1, keepdims=True)), 1e-12)
    k = k * (1.0 + (a - 1.0) * k_a)
    rh, kh, vh, ah = [t.reshape(B, S, H, N).astype(jnp.float32) for t in (r, k, v, a)]
    decay = jnp.exp(-jnp.exp(w.reshape(B, S, H, N).astype(jnp.float32)))
    y = wkv7_scan(rh, decay, kh, vh, -kk, kk * ah)
    ym = jnp.mean(y, -1, keepdims=True)
    yv = jnp.mean(jnp.square(y - ym), -1, keepdims=True)
    y = (y - ym) * lax.rsqrt(yv + RW_GN_EPS) * lnx_g.reshape(H, N) + lnx_b.reshape(H, N)
    y = y + jnp.sum(rh * kh * r_k, -1, keepdims=True) * vh
    out = (y.reshape(B, S, D).astype(x.dtype) * g) @ w_o
    return out, v_first

def hier_moe(x, rg_w, rg_b, re_w, re_b, w_gu, w_down):
    B, S, D = x.shape
    n_tok = B * S
    t = x.reshape(n_tok, D)
    g_prob = jax.nn.softmax((t @ rg_w + rg_b).astype(jnp.float32), axis=-1)
    g_p, g_idx = lax.top_k(g_prob, 1)
    e_logits = (t @ re_w + re_b).astype(jnp.float32).reshape(n_tok, MOE_GROUPS, MOE_EPG)
    e_logits = jnp.take_along_axis(e_logits, g_idx[:, :, None], axis=1)[:, 0]
    e_p, e_idx = lax.top_k(jax.nn.softmax(e_logits, axis=-1), MOE_TOPK)
    e_p = e_p / jnp.sum(e_p, -1, keepdims=True)
    gate = (g_p * e_p).reshape(-1)
    expert = (g_idx * MOE_EPG + e_idx).reshape(-1).astype(jnp.int32)
    tok = jnp.repeat(jnp.arange(n_tok, dtype=jnp.int32), MOE_TOPK)
    n_assign = n_tok * MOE_TOPK
    order = jnp.argsort(expert)
    e_sorted, tok_sorted, gate_sorted = expert[order], tok[order], gate[order]
    counts = jnp.bincount(expert, length=MOE_EXPERTS).astype(jnp.int32)
    padded = (counts + MOE_BLOCK - 1) // MOE_BLOCK * MOE_BLOCK
    pad_end = jnp.cumsum(padded)
    pad_start = pad_end - padded
    start = jnp.cumsum(counts) - counts
    dest = pad_start[e_sorted] + jnp.arange(n_assign, dtype=jnp.int32) - start[e_sorted]
    n_blocks = -(-n_assign // MOE_BLOCK) + MOE_EXPERTS
    n_rows = n_blocks * MOE_BLOCK
    tok_buf = jnp.full((n_rows,), n_tok, jnp.int32).at[dest].set(tok_sorted)
    gate_buf = jnp.zeros((n_rows,), jnp.float32).at[dest].set(gate_sorted)
    t_pad = jnp.concatenate([t, jnp.zeros((1, D), t.dtype)], axis=0)
    x_buf = t_pad[tok_buf].reshape(n_blocks, MOE_BLOCK, D)
    block_e = jnp.minimum(jnp.searchsorted(pad_end, jnp.arange(n_blocks) * MOE_BLOCK, side='right'),
                          MOE_EXPERTS - 1)

    def expert_block(args):
        xb, e = args
        hg, hu = jnp.split(xb @ w_gu[e], 2, axis=-1)
        return (jax.nn.silu(hg) * hu) @ w_down[e]

    y = lax.map(expert_block, (x_buf, block_e)).reshape(n_rows, D)
    y = y * gate_buf[:, None].astype(y.dtype)
    out = jax.ops.segment_sum(y, tok_buf, num_segments=n_tok + 1)[:n_tok]
    return out.reshape(B, S, D)

def second_inputs(seed: int = 0) -> dict:
    key = jax.random.key(seed)
    k = jax.random.split(key, 34)
    D, L, NA, NR = D_MODEL, DEPTH, N_ATTN_LAYERS, N_RWKV_LAYERS
    H, N = RW_HEADS, RW_HEAD
    f32 = jnp.float32

    def nrm(i, shape, scale):
        return scale * jax.random.normal(k[i], shape, f32)

    def unif(i, shape, lo, hi):
        return jax.random.uniform(k[i], shape, f32, lo, hi)

    return {
        'x': nrm(0, (BATCH, SEQ, D), 1.0),
        'ln1_g': 1.0 + nrm(1, (L, D), 0.02),
        'ln1_b': nrm(2, (L, D), 0.02),
        'ln2_g': 1.0 + nrm(3, (L, D), 0.02),
        'ln2_b': nrm(4, (L, D), 0.02),
        'attn_w_qkv': nrm(5, (NA, D, 3 * D), D ** -0.5),
        'attn_w_o': nrm(6, (NA, D, D), DEEPNORM_BETA * D ** -0.5),
        'attn_lambda': nrm(7, (NA, 4, DA_HEAD_DIM), 0.1),
        'attn_subln_g': 1.0 + nrm(8, (NA, 2 * DA_HEAD_DIM), 0.02),
        'rw_mu': unif(9, (NR, 6, D), 0.0, 1.0),
        'rw_w_rkv': nrm(10, (NR, 3, D, D), D ** -0.5),
        'rw_w_o': nrm(11, (NR, D, D), DEEPNORM_BETA * D ** -0.5),
        'rw_w0': unif(12, (NR, D), -6.0, -1.0),
        'rw_w1': nrm(13, (NR, D, RW_DECAY_LORA), D ** -0.5),
        'rw_w2': nrm(14, (NR, RW_DECAY_LORA, D), 0.1 * RW_DECAY_LORA ** -0.5),
        'rw_a0': nrm(15, (NR, D), 0.1),
        'rw_a1': nrm(16, (NR, D, RW_AAA_LORA), D ** -0.5),
        'rw_a2': nrm(17, (NR, RW_AAA_LORA, D), 0.5 * RW_AAA_LORA ** -0.5),
        'rw_g1': nrm(18, (NR, D, RW_GATE_LORA), D ** -0.5),
        'rw_g2': nrm(19, (NR, RW_GATE_LORA, D), RW_GATE_LORA ** -0.5),
        'rw_k_k': 0.85 + nrm(20, (NR, D), 0.02),
        'rw_k_a': 1.0 + nrm(21, (NR, D), 0.02),
        'rw_r_k': nrm(22, (NR, H, N), 0.1),
        'rw_lnx_g': 1.0 + nrm(23, (NR, D), 0.02),
        'rw_lnx_b': nrm(24, (NR, D), 0.02),
        'rw_v0': 1.0 + nrm(25, (NR - 1, D), 0.1),
        'rw_v1': nrm(26, (NR - 1, D, RW_MV_LORA), D ** -0.5),
        'rw_v2': nrm(27, (NR - 1, RW_MV_LORA, D), 0.5 * RW_MV_LORA ** -0.5),
        'moe_rg_w': nrm(28, (L, D, MOE_GROUPS), D ** -0.5),
        'moe_rg_b': nrm(29, (L, MOE_GROUPS), 0.01),
        'moe_re_w': nrm(30, (L, D, MOE_EXPERTS), D ** -0.5),
        'moe_re_b': nrm(31, (L, MOE_EXPERTS), 0.01),
        'moe_w_gu': nrm(32, (L, MOE_EXPERTS, D, 2 * MOE_HIDDEN), D ** -0.5),
        'moe_w_down': nrm(33, (L, MOE_EXPERTS, MOE_HIDDEN, D), DEEPNORM_BETA * MOE_HIDDEN ** -0.5),
    }

def second_block(x, ln1_g, ln1_b, ln2_g, ln2_b, attn_w_qkv, attn_w_o, attn_lambda, attn_subln_g,
              rw_mu, rw_w_rkv, rw_w_o, rw_w0, rw_w1, rw_w2, rw_a0, rw_a1, rw_a2, rw_g1, rw_g2,
              rw_k_k, rw_k_a, rw_r_k, rw_lnx_g, rw_lnx_b, rw_v0, rw_v1, rw_v2,
              moe_rg_w, moe_rg_b, moe_re_w, moe_re_b, moe_w_gu, moe_w_down):
    v_first = None
    for i in range(DEPTH):
        j = i // N_MIXERS
        if i % N_MIXERS == 0:
            lambda_init = 0.8 - 0.6 * math.exp(-0.3 * i)
            h = diff_attention(x, attn_w_qkv[j], attn_w_o[j], attn_lambda[j], attn_subln_g[j], lambda_init)
        else:
            value_mix = None if j == 0 else (rw_v0[j - 1], rw_v1[j - 1], rw_v2[j - 1])
            h, v_first = rwkv7_time_mix(x, rw_mu[j], rw_w_rkv[j], rw_w_o[j], rw_w0[j], rw_w1[j], rw_w2[j],
                                        rw_a0[j], rw_a1[j], rw_a2[j], rw_g1[j], rw_g2[j], rw_k_k[j],
                                        rw_k_a[j], rw_r_k[j], rw_lnx_g[j], rw_lnx_b[j], v_first, value_mix)
        x = layer_norm(DEEPNORM_ALPHA * x + h, ln1_g[i], ln1_b[i])
        f = hier_moe(x, moe_rg_w[i], moe_rg_b[i], moe_re_w[i], moe_re_b[i], moe_w_gu[i], moe_w_down[i])
        x = layer_norm(DEEPNORM_ALPHA * x + f, ln2_g[i], ln2_b[i])
    return x


def setup_inputs(seed=0):
    out = dict(first_inputs(seed))
    for name, value in second_inputs(seed + 1).items():
        if name != "x":
            out[name + "_2"] = value
    return out


def reference(
    x, norm_g, w_in, mla_q_norm, mla_w_uq, mla_kv_norm, mla_w_ukv, nsa_pos, nsa_w1, nsa_b1,
    nsa_w2, nsa_b2, w_branch, w_merge, b_merge, w_out, final_norm_g, ln1_g_2, ln1_b_2, ln2_g_2,
    ln2_b_2, attn_w_qkv_2, attn_w_o_2, attn_lambda_2, attn_subln_g_2, rw_mu_2, rw_w_rkv_2,
    rw_w_o_2, rw_w0_2, rw_w1_2, rw_w2_2, rw_a0_2, rw_a1_2, rw_a2_2, rw_g1_2, rw_g2_2, rw_k_k_2,
    rw_k_a_2, rw_r_k_2, rw_lnx_g_2, rw_lnx_b_2, rw_v0_2, rw_v1_2, rw_v2_2, moe_rg_w_2,
    moe_rg_b_2, moe_re_w_2, moe_re_b_2, moe_w_gu_2, moe_w_down_2,
):
    x = first_block(
        x, norm_g, w_in, mla_q_norm, mla_w_uq, mla_kv_norm, mla_w_ukv, nsa_pos, nsa_w1, nsa_b1,
        nsa_w2, nsa_b2, w_branch, w_merge, b_merge, w_out, final_norm_g,
    )
    return second_block(
        x, ln1_g_2, ln1_b_2, ln2_g_2, ln2_b_2, attn_w_qkv_2, attn_w_o_2, attn_lambda_2,
        attn_subln_g_2, rw_mu_2, rw_w_rkv_2, rw_w_o_2, rw_w0_2, rw_w1_2, rw_w2_2, rw_a0_2,
        rw_a1_2, rw_a2_2, rw_g1_2, rw_g2_2, rw_k_k_2, rw_k_a_2, rw_r_k_2, rw_lnx_g_2,
        rw_lnx_b_2, rw_v0_2, rw_v1_2, rw_v2_2, moe_rg_w_2, moe_rg_b_2, moe_re_w_2, moe_re_b_2,
        moe_w_gu_2, moe_w_down_2,
    )


_drawn_inputs = setup_inputs


def setup_inputs(seed=0):
    import zlib

    import numpy as np

    out = dict(_drawn_inputs(seed))
    spreads = {}
    factors = {'mla_q_norm': 7.563,
     'mla_kv_norm': 4.418,
     'nsa_b1': 8.0,
     'nsa_b2': 6.786,
     'b_merge': 8.0,
     'attn_subln_g_2': 6.259,
     'rw_w1_2': 8.0,
     'rw_w2_2': 8.0,
     'rw_a0_2': 5.66,
     'rw_k_k_2': 8.0,
     'rw_k_a_2': 7.034,
     'rw_lnx_g_2': 22.492,
     'rw_lnx_b_2': 24.318,
     'moe_rg_b_2': 8.0,
     'moe_re_b_2': 8.0}
    for name, (base, spread) in spreads.items():
        noise = np.random.default_rng([zlib.crc32(name.encode()), seed]).standard_normal(out[name].shape)
        drawn = base * np.exp(spread * noise) if base else spread * noise
        out[name] = __import__('jax').numpy.asarray(drawn.astype(out[name].dtype))
    for name, factor in factors.items():
        out[name] = (out[name] * factor).astype(out[name].dtype)
    return out
```

```python
import math
from contextlib import ExitStack

import numpy as np
import concourse.bass as bass
from concourse import mybir

F = mybir.dt.float32
ALU = mybir.AluOpType
ACT = mybir.ActivationFunctionType
AX = mybir.AxisListType.X
ADD, SUB, MUL, MAX, MIN = ALU.add, ALU.subtract, ALU.mult, ALU.max, ALU.min

P = 128
S = 256
D = 1024
NT = 2
KT = 8
L1 = 2
RING = 4
MORE = 2
CAP = 64
SLOT = 4096
NEG = -1e30
E = 32
ALPHA = 4.0 ** 0.25
HORD = (0, 2, 1, 3)


def tables():
    s = 2.0 ** -(np.arange(8) + 1.0)
    sl_a, sl_c = s[0::2], s[1::2]
    t = np.arange(S)
    dist = t[:, None] - t[None, :]
    cnt = np.zeros((S, S))
    for win, dil in ((128, 1), (512, 4), (2048, 16)):
        cnt += (dist >= 0) & (dist % dil == 0) & (dist <= win)
    lc = np.where(cnt > 0, np.log(np.maximum(cnt, 1)), NEG)
    causal = np.where(dist >= 0, 0.0, NEG)
    out = {}

    def per_tile(name, full):
        for tt in range(NT):
            w = P * (tt + 1)
            out[f"{name}{tt}"] = full[:, tt * P:(tt + 1) * P, :w].transpose(1, 0, 2).reshape(P, 4 * w)

    per_tile("ba", np.stack([np.where(cnt > 0, lc - sl_a[h] * dist, NEG) for h in HORD]))
    per_tile("bc", np.stack([np.where(dist >= 0, -sl_c[h] * dist, NEG) for h in HORD]))
    per_tile("cz", np.stack([causal] * 4))
    dc = t[:, None] - (np.arange(15) * 16 + 31)[None, :]
    cmp_b = np.full((NT, P, 4, 32), NEG)
    for u, h in enumerate(HORD):
        b = np.where(dc >= 0, -sl_c[h] * dc, NEG)
        cmp_b[:, :, u, :15] = b.reshape(NT, P, 15)
    for tt in range(NT):
        out[f"cm{tt}"] = cmp_b[tt].reshape(P, 128)
    strict = (t[:, None] < t[None, :]).astype(np.float64)
    out["st0"] = strict[:P, :]
    out["st1"] = strict[P:, P:]
    inv = 10000.0 ** (-np.arange(16) / 16.0)
    ang = (t[:, None] * inv[None, :]).reshape(NT, P, 16)
    for name, f in (("cos", np.cos), ("sin", np.sin)):
        v = f(ang).transpose(1, 0, 2)
        v = np.repeat(v[:, :, None, :], 4, axis=2).reshape(P, 8, 16)
        out[name] = np.concatenate([v, v], axis=1).reshape(P, 256)
    out["idn"] = np.eye(P)
    i = np.arange(P)
    out["upp"] = (i[:, None] > i[None, :]).astype(float)
    out["one"] = np.ones((P, P))
    out["blk"] = (i[:, None] // 64 == i[None, :] // 64).astype(float)
    out["hnd"] = (i[:, None] // 64 == np.arange(2)[None, :]).astype(float)
    a, b = i[:, None] % 64, np.arange(64)[None, :]
    out["mlt"] = (a < b).astype(float)
    out["mle"] = (a <= b).astype(float)
    out["m16"] = ((a < b) & (a // 16 == b // 16)).astype(float)
    out["n16"] = ((a > b) & (a // 16 == b // 16)).astype(float)
    out["m32"] = ((a < b) & (a // 16 != b // 16) & (a // 32 == b // 32)).astype(float)
    out["n32"] = ((a > b) & (a // 16 != b // 16) & (a // 32 == b // 32)).astype(float)
    out["m64"] = ((a < b) & (a // 32 != b // 32)).astype(float)
    out["n64"] = ((a > b) & (a // 32 != b // 32)).astype(float)
    out["mgt"] = (a > b).astype(float)
    out["i64"] = (a == b).astype(float)
    out["iog"] = np.tile(np.arange(4.0), (P, 1))
    out["ios"] = np.tile(np.arange(64.0), (P, 1))
    out["ioe"] = np.tile(np.arange(32.0), (P, 1))
    out["rst"] = np.tile((np.arange(S) % 64 != 0).astype(float), (P, 1))
    return {k: np.ascontiguousarray(v, np.float32) for k, v in out.items()}


FIRST_TABLES = ("ba0", "ba1", "bc0", "bc1", "cm0", "cm1", "st0", "cos", "sin", "upp")


class Queue:

    def __init__(self, name, sem, chained):
        self.name, self.sem, self.chained = name, sem, chained
        self.items, self.n, self.first = [], 0, []

    def add(self, fn, waits=(), inc=1, chain=None):
        waits = list(waits) + self.first
        self.first = []
        if (self.chained if chain is None else chain) and self.n:
            waits.append((self.sem, self.n))
        self.items.append((fn, waits, self.sem if inc else None, 1))
        self.n += 1 if inc else 0
        return (self.sem, self.n)

    def dma(self, out, in_, sem, waits=()):
        self.items.append((lambda e: e.dma_start(out, in_), list(waits) + self.first, sem, 16))
        self.first = []

    def last(self):
        return (self.sem, self.n)

    def ago(self, k):
        return (self.sem, self.n - k)

    def wait_for(self, eng, waits, seen):
        for w in waits:
            w = w() if callable(w) else w
            if w is None:
                continue
            s, v = w
            if v > seen.get(id(s), 0) and not (s is self.sem and not self.chained):
                eng.wait_ge(s, v)
                seen[id(s)] = v

    def split(self, flag, waits):
        self.outer, self.n0 = self.items, self.n
        self.items = []
        self.fl = (flag, list(waits) + self.first)
        self.first = []

    def other(self):
        self.yes, self.n1 = self.items, self.n
        self.items, self.n = [], self.n0

    def join(self):
        assert self.n == self.n1, (self.name, self.n - self.n0, self.n1 - self.n0)
        self.outer.append((self.fl[0], self.fl[1], (self.yes, self.items), None))
        self.items = self.outer

    def emit(self, eng, items=None, seen=None):
        seen = {} if seen is None else seen
        for fn, waits, sem, by in self.items if items is None else items:
            self.wait_for(eng, waits, seen)
            if by is None:
                flag = eng.value_load(fn, min_val=0, max_val=1)
                a, b = dict(seen), dict(seen)
                with eng.If(flag != 0):
                    self.emit(eng, sem[0], a)
                with eng.Else():
                    self.emit(eng, sem[1], b)
                seen.update({k: min(a[k], b[k]) for k in a if k in b})
                continue
            ins = fn(eng)
            if sem is not None:
                ins.then_inc(sem, by)


class Chunk:

    def __init__(self, ap, tok):
        self.ap, self.tok, self.free = ap, tok, None


def program(nc, T, out, stop=None, dump=None):
    tabs = tables()
    with ExitStack() as ctx:
        def sb(name, w, parts=P):
            return ctx.enter_context(nc.sbuf_tensor(name, [parts, w], F))[:, :]

        def sem(name):
            return ctx.enter_context(nc.semaphore(name))

        V = Queue("vector", sem("sv"), True)
        A = Queue("scalar", sem("sa"), True)
        G = Queue("gpsimd", sem("sg"), True)
        M = Queue("tensor", sem("sm"), False)
        W = Queue("sync", sem("sw"), False)
        queues = (V, A, G, M, W)

        psum = [ctx.enter_context(nc.psum_tensor(f"ps{i}", [P, 1024], F))[:, :] for i in range(4)]
        pfree = [[] for _ in range(4)]
        pnext = [0]

        def ps():
            i = pnext[0] % 4
            pnext[0] += 1
            return i, psum[i]

        def tt(q, o, a, b, op, *w, **k):
            return q.add(lambda e: e.tensor_tensor(o, a, b, op), w, **k)

        def ts(q, o, a, s1, s2, op0, op1, *w, **k):
            if op1 is None:
                return q.add(lambda e: e.tensor_scalar(o, a, s1, None, op0), w, **k)
            return q.add(lambda e: e.tensor_scalar(o, a, s1, s2, op0, op1), w, **k)

        def stt(o, a, s, b, op0, op1, *w, **k):
            return V.add(lambda e: e.scalar_tensor_tensor(out=o, in0=a, scalar=s, in1=b, op0=op0, op1=op1), w, **k)

        def red(o, a, op, *w, **k):
            return V.add(lambda e: e.tensor_reduce(o, a, AX, op), w, **k)

        def rec(o, a, *w, **k):
            return V.add(lambda e: e.reciprocal(o, a), w, **k)

        def cp(q, o, a, *w, **k):
            if q is A:
                return q.add(lambda e: e.activation(o, a, ACT.Copy), w, **k)
            return q.add(lambda e: e.tensor_copy(o, a), w, **k)

        def act(o, a, f, *w, bias=None, scale=1.0, acc=None, **k):
            kw = {"scale": scale}
            if bias is not None:
                kw["bias"] = bias
            if acc is not None:
                kw["accum_out"] = acc
            return A.add(lambda e: e.activation(o, a, f, **kw), w, **k)

        def ms(q, o, v, *w):
            return q.add(lambda e: e.memset(o, v), w)

        def mm(lst, *w):
            tok = None
            for n, (o, l, r, s0, s1) in enumerate(lst):
                end = n == len(lst) - 1
                tok = M.add(lambda e, o=o, l=l, r=r, s0=s0, s1=s1:
                            e.matmul(o, l, r, start=s0, stop=s1, skip_group_check=True),
                            w if n == 0 else (), inc=1 if end else 0)
            return tok

        def tr(lst, *w):
            tok = None
            for n, (o, i, idt) in enumerate(lst):
                end = n == len(lst) - 1
                tok = M.add(lambda e, o=o, i=i, idt=idt: e.transpose(o, i, idt), w if n == 0 else (),
                            inc=1 if end else 0)
            return tok

        def barrier():
            toks = [q.last() for q in queues if q.n and q is not W]
            for q in (V, A, G, M):
                q.first += [t for t in toks if t[0] is not q.sem]

        def bc(ap, shape):
            return ap.to_broadcast(shape)

        ring = [sb(f"ring{i}", SLOT) for i in range(RING)]
        rsem = [sem(f"sr{i}") for i in range(RING + MORE)]
        rcount = [0] * (RING + MORE)
        rwait = [None] * (RING + MORE)
        order = list(range(RING))

        def lend(aps, waits):
            for m, ap in enumerate(aps):
                ring.append(ap)
                rwait[RING + m] = list(waits)
                order.insert(0, RING + m)

        def give_back():
            del ring[RING:]
            order[:] = [k for k in order if k < RING]

        def load(*parts):
            k = order.pop(0)
            order.append(k)
            old = rwait[k]
            for j, (dst, src) in enumerate(parts):
                waits = []
                if j == 0 and old is not None:
                    waits = old if isinstance(old, list) else [lambda: old.free]
                W.dma(dst(ring[k]), src, rsem[k], waits)
                rcount[k] += 16
            rwait[k] = c = Chunk(ring[k], (rsem[k], rcount[k]))
            return c

        def cols(w, kt=KT):
            return lambda s: s[:, 0:kt * w].rearrange("p (k n) -> p k n", k=kt)

        def wsrc(ap, c0, w):
            return ap.rearrange("(k p) n -> p k n", p=P)[:, :, c0:c0 + w]

        def load_cols(ap, c0, w):
            c = load((cols(w, ap.shape[0] // P), wsrc(ap, c0, w)))
            c.v = c.ap[:, 0:ap.shape[0] // P * w].rearrange("p (k n) -> p k n", n=w)
            return c

        x = sb("x", 2 * D).rearrange("p (t d) -> p t d", t=NT)
        hb = sb("hb", 2 * D).rearrange("p (t d) -> p t d", t=NT)
        hT = sb("hT", 2 * D).rearrange("p (k s) -> p k s", k=KT)
        mT = sb("mT", 2 * D).rearrange("p (k s) -> p k s", k=KT)
        small = sb("small", 256)
        arena = sb("arena", 21900)
        apos = [0]

        def carve(w):
            a = arena[:, apos[0]:apos[0] + w]
            apos[0] += w
            assert apos[0] <= 21900, apos[0]
            return a

        s_c = sem("s_c")
        nload = [0]

        def start_load(dst, src):
            A.dma(dst, src, s_c)
            nload[0] += 16

        tab = {}
        common = [k for k in tabs if k not in FIRST_TABLES and k[0:2] != "cz"]
        wc = sum(tabs[k].shape[1] for k in common)
        tcom = sb("tcom", wc)
        o = 0
        for k in common:
            tab[k] = tcom[:, o:o + tabs[k].shape[1]]
            o += tabs[k].shape[1]
        for tt_ in range(NT):
            tab[f"cz{tt_}"] = sb(f"cz{tt_}", tabs[f"cz{tt_}"].shape[1])
        vec = sb("vec", T["vecs"].shape[1])
        row = sb("row", T["rows"].shape[1])
        rw36 = sb("rw36", 2 * KT * 36).rearrange("p (l k n) -> p l k n", l=2, k=KT)
        lnr = [sb(f"lnr{i}", 2 * D).rearrange("p (a d) -> p a d", a=2) for i in range(1)]
        s_ln = [sem(f"s_ln{i}") for i in range(1)]
        nln = [0]
        lnfree = [None]

        def rows_in(i):
            w = [lnfree[0]] if lnfree[0] else []
            G.dma(lnr[0], T["lrows"][i], s_ln[0], w)
            nln[0] += 16
            return lnr[0], (s_ln[0], nln[0])

        s_x = sem("s_x")
        A.dma(x, T["x"].rearrange("b (t p) d -> p (b t) d", p=P), s_x)
        start_load(tcom, T["tcom"])
        start_load(vec, T["vecs"])
        start_load(row, T["rows"])
        for k in FIRST_TABLES:
            tab[k] = carve(tabs[k].shape[1])
        wf = apos[0]
        start_load(arena[:, 0:wf], T["tfirst"])
        for tt_ in range(NT):
            start_load(tab[f"cz{tt_}"], T[f"cz{tt_}"])
        for l in range(2):
            start_load(rw36[:, l], T["wr"][l].rearrange("(k p) n -> p k n", p=P))
        w_uq = [carve(2 * 384).rearrange("p (k n) -> p k n", k=2) for _ in range(L1)]
        w_ukv = [carve(512) for _ in range(L1)]
        w2n = [carve(128).rearrange("p (a n) -> p a n", a=2) for _ in range(L1)]
        posT = [carve(32) for _ in range(L1)]
        for l in range(L1):
            start_load(w_uq[l][:, 0], T["mla_w_uq"][l, 0:P])
            start_load(w_uq[l][0:64, 1], T["mla_w_uq"][l, P:192])
            start_load(w_ukv[l], T["mla_w_ukv"][l])
            start_load(w2n[l], T["nsa_w2"][l].rearrange("a p n -> p a n"))
            start_load(posT[l], T["pos"][l])
        C0 = (s_c, nload[0])
        X0 = (s_x, 16)
        for q in (V, A, G, M):
            q.first += [C0, X0]
        idn = tab["idn"]

        VO, RO = vec_layout(), row_layout()

        def vcol(name, k=0, parts=slice(0, P)):
            o = VO[name] + k
            return vec[parts, o:o + 1]

        def rrow(name, w, off=0):
            o = RO[name] + off
            return row[:, o:o + w]

        sm_pos = [0]

        def sml(w):
            if sm_pos[0] + w > 256:
                sm_pos[0] = 0
            o = sm_pos[0]
            sm_pos[0] += w
            return small[:, o:o + w]

        def rms_scale(ss, n, eps, *w):
            t = ts(V, ss, ss, 1.0 / n, eps, MUL, ADD, *w)
            t = act(ss, ss, ACT.Sqrt, t)
            return rec(ss, ss, t)

        def to_T(src, dst, *w, scale=None):
            toks = []
            for half in range(2):
                i, p = ps()
                lst = [(p[:, (k % 4) * 256 + t * P:(k % 4) * 256 + t * P + P],
                        src[:, t, k * P:(k + 1) * P], idn) for k in range(4 * half, 4 * half + 4) for t in range(NT)]
                tok = tr(lst, *w, *pfree[i])
                q = V if half else A
                if scale is None:
                    e = cp(q, dst[:, 4 * half:4 * half + 4, :], p.rearrange("p (k s) -> p k s", k=4), tok)
                else:
                    for k in range(4 * half, 4 * half + 4):
                        pk = p[:, (k % 4) * 256:(k % 4) * 256 + 256]
                        if q is V:
                            e = ts(V, dst[:, k, :], pk, scale(k), None, MUL, None, tok)
                        else:
                            e = act(dst[:, k, :], pk, ACT.Copy, tok, scale=scale(k))
                pfree[i] = [e]
                toks.append(e)
            return toks

        def proj_T(lhs, rhs, nk, outs, *w):
            lst = []
            for o, c in outs:
                for k in range(nk):
                    lst.append((o, lhs[:, k, c], rhs[:, k, :], k == 0, k == nk - 1))
            return mm(lst, *w)

        def proj_tok(lhs, rhs, nk, o, c, *w):
            lst = []
            for t in range(NT):
                for k in range(nk):
                    lst.append((o[t], lhs[:, k, t * P:(t + 1) * P], rhs[:, k, c], k == 0, k == nk - 1))
            return mm(lst, *w)

        def silu(dst, src, tmp, *w):
            act(tmp, src, ACT.Sigmoid, *w)
            return tt(V, dst, src, tmp, MUL, A.last())

        def two(p, w):
            return p.rearrange("p (a n) -> p a n", a=2)[:, :, 0:w]

        Sb = [carve(1024) for _ in range(1)]
        Pb = [carve(1024) for _ in range(1)]
        PTb = [carve(1024) for _ in range(1)]
        base_first = apos[0]

        def softmax4(score, SL, scale, bias, guard, *w):
            i, p = ps()
            tok = mm(score(p), *w, *pfree[i])
            s_, p_ = Sb[0][:, 0:4 * SL], Pb[0][:, 0:4 * SL]
            e = stt(s_.rearrange("p (a n) -> p a n", a=2), two(p, 2 * SL), scale,
                    bias.rearrange("p (a n) -> p a n", a=2), MUL, ADD, tok, A.last())
            pfree[i] = [e]
            mx, sm = sml(4), sml(4)
            s4, p4 = s_.rearrange("p (u n) -> p u n", u=4), p_.rearrange("p (u n) -> p u n", u=4)
            red(mx, s4, MAX)
            if guard:
                ts(V, mx, mx, -1e29, None, MAX, None)
            tt(V, s4, s4, bc(mx.unsqueeze(2), [P, 4, SL]), SUB)
            act(p_, s_, ACT.Exp, V.last(), M.last())
            red(sm, p4, ADD, A.last())
            if guard:
                ts(V, sm, sm, 1e-30, None, MAX, None)
            rec(sm, sm)
            return p4, sm

        def attn4(t, score, scale, bias, vals, dst, *w):
            SL = P * (t + 1)
            p4, ri = softmax4(score, SL, scale, bias, False, *w)
            i, p = ps()
            tok = tr([(p[:, (u * (t + 1) + s) * P:(u * (t + 1) + s + 1) * P], p4[:, u, s * P:(s + 1) * P], idn)
                      for u in range(4) for s in range(t + 1)], A.last(), *pfree[i])
            pt = PTb[0][:, 0:4 * SL]
            e = cp(A, pt, p[:, 0:4 * SL], tok)
            pfree[i] = [e]
            i, p = ps()
            lst = []
            for u, h in enumerate(HORD):
                for s in range(t + 1):
                    lst.append((p[:, u * 64:(u + 1) * 64], pt[:, (u * (t + 1) + s) * P:(u * (t + 1) + s + 1) * P],
                                vals(h, s), s == 0, s == t))
            tok = mm(lst, e, *pfree[i])
            d4 = dst.rearrange("p (j a) n -> p a j n", j=2)
            e = tt(V, d4, p[:, 0:256].rearrange("p (a j n) -> p a j n", a=2, j=2),
                   bc(ri.rearrange("p (a j) -> p a j", a=2).unsqueeze(3), [P, 2, 2, 64]), MUL, tok)
            pfree[i] = [e]
            return e

        def dmp(name, ap):
            if dump is not None and name in dump:
                s_ = sem(f"s_d{name}")
                W.dma(dump[name], ap, s_, [q.last() for q in (V, A, G, M) if q.n])
                dumps.append((s_, 16))
                for q in (V, A, G, M):
                    q.first.append((s_, 16))

        dumps = []

        def first_layer(l):
            apos[0] = base_first
            gate = [carve(512).rearrange("p (t n) -> p t n", t=NT) for _ in range(4)]
            y = [carve(512).rearrange("p (t n) -> p t n", t=NT) for _ in range(4)]
            yT = [carve(512).rearrange("p (k s) -> p k s", k=2) for _ in range(4)]
            qT = carve(512).rearrange("p (j s) -> p j s", j=2)
            kT = carve(512).rearrange("p (j s) -> p j s", j=2)
            v = carve(512).rearrange("p (t n) -> p t n", t=NT)
            tmp = carve(1024)

            ss = sml(2)
            for t in range(NT):
                act(hb[:, t, :], x[:, t, :], ACT.Square, V.last() if V.n else X0, acc=ss[:, t:t + 1])
            rms_scale(ss, D, 1e-6, A.last())
            for t in range(NT):
                ts(V, hb[:, t, :], x[:, t, :], ss[:, t:t + 1], None, MUL, None)
            hTok = to_T(hb, hT, V.last(), scale=lambda k: vcol("norm_g", 8 * l + k))
            win = T["w_in"][l]

            def tok_major(c, w, c0=0):
                i, p = ps()
                o = p.rearrange("p (t n) -> p t n", t=NT)
                tok = proj_tok(hT, c.v, KT, [o[:, t, 0:w] for t in range(NT)], slice(c0, c0 + w),
                               c.tok, *hTok, *pfree[i])
                return i, two(p, w), tok

            def gate_of(i, src, tok, g):
                e = silu(g, src, tmp[:, 0:512].rearrange("p (t n) -> p t n", t=NT), tok, V.last())
                pfree[i] = [e]

            def heads_T(c, c0, dsts):
                i, p = ps()
                tok = proj_T(c.v, hT, KT, [(p[:, n * 256:(n + 1) * 256], slice(c0 + n * P, c0 + (n + 1) * P))
                                           for n in range(2 * len(dsts))], c.tok, *hTok, *pfree[i])
                for n, d in enumerate(dsts):
                    e = cp(A, d, p[:, n * 512:(n + 1) * 512].rearrange("p (j s) -> p j s", j=2), tok, M.last())
                pfree[i] = [e]
                return e

            def score_qk(q, k, t):
                SL = P * (t + 1)

                def go(p):
                    return [(p[:, hh * 512 + j * SL:hh * 512 + (j + 1) * SL],
                             q[64 * hh:64 * hh + 64, j, t * P:(t + 1) * P],
                             k(hh, j)[:, 0:SL], True, True) for j in range(2) for hh in range(2)]
                return go

            c = load_cols(win, 0, 512)
            qe = heads_T(c, 0, (qT, kT))
            c.free = M.last()
            c = load_cols(win, 512, 512)
            i, pv, tok = tok_major(c, 512)
            c.free = M.last()
            ve = cp(V, v, pv[:, :, 0:256], tok)
            gate_of(i, pv[:, :, 256:512], tok, gate[0])
            for t in range(NT):
                attn4(t, score_qk(qT, lambda hh, j: kT[64 * hh:64 * hh + 64, j], t), 0.125, tab[f"ba{t}"],
                      lambda h, s: v[:, s, h * 64:(h + 1) * 64],
                      y[0][:, t, :].rearrange("p (h n) -> p h n", h=4), qe, ve)

            barrier()
            b0 = apos[0]
            cq = carve(704).rearrange("p (t n) -> p t n", t=NT)
            cT = carve(768).rearrange("p (k s) -> p k s", k=3)
            qk = carve(512).rearrange("p (u n) -> p u n", u=16)
            rp = carve(512).rearrange("p (u n) -> p u n", u=16)
            rT = carve(256).rearrange("p (k s) -> p k s", k=1)
            c = load_cols(win, 1024, 352)
            i, pv, tok = tok_major(c, 352)
            c.free = M.last()
            e = cp(V, cq, pv, tok)
            pfree[i] = [e]
            ss = sml(4)
            for t in range(NT):
                act(tmp[:, 0:192], cq[:, t, 0:192], ACT.Square, e, acc=ss[:, t:t + 1])
                act(tmp[:, 0:128], cq[:, t, 192:320], ACT.Square, acc=ss[:, 2 + t:3 + t])
            ts(V, ss[:, 0:2], ss[:, 0:2], 1.0 / 192, 1e-6, MUL, ADD, A.last())
            ts(V, ss[:, 2:4], ss[:, 2:4], 1.0 / 128, 1e-6, MUL, ADD)
            act(ss, ss, ACT.Sqrt, V.last())
            rec(ss, ss, A.last())
            for t in range(NT):
                ts(V, cq[:, t, 0:192], cq[:, t, 0:192], ss[:, t:t + 1], None, MUL, None)
                ts(V, cq[:, t, 192:320], cq[:, t, 192:320], ss[:, 2 + t:3 + t], None, MUL, None)
            i, p = ps()
            tok = tr([(p[0:m, k * 256 + t * P:k * 256 + t * P + P], cq[:, t, o:o + m], idn)
                      for k, (o, m) in enumerate(((0, 128), (128, 64), (192, 128))) for t in range(NT)],
                     V.last(), *pfree[i])
            ts(V, cT[:, 0, :], p[:, 0:256], vcol("qn", 2 * l), None, MUL, None, tok)
            ts(V, cT[0:64, 1, :], p[0:64, 256:512], vcol("qn", 2 * l + 1, slice(0, 64)), None, MUL, None)
            e = ts(V, cT[:, 2, :], p[:, 512:768], vcol("kvn", l), None, MUL, None)
            pfree[i] = [e]
            i, p = ps()
            lst = []
            for h in range(4):
                j, hh = h // 2, h % 2
                o = p[64 * hh:64 * hh + 64, j * 256:(j + 1) * 256]
                lst.append((o, w_uq[l][:, 0, h * 96:h * 96 + 64], cT[:, 0, :], True, False))
                lst.append((o, w_uq[l][0:64, 1, h * 96:h * 96 + 64], cT[0:64, 1, :], False, True))
            for h in range(4):
                j, hh = h // 2, h % 2
                lst.append((p[64 * hh:64 * hh + 64, 512 + j * 256:512 + (j + 1) * 256],
                            w_ukv[l][:, h * 128:h * 128 + 64], cT[:, 2, :], True, True))
            tok = mm(lst, e, *pfree[i])
            cp(A, qT, p[:, 0:512].rearrange("p (j s) -> p j s", j=2), tok)
            e2 = cp(A, kT, p[:, 512:1024].rearrange("p (j s) -> p j s", j=2))
            pfree[i] = [e2]
            i, p = ps()
            lst = []
            wq4 = w_uq[l].rearrange("p k (h n) -> p k h n", h=4)
            wv4 = w_ukv[l].rearrange("p (h n) -> p h n", h=4)
            for t in range(NT):
                tk = slice(t * P, (t + 1) * P)
                lst.append((p[:, t * P:(t + 1) * P], cT[:, 0, tk], wq4[:, 0, :, 64:96], True, False))
                lst.append((p[:, t * P:(t + 1) * P], cT[0:64, 1, tk], wq4[0:64, 1, :, 64:96], False, True))
            for t in range(NT):
                lst.append((p[:, 512 + t * 256:512 + (t + 1) * 256], cT[:, 2, t * P:(t + 1) * P],
                            wv4[:, :, 64:128], True, True))
            tok = mm(lst, *pfree[i])
            cp(V, qk[:, 0:8, :], p[:, 0:256].rearrange("p (u n) -> p u n", u=8), tok)
            ve = cp(V, v, p[:, 512:1024].rearrange("p (t n) -> p t n", t=NT))
            pfree[i] = [ve]
            for t in range(NT):
                cp(V, qk[:, 8 + 4 * t:12 + 4 * t, :], bc(cq[:, t, 320:352].unsqueeze(1), [P, 4, 32]))
            cos = tab["cos"].rearrange("p (u n) -> p u n", u=16)
            sin = tab["sin"].rearrange("p (u n) -> p u n", u=16)
            t1 = tmp[:, 0:256].rearrange("p (u n) -> p u n", u=16)
            x1, x2 = qk[:, :, 0:16], qk[:, :, 16:32]
            tt(V, rp[:, :, 0:16], x1, cos, MUL)
            tt(V, t1, x2, sin, MUL)
            tt(V, rp[:, :, 0:16], rp[:, :, 0:16], t1, SUB)
            tt(V, rp[:, :, 16:32], x1, sin, MUL)
            tt(V, t1, x2, cos, MUL)
            e = tt(V, rp[:, :, 16:32], rp[:, :, 16:32], t1, ADD)
            i, p = ps()
            rpf = rp.rearrange("p u n -> p (u n)")
            tok = tr([(p[:, k * 256 + t * P:k * 256 + t * P + P], rpf[:, (k * 2 + t) * P:(k * 2 + t + 1) * P], idn)
                      for k in range(2) for t in range(NT)], e, *pfree[i])
            cp(V, rT[:, 0, :], p[:, 0:256], tok)
            krm = tmp.rearrange("p (h s) -> p h s", h=4)
            ms(V, tmp, 0.0)
            for h in range(4):
                cp(V, krm[32 * h:32 * h + 32, h, :], p[32 * h:32 * h + 32, 256:512])
            e = V.last()
            pfree[i] = [e]
            for t in range(NT):
                def score_b(p, t=t):
                    SL = P * (t + 1)
                    lst = []
                    for j in range(2):
                        for hh in range(2):
                            h = 2 * j + hh
                            o = p[:, hh * 512 + j * SL:hh * 512 + (j + 1) * SL]
                            tk = slice(t * P, (t + 1) * P)
                            lst.append((o, qT[64 * hh:64 * hh + 64, j, tk], kT[64 * hh:64 * hh + 64, j, 0:SL], True, False))
                            lst.append((o, rT[:, 0, tk], krm[:, h, 0:SL], False, True))
                    return lst
                attn4(t, score_b, 96.0 ** -0.5, tab[f"cz{t}"], lambda h, s: v[:, s, h * 64:(h + 1) * 64],
                      y[1][:, t, :].rearrange("p (h n) -> p h n", h=4), e, e2, ve)
            barrier()
            apos[0] = b0

            c = load_cols(win, 1376, 512)
            i, pv, tok = tok_major(c, 256)
            gate_of(i, pv, tok, gate[1])
            qe = heads_T(c, 256, (qT,))
            c.free = M.last()
            kcv = carve(256)
            ksd, kwd = carve(256), carve(256)
            vs, vw = (carve(128).rearrange("p (t n) -> p t n", t=NT) for _ in range(2))
            cg = carve(24).rearrange("p (t n) -> p t n", t=NT)
            blk = carve(480).rearrange("p (q n) -> p q n", q=32)
            hid = carve(64).rearrange("p (a n) -> p a n", a=2)
            kcd = carve(32)
            vcb = carve(256)
            ob = carve(512).rearrange("p (t n) -> p t n", t=NT)
            c = load_cols(win, 1888, 396)
            i, p = ps()
            lst = [(p[:, 0:256], c.v[:, k, 0:128], hT[:, k, :], k == 0, k == 7) for k in range(KT)]
            for n, c0 in enumerate((128, 256)):
                for hh in range(2):
                    lst += [(p[64 * hh:64 * hh + 64, 512 + n * 256:768 + n * 256], c.v[:, k, c0:c0 + 64], hT[:, k, :],
                             k == 0, k == 7) for k in range(KT)]
            tok = mm(lst, c.tok, *hTok, *pfree[i])
            cp(V, kcv, p[:, 0:256], tok)
            cp(V, ksd, p[:, 512:768])
            e = cp(V, kwd, p[:, 768:1024])
            pfree[i] = [e]
            i, p = ps()
            lst = []
            for t in range(NT):
                for c0, w, o0 in ((192, 64, 0), (320, 76, 64)):
                    lst += [(p[:, t * 512 + o0:t * 512 + o0 + w], hT[:, k, t * P:(t + 1) * P], c.v[:, k, c0:c0 + w],
                             k == 0, k == 7) for k in range(KT)]
            tok = mm(lst, *pfree[i])
            c.free = M.last()
            o = p.rearrange("p (t n) -> p t n", t=NT)
            cp(V, vs, o[:, :, 0:64], tok)
            cp(V, vw, o[:, :, 64:128])
            act(cg, o[:, :, 128:140], ACT.Exp, V.last(), scale=-1.0)
            pfree[i] = [A.last()]
            ts(V, cg, cg, 1.0, None, ADD, None, A.last())
            rec(cg, cg)
            c = load(*[((lambda a: lambda s: s[64 * a:64 * a + 64, :].rearrange("d (q c) -> d q c", q=32))(a),
                        T["nsa_w1"][l, a].rearrange("(q d) c -> d q c", d=64)) for a in range(2)])
            w1v = c.ap.rearrange("d (q c) -> d q c", q=32)
            for q_ in range(2):
                win_ap = kcv[:, 16 * q_:16 * q_ + 240].rearrange("p (n q) -> p q n", q=16)
                tt(V, blk[:, 16 * q_:16 * q_ + 16, :], win_ap, bc(posT[l][:, 16 * q_:16 * q_ + 16].unsqueeze(2), [P, 16, 15]), ADD)
            i, p = ps()
            tok = mm([(p[:, a * 512:a * 512 + 15], w1v[64 * a:64 * a + 64, q, :], blk[64 * a:64 * a + 64, q, :],
                       q == 0, q == 31) for q in range(32) for a in range(2)], c.tok, V.last(), *pfree[i])
            c.free = M.last()
            ms(V, hid, 0.0, tok)
            g1, g2 = tmp[:, 0:32].rearrange("p (a n) -> p a n", a=2), tmp[:, 32:64].rearrange("p (a n) -> p a n", a=2)
            g1, g2 = g1[:, :, 0:15], g2[:, :, 0:15]
            h15 = hid[:, :, 0:15]
            for a in range(2):
                ts(V, h15[:, a, :], p[:, a * 512:a * 512 + 15], vcol("nb1", 2 * l + a), None, ADD, None)
            pfree[i] = [V.last()]
            tt(V, g1, h15, h15, MUL)
            ts(V, g1, g1, 0.044715, 1.0, MUL, ADD)
            tt(V, g1, g1, h15, MUL)
            act(g2, g1, ACT.Exp, V.last(), scale=-2.0 * 0.7978845608028654)
            ts(V, g2, g2, 1.0, None, ADD, None, A.last())
            rec(g2, g2)
            tt(V, h15, h15, g2, MUL)
            i, p = ps()
            lst = [(p[64 * hh:64 * hh + 64, 0:32], w2n[l][:, 0, :], hid[:, 0, :], True, True) for hh in range(2)]
            lst += [(p[32 * u:32 * u + 32, 512:576], hid[:, 1, :], w2n[l][:, 1, :], True, True) for u in range(4)]
            tok = mm(lst, V.last(), *pfree[i])
            ts(V, kcd, p[:, 0:32], vcol("nb2", l), None, ADD, None, tok)
            ms(V, vcb, 0.0)
            for u in range(4):
                tt(V, vcb[32 * u:32 * u + 32, u * 64:u * 64 + 64], p[32 * u:32 * u + 32, 512:576],
                   rrow("nb2v", 64, 64 * l)[32 * u:32 * u + 32], ADD)
            pfree[i] = [V.last()]
            kve = V.last()
            yc = y[2]
            for t in range(NT):
                tk = slice(t * P, (t + 1) * P)

                def score_c(p, tk=tk):
                    return [(p[:, hh * 512 + j * 32:hh * 512 + j * 32 + 32], qT[64 * hh:64 * hh + 64, j, tk],
                             kcd[64 * hh:64 * hh + 64, :], True, True) for j in range(2) for hh in range(2)]
                p4, ri = softmax4(score_c, 32, 0.125, tab[f"cm{t}"], True, qe, kve)
                i, p = ps()
                tok = tr([(p[:, 0:P], Pb[0][:, 0:P], idn)], A.last(), *pfree[i])
                e = cp(A, PTb[0][:, 0:P], p[:, 0:P], tok)
                pfree[i] = [e]
                i, p = ps()
                tok = mm([(p[:, 0:256], PTb[0][:, 0:P], vcb, True, True)], e, *pfree[i])
                d4 = yc[:, t, :].rearrange("p (j a n) -> p a j n", j=2, a=2)
                pfree[i] = [tt(V, d4, p[:, 0:256].rearrange("p (a j n) -> p a j n", a=2, j=2),
                               bc(ri.rearrange("p (a j) -> p a j", a=2).unsqueeze(3), [P, 2, 2, 64]), MUL, tok)]
            c3 = cg.rearrange("p t (h g) -> p t h g", g=3)
            y4 = yc.rearrange("p t (h n) -> p (t h) n", h=4)
            o4 = ob.rearrange("p t (h n) -> p (t h) n", h=4)
            gg = [cg.rearrange("p t (h g) -> p (t h) g", g=3)[:, :, g:g + 1] for g in range(3)]
            tt(V, y4, y4, bc(gg[0], [P, 8, 64]), MUL)
            for n, (kd, vv) in enumerate(((ksd, vs), (kwd, vw))):
                for t in range(NT):
                    attn4(t, score_qk(qT, lambda hh, j: kd[64 * hh:64 * hh + 64, :], t), 0.125, tab[f"bc{t}"],
                          lambda h, s: vv[:, s, :], ob[:, t, :].rearrange("p (h n) -> p h n", h=4), qe, kve)
                tt(V, o4, o4, bc(gg[1 + n], [P, 8, 64]), MUL)
                tt(V, y4, y4, o4, ADD)
            c = load_cols(win, 2284, 512)
            i, pv, tok = tok_major(c, 256)
            gate_of(i, pv, tok, gate[2])
            barrier()
            apos[0] = b0

            qe = heads_T(c, 256, (qT,))
            c.free = M.last()
            c = load_cols(win, 2796, 512)
            ke = heads_T(c, 0, (kT,))
            i, pv, tok = tok_major(c, 256, 256)
            c.free = M.last()
            ve = cp(V, v, pv, tok)
            pfree[i] = [ve]
            c = load_cols(win, 3308, 256)
            i, pv, tok = tok_major(c, 256)
            c.free = M.last()
            gate_of(i, pv, tok, gate[3])
            zb = [carve(1024), carve(512)]
            sp = [Sb[0], PTb[0][:, 512:1024]]
            lg = [Pb[0], PTb[0][:, 0:512]]
            for s in range(2):
                w = S - s * P
                i, p = ps()
                tok = mm([(p[:, hh * 512 + j * w:hh * 512 + (j + 1) * w], kT[64 * hh:64 * hh + 64, j, s * P:(s + 1) * P],
                           qT[64 * hh:64 * hh + 64, j, s * P:S], True, True) for j in range(2) for hh in range(2)],
                         qe, ke, *pfree[i])
                z3 = zb[s].rearrange("p (a n) -> p a n", a=2)
                e = ts(V, z3, two(p, 2 * w), 0.125, None, MUL, None, tok)
                pfree[i] = [e]
                act(lg[s], zb[s], ACT.Abs, e)
                act(lg[s], lg[s], ACT.Exp, scale=-1.0)
                act(lg[s], lg[s], ACT.Ln, bias=1.0)
                e = stt(sp[s], zb[s], 0.0, lg[s], MAX, ADD, A.last())
                tt(V, zb[s], zb[s], sp[s], SUB)
                sp4 = sp[s].rearrange("p (u n) -> p u n", u=4)
                tt(V, sp4, sp4, bc(tab[f"st{s}"].unsqueeze(1), [P, 4, w]), MUL)
            i, p = ps()
            lst = []
            for u in range(4):
                o = p[:, u * 256:(u + 1) * 256]
                lst.append((o, tab["upp"], sp[0][:, u * 256:(u + 1) * 256], True, False))
                lst.append((o[:, P:256], tab["one"], sp[1][:, u * P:(u + 1) * P], False, True))
            i2, p2 = ps()
            tok = mm(lst, V.last(), *pfree[i])
            tok2 = mm([(p2[:, 0:512], tab["upp"], sp[1], True, True)], *pfree[i2])
            tt(V, zb[0], zb[0], p, SUB, tok)
            pfree[i] = [V.last()]
            tt(V, zb[1], zb[1], p2[:, 0:512], SUB, tok2)
            pfree[i2] = [V.last()]
            for s in range(2):
                w = S - s * P
                act(lg[s], zb[s], ACT.Exp, V.last())
                l4 = lg[s].rearrange("p (u n) -> p u n", u=4)
                tt(V, l4, l4, bc(tab[f"st{s}"].unsqueeze(1), [P, 4, w]), MUL, A.last())
            i, p = ps()
            lst = []
            for t in range(NT):
                for u, h in enumerate(HORD):
                    for s in range(t + 1):
                        w = S - s * P
                        a = lg[s][:, u * w + (t - s) * P:u * w + (t - s + 1) * P]
                        lst.append((p[:, t * 512 + h * 64:t * 512 + (h + 1) * 64], a, v[:, s, h * 64:(h + 1) * 64], s == 0, s == t))
            tok = mm(lst, V.last(), *pfree[i])
            tt(V, y[3], two(p, 256), gate[3], MUL, tok)
            pfree[i] = [V.last()]
            for b in range(4):
                dmp(f"y{l}{b}", y[b])
            for b in range(3):
                tt(V, y[b], y[b], gate[b], MUL)
            for b in range(4):
                i, p = ps()
                tok = tr([(p[:, k * 256 + t * P:k * 256 + t * P + P], y[b][:, t, k * P:(k + 1) * P], idn)
                          for k in range(2) for t in range(NT)], V.last(), *pfree[i])
                pfree[i] = [cp(A, yT[b], p[:, 0:512].rearrange("p (k s) -> p k s", k=2), tok)]
            cb = None
            sg = tmp
            for b in range(4):
                cb = load_cols(T["w_branch"][l, b], 0, D)
                wb = cb.v
                for half in range(2):
                    c = load_cols(T["w_merge"][l, b], 512 * half, 512)
                    i, p = ps()
                    i2, p2 = ps()
                    tok = proj_T(c.v, hT, KT, [(p[:, n * 256:(n + 1) * 256], slice(n * P, (n + 1) * P)) for n in range(4)],
                                 c.tok, *pfree[i])
                    c.free = M.last()
                    tok2 = proj_T(wb, yT[b], 2, [(p2[:, n * 256:(n + 1) * 256], slice((4 * half + n) * P, (4 * half + n + 1) * P))
                                                 for n in range(4)], cb.tok, A.last(), *pfree[i2])
                    cb.free = M.last()
                    for n in range(4):
                        act(sg[:, n * 256:(n + 1) * 256], p[:, n * 256:(n + 1) * 256], ACT.Sigmoid, tok, V.last(),
                            bias=vcol("bm", 32 * l + 8 * b + 4 * half + n))
                    pfree[i] = [A.last()]
                    m3 = mT[:, 4 * half:4 * half + 4, :].rearrange("p k s -> p (k s)")
                    if b == 0:
                        e = tt(V, m3, sg, p2, MUL, A.last(), tok2)
                    else:
                        e = tt(V, sg, sg, p2, MUL, A.last(), tok2)
                    pfree[i2] = [e]
                    if b:
                        tt(V, m3, m3, sg, ADD)
            dmp(f"mT{l}", mT)
            for half in range(2):
                c = load_cols(T["w_out"][l], 512 * half, 512)
                i, p = ps()
                o = p.rearrange("p (t n) -> p t n", t=NT)
                tok = proj_tok(mT, c.v, KT, [o[:, t, :] for t in range(NT)], slice(0, 512), c.tok, V.last(), *pfree[i])
                c.free = M.last()
                xs = x[:, :, 512 * half:512 * half + 512]
                pfree[i] = [tt(V, xs, xs, o, ADD, tok)]
            barrier()

        for l in range(L1):
            first_layer(l)
            if stop == f"l{l}":
                break

        def final_norm():
            r, rt = rows_in(0)
            ss = sml(2)
            for t in range(NT):
                act(hb[:, t, :], x[:, t, :], ACT.Square, acc=ss[:, t:t + 1])
            rms_scale(ss, D, 1e-6, A.last())
            for t in range(NT):
                lnfree[0] = stt(x[:, t, :], x[:, t, :], ss[:, t:t + 1], r[:, 0, :], MUL, MUL, rt)

        def layer_norm(src, i, *w):
            r, rt = rows_in(i)
            ss = sml(4)
            for t in range(NT):
                stt(x[:, t, :], x[:, t, :], ALPHA, src(t), MUL, ADD, *w)
            for t in range(NT):
                red(ss[:, t:t + 1], x[:, t, :], ADD)
            ts(V, ss[:, 0:2], ss[:, 0:2], 1.0 / D, None, MUL, None)
            for t in range(NT):
                ts(V, x[:, t, :], x[:, t, :], ss[:, t:t + 1], None, SUB, None)
            for t in range(NT):
                act(hb[:, t, :], x[:, t, :], ACT.Square, V.last(), acc=ss[:, 2 + t:3 + t])
            rms_scale(ss[:, 2:4], D, 1e-5, A.last())
            for t in range(NT):
                stt(x[:, t, :], x[:, t, :], ss[:, 2 + t:3 + t], r[:, 0, :], MUL, MUL, rt)
            for t in range(NT):
                lnfree[0] = tt(V, x[:, t, :], x[:, t, :], r[:, 1, :], ADD)
            return V.last()

        def diff_attention():
            apos[0] = 0
            qT = carve(2048).rearrange("p (h s) -> p h s", h=8)
            kT = carve(2048).rearrange("p (h s) -> p h s", h=8)
            v = carve(2048).rearrange("p (t n) -> p t n", t=NT)
            o = carve(2048).rearrange("p (t n) -> p t n", t=NT)
            oT = carve(2048).rearrange("p (k s) -> p k s", k=KT)
            Sb[0], Pb[0], PTb[0] = carve(1024), carve(1024), carve(1024)
            tmp = carve(256)
            wq = T["attn_w_qkv_2"][0]
            xe = to_T(x, hT, V.last())
            lam = sml(4)
            for n in range(2):
                tt(V, tmp[:, 0:64], rrow("lam", 64, 128 * n), rrow("lam", 64, 128 * n + 64), MUL)
                red(lam[:, n:n + 1], tmp[:, 0:64], ADD)
            act(lam[:, 0:2], lam[:, 0:2], ACT.Exp, V.last())
            tt(V, lam[:, 2:3], lam[:, 1:2], lam[:, 0:1], SUB, A.last())
            lneg = carve(1)
            ts(V, lneg, lam[:, 2:3], 0.2, None, SUB, None)
            sub = carve(128)
            ts(V, sub, rrow("subln", 128), 0.8, None, MUL, None)
            toks = []
            for n, d in enumerate((qT, qT, kT, kT)):
                c = load_cols(wq, 512 * n, 512)
                i, p = ps()
                tok = proj_T(c.v, hT, KT, [(p[:, m * 256:(m + 1) * 256], slice(m * P, (m + 1) * P)) for m in range(4)],
                             c.tok, *xe, *pfree[i])
                c.free = M.last()
                e = cp(A, d[:, 4 * (n % 2):4 * (n % 2) + 4, :], p.rearrange("p (h s) -> p h s", h=4), tok)
                pfree[i] = [e]
            toks.append(e)
            for n in range(2):
                c = load_cols(wq, 2048 + 512 * n, 512)
                i, p = ps()
                o3 = p.rearrange("p (t n) -> p t n", t=NT)
                tok = proj_tok(hT, c.v, KT, [o3[:, t, :] for t in range(NT)], slice(0, 512), c.tok, *pfree[i])
                c.free = M.last()
                e = cp(V, v[:, :, 512 * n:512 * n + 512], o3, tok)
                pfree[i] = [e]
            toks.append(e)
            for g in range(4):
                for t in range(NT):
                    SL = P * (t + 1)

                    def score(p, g=g, t=t, SL=SL):
                        return [(p[:, cc * 512 + hl * SL:cc * 512 + (hl + 1) * SL],
                                 qT[64 * cc:64 * cc + 64, 2 * g + hl, t * P:(t + 1) * P],
                                 kT[64 * cc:64 * cc + 64, 2 * g + hl, 0:SL], True, True)
                                for hl in range(2) for cc in range(2)]
                    p4, ri = softmax4(score, SL, 0.125, tab[f"cz{t}"], False, *toks)
                    ts(V, ri[:, 2:4], ri[:, 2:4], lneg, None, MUL, None)
                    s4 = Sb[0][:, 0:4 * SL].rearrange("p (u n) -> p u n", u=4)
                    tt(V, s4, p4, bc(ri.unsqueeze(2), [P, 4, SL]), MUL)
                    a = Sb[0][:, 0:2 * SL]
                    e = tt(V, a, a, Sb[0][:, 2 * SL:4 * SL], ADD)
                    i, p = ps()
                    tok = tr([(p[:, n * P:(n + 1) * P], a[:, n * P:(n + 1) * P], idn) for n in range(2 * (t + 1))],
                             e, *pfree[i])
                    pt = PTb[0][:, 0:2 * SL]
                    e = cp(A, pt, p[:, 0:2 * SL], tok)
                    pfree[i] = [e]
                    i, p = ps()
                    lst = []
                    for hl in range(2):
                        for s in range(t + 1):
                            n = hl * (t + 1) + s
                            h = 2 * g + hl
                            lst.append((p[:, hl * P:(hl + 1) * P], pt[:, n * P:(n + 1) * P], v[:, s, h * P:(h + 1) * P], s == 0, s == t))
                    tok = mm(lst, e, *pfree[i])
                    pfree[i] = [cp(V, o[:, t, 2 * g * P:(2 * g + 2) * P], p[:, 0:256], tok)]
            o8 = o.rearrange("p t (h n) -> p (t h) n", h=8)
            h8 = hb.rearrange("p t (h n) -> p (t h) n", h=8)
            ss = sml(16)
            tt(V, h8, o8, o8, MUL)
            red(ss, h8, ADD)
            rms_scale(ss, 128, 1e-5)
            tt(V, o8, o8, bc(ss.unsqueeze(2), [P, 16, 128]), MUL)
            tt(V, o8, o8, bc(sub.unsqueeze(1), [P, 16, 128]), MUL)
            e = to_T(o, oT, V.last())
            out_proj(T["attn_w_o_2"][0], oT, 1, *e)

        def out_proj(w, srcT, lni, *wt):
            i0, p0 = ps()
            i1, p1 = ps()
            pp = (p0, p1)
            for half in range(2):
                c = load_cols(w, 512 * half, 512)
                tok = proj_tok(srcT, c.v, KT, [pp[t][:, 512 * half:512 * half + 512] for t in range(NT)], slice(0, 512),
                               c.tok, *wt, *pfree[i0], *pfree[i1])
                c.free = M.last()
            e = layer_norm(lambda t: pp[t], lni, tok)
            pfree[i0] = pfree[i1] = [e]
            barrier()

        def route(l, gates, sel):
            xe = to_T(x, hT, V.last())
            i, p = ps()
            tok = proj_tok(hT, rw36[:, l], KT, [p[:, t * 512:t * 512 + 36] for t in range(NT)], slice(0, 36), *xe, *pfree[i])
            lo = carve(72).rearrange("p (t n) -> p t n", t=NT)
            e = tt(V, lo, two(p, 36), bc(rrow("mb", 36, 36 * l).unsqueeze(1), [P, 2, 36]), ADD, tok)
            pfree[i] = [e]
            gl, el = lo[:, :, 0:4], lo[:, :, 4:36]
            ex = carve(64).rearrange("p (t n) -> p t n", t=NT)
            eq = carve(64).rearrange("p (t n) -> p t n", t=NT)
            k1 = carve(64).rearrange("p (t n) -> p t n", t=NT)
            mx, gp, ix, m1, m2 = (carve(2) for _ in range(5))

            def col(a, n):
                return bc(a.unsqueeze(2), [P, 2, n])

            def first_of(dst, val, n, iota, m):
                tt(V, eq[:, :, 0:n], val, col(m, n), ALU.is_ge)
                ts(V, eq[:, :, 0:n], eq[:, :, 0:n], -1000.0, 1000.0, MUL, ADD)
                tt(V, eq[:, :, 0:n], eq[:, :, 0:n], bc(iota.unsqueeze(1), [P, 2, n]), ADD)
                red(ix, eq[:, :, 0:n], MIN)
                tt(V, dst, bc(iota.unsqueeze(1), [P, 2, n]), col(ix, n), ALU.is_equal)

            red(mx, gl, MAX)
            g4 = ex[:, :, 0:4]
            tt(V, g4, gl, col(mx, 4), SUB)
            act(g4, g4, ACT.Exp, V.last())
            red(gp, g4, ADD, A.last())
            rec(gp, gp)
            oh = carve(8).rearrange("p (t n) -> p t n", t=NT)
            first_of(oh, gl, 4, tab["iog"], mx)
            ts(V, oh, oh, -2 * NEG, NEG, MUL, ADD)
            oh8 = bc(oh.rearrange("p t g -> p (t g)").unsqueeze(2), [P, 8, 8])
            el8 = lambda a: a.rearrange("p t (g n) -> p (t g) n", g=4)
            em = carve(64).rearrange("p (t n) -> p t n", t=NT)
            ec = carve(64).rearrange("p (t n) -> p t n", t=NT)
            cp(V, ec, el)
            tt(V, el8(em), el8(ec), oh8, MIN)
            red(m1, em, MAX)
            o1 = k1
            first_of(o1, em, 32, tab["ioe"], m1)
            e2 = carve(64).rearrange("p (t n) -> p t n", t=NT)
            stt(e2.rearrange("p t n -> p (t n)"), o1.rearrange("p t n -> p (t n)"), 2 * NEG, em.rearrange("p t n -> p (t n)"), MUL, ADD)
            red(m2, e2, MAX)
            o2 = ex
            first_of(o2, e2, 32, tab["ioe"], m2)
            tt(V, m2, m2, m1, SUB)
            act(m2, m2, ACT.Exp, V.last())
            ts(V, m1, m2, 1.0, None, ADD, None, A.last())
            rec(m1, m1)
            tt(V, m1, m1, gp, MUL)
            tt(V, m2, m2, m1, MUL)
            tt(V, sel, o1, o2, ADD)
            tt(V, o1, o1, col(m1, 32), MUL)
            tt(V, o2, o2, col(m2, 32), MUL)
            tt(V, gates, o1, o2, ADD)

        def moe(l, lni):
            apos[0] = 0
            acc = mT.rearrange("p k s -> p (k s)").rearrange("p (t d) -> p t d", t=NT)
            gates = carve(64).rearrange("p (t n) -> p t n", t=NT)
            sel = carve(64).rearrange("p (t n) -> p t n", t=NT)
            pos = carve(64).rearrange("p (t n) -> p t n", t=NT)
            flag = carve(16).bitcast(mybir.dt.int32)
            pad = carve(1)
            xe = carve(4096).rearrange("p (k n) -> p k n", k=KT)
            gu = [carve(512), carve(512)]
            hs_ = [carve(256).rearrange("p (k n) -> p k n", k=4) for _ in range(2)]
            sg = [carve(256).rearrange("p (k n) -> p k n", k=4) for _ in range(2)]
            oh, og = carve(1024), carve(1024)
            ogT = carve(256)
            yb = carve(1024)
            hid = [carve(1024), carve(1024)]
            dsg = carve(1024)
            lend([carve(SLOT) for _ in range(MORE)], [q.last() for q in (V, A, G, M)])
            scratch = apos[0]
            route(l, gates, sel)
            apos[0] = scratch
            dmp(f"g{l}", gates)
            ms(V, acc, 0.0)
            i, p = ps()
            tok = mm([(p[:, 0:32], tab["st1"], sel[:, 0, :], True, True),
                      (p[:, 32:64], tab["st1"], sel[:, 1, :], True, False),
                      (p[:, 32:64], tab["one"], sel[:, 0, :], False, True),
                      (p[:, 64:96], tab["one"], sel[:, 0, :], True, False),
                      (p[:, 64:96], tab["one"], sel[:, 1, :], False, True)], V.last(), *pfree[i])
            ts(V, pos, sel, -1000.0, 1000.0, MUL, ADD)
            tt(V, pos, pos, p[:, 0:64].rearrange("p (t n) -> p t n", t=NT), ADD, tok)
            cnt = sml(16)
            red(cnt, p[:, 64:96].rearrange("p (q a) -> p q a", a=2), MAX)
            pfree[i] = [V.last()]
            ts(V, cnt, cnt, CAP + 0.5, None, ALU.is_gt, None)
            fl = cp(V, flag, cnt)
            oh4 = oh.rearrange("p (t e n) -> p (t e) n", t=NT, e=8)
            og4 = og.rearrange("p (t e n) -> p (t e) n", t=NT, e=8)
            barrier()
            pg, pt = psum[2], psum[3]
            for pr in range(E // 2):
                if pr % 4 == 0:
                    e8 = slice(2 * pr, 2 * pr + 8)
                    for t in range(NT):
                        o8 = oh[:, 512 * t:512 * t + 512].rearrange("p (e n) -> p e n", e=8)
                        g8 = og[:, 512 * t:512 * t + 512].rearrange("p (e n) -> p e n", e=8)
                        tt(V, o8, bc(pos[:, t, e8].unsqueeze(2), [P, 8, CAP]), bc(tab["ios"].unsqueeze(1), [P, 8, CAP]),
                           ALU.is_equal, M.last())
                        tt(V, g8, o8, bc(gates[:, t, e8].unsqueeze(2), [P, 8, CAP]), MUL)
                    for k2 in range(4):
                        buf = (pg, pt)[k2 % 2]
                        lst = [(buf[:, 512 * m:512 * m + 512], x[:, t, (2 * k2 + m) * P:(2 * k2 + m + 1) * P],
                                oh[:, 512 * t:512 * t + 512], t == 0, t == 1) for m in range(2) for t in range(NT)]
                        tok = mm(lst, V.last(), A.last())
                        cp((A, V)[k2 % 2], xe[:, 2 * k2:2 * k2 + 2, :].rearrange("p k n -> p (k n)"), buf, tok)
                    v_prev, a_prev = V.last(), A.last()
                    v_hid = V.last()
                else:
                    v_hid, v_prev, a_prev = V.ago(4), V.last(), A.last()
                gu_c, dn_c = [], []
                for a in range(2):
                    wg = T["moe_w_gu_2"][l, 2 * pr + a]
                    gu_c.append([load_cols(wg, 0, 512), load_cols(wg, 512, 512)])
                for a in range(2):
                    dn_c.append(load_cols(T["moe_w_down_2"][l, 2 * pr + a], 0, D))
                m0 = M.n
                for q in (V, A, M):
                    q.split(flag[0:1, pr:pr + 1], [fl])

                for a in range(2):
                    c0, c1 = gu_c[a]
                    lst = [(dst[:, n * 256:(n + 1) * 256], c.v[:, k, n * P:(n + 1) * P], hT[:, k, :], k == 0, k == KT - 1)
                           for dst, c in ((pg, c0), (pt, c1)) for n in range(4) for k in range(KT)]
                    tok = mm(lst, c0.tok, c1.tok, v_hid, a_prev)
                    act(dsg, pg, ACT.Sigmoid, tok, V.last())
                    tt(V, hid[a], dsg, pg, MUL, A.last())
                    v_hid = tt(V, hid[a], hid[a], pt, MUL)
                    for c in gu_c[a]:
                        c.free = M.last()
                for a in range(2):
                    h3 = hid[a].rearrange("p (k s) -> p k s", k=4)
                    for t in range(NT):
                        tok = mm([(psum[t][:, n * 512:(n + 1) * 512], h3[:, k, t * P:(t + 1) * P],
                                   dn_c[a].v[:, k, n * 512:(n + 1) * 512], k == 0, k == 3) for n in range(2) for k in range(4)],
                                 dn_c[a].tok, v_hid if a == 0 else V.ago(1 - t), v_prev)
                        stt(acc[:, t, :], psum[t], gates[:, t, 2 * pr + a:2 * pr + a + 1], acc[:, t, :], MUL, ADD, tok)
                mm([(pg[0:1, 0:1], idn[:, 0:1], idn[:, 0:1], True, True)], V.last())
                for _ in range(4):
                    act(pad[0:1], tab["one"][0:1, 0:1], ACT.Copy)

                for q in (V, A, M):
                    q.other()
                if pr % 4:
                    v_hid = (V.sem, V.n - 4)
                else:
                    v_hid = v_prev
                for a in range(2):
                    c0, c1 = gu_c[a]
                    n0 = (2 * (pr % 4) + a) * CAP
                    o = pg[:, 512 * a:512 * a + 512]
                    lst = [(o[64 * m:64 * m + 64, :], xe[:, k, n0:n0 + CAP], c.v[:, k, :], k == 0, k == KT - 1)
                           for k in range(KT) for m, c in enumerate((c0, c1))]
                    tok = mm(lst, c0.tok, c1.tok, v_hid, a_prev)
                    cp(A, gu[a], o, tok)
                for a in range(2):
                    o = pt[:, 512 * a:512 * a + 512]
                    tok = tr([(o[:, k * P:(k + 1) * P], gu[a][:, k * P:(k + 1) * P], idn) for k in range(4)], A.ago(1 - a))
                    o4 = o.rearrange("p (k n) -> p k n", k=4)
                    act(sg[a], o4[:, :, 0:64], ACT.Sigmoid, tok)
                    tt(V, sg[a], sg[a], o4[:, :, 0:64], MUL, A.last())
                    tt(V, hs_[a], sg[a], o4[:, :, 64:128], MUL)
                tok = tr([(psum[1][:, t * P:(t + 1) * P], og[:, 512 * t + 128 * (pr % 4):512 * t + 128 * (pr % 4) + 128], idn)
                          for t in range(NT)], v_prev)
                cp(A, ogT, psum[1][:, 0:256], tok)
                lst = [(pg[64 * a:64 * a + 64, n * 512:(n + 1) * 512], hs_[a][:, k, :], dn_c[a].v[:, k, n * 512:(n + 1) * 512],
                        k == 0, k == 3) for n in range(2) for k in range(4) for a in range(2)]
                tok = mm(lst, dn_c[0].tok, dn_c[1].tok, V.last())
                cp(A, yb, pg, tok)
                lst = [(psum[t][:, n * 512:(n + 1) * 512], ogT[:, t * P:(t + 1) * P], yb[:, n * 512:(n + 1) * 512], True, True)
                       for t in range(NT) for n in range(2)]
                tok = mm(lst, A.last())
                for t in range(NT):
                    tt(V, acc[:, t, :], acc[:, t, :], psum[t], ADD, tok)
                for _ in range(2):
                    ms(V, pad[0:1], 0.0)
                for q in (V, A, M):
                    q.join()
                for a in range(2):
                    for c in gu_c[a]:
                        c.free = (M.sem, m0 + 1 + a)
                    dn_c[a].free = M.last()
            give_back()
            for k in range(4):
                pfree[k] = [V.last(), A.last()]
            dmp(f"moe{l}", acc)
            layer_norm(lambda t: acc[:, t, :], lni)
            barrier()

        def rwkv():
            apos[0] = 0

            def big():
                return carve(2048).rearrange("p (k s) -> p k s", k=KT)

            def flat(a):
                return a.rearrange("p k s -> p (k s)")

            rT, kT, kk, aT, Lc = (big() for _ in range(5))
            vt = carve(2048).rearrange("p (t n) -> p t n", t=NT)
            gt = carve(2048).rearrange("p (t n) -> p t n", t=NT)
            bon = carve(32).rearrange("p (t h) -> p t h", t=NT)
            pc = carve(32).rearrange("p (k c) -> p k c", k=KT)
            st = carve(512).rearrange("p (k n) -> p k n", k=KT)
            mark = apos[0]
            xx, xm, lw = (big() for _ in range(3))
            lo1 = carve(512)
            xe = to_T(x, hT, V.last())
            ts(V, xx[:, :, 0:1], hT[:, :, 0:1], -1.0, None, MUL, None, *xe)
            tt(V, xx[:, :, 1:S], hT[:, :, 0:S - 1], hT[:, :, 1:S], SUB)

            def mix(i):
                for k in range(KT):
                    stt(xm[:, k, :], xx[:, k, :], vcol("mu", 8 * i + k), hT[:, k, :], MUL, ADD, M.last())
                return V.last()

            for n, d in ((0, rT), (1, kT)):
                xw = mix(n)
                for half in range(2):
                    c = load_cols(T["rw_w_rkv_2"][0, n], 512 * half, 512)
                    i, p = ps()
                    tok = proj_T(c.v, xm, KT, [(p[:, m * 256:(m + 1) * 256], slice(m * P, (m + 1) * P)) for m in range(4)],
                                 c.tok, xw, *pfree[i])
                    c.free = M.last()
                    pfree[i] = [cp(A, d[:, 4 * half:4 * half + 4, :], p.rearrange("p (k s) -> p k s", k=4), tok)]
            xw = mix(2)
            for half in range(2):
                c = load_cols(T["rw_w_rkv_2"][0, 2], 512 * half, 512)
                i, p = ps()
                o3 = p.rearrange("p (t n) -> p t n", t=NT)
                tok = proj_tok(xm, c.v, KT, [o3[:, t, :] for t in range(NT)], slice(0, 512), c.tok, xw, *pfree[i])
                c.free = M.last()
                pfree[i] = [cp(A, vt[:, :, 512 * half:512 * half + 512], o3, tok)]
            c = load((cols(288), T["lora1"].rearrange("(k p) n -> p k n", p=P)))
            lv = c.ap[:, 0:KT * 288].rearrange("p (k n) -> p k n", k=KT)
            c2 = load((lambda s: s[:, 0:1024], T["lora2"]), (lambda s: s[:, 1024:2048], T["rw_g2_2"][0, 0:128]),
                      (lambda s: s[0:32, 2048:3072], T["rw_g2_2"][0, 128:160]))
            lora2, g2a, g2b = c2.ap[:, 0:1024], c2.ap[:, 1024:2048], c2.ap[0:32, 2048:3072]
            loT = lo1[:, 0:256]
            xw = mix(3)
            i, p = ps()
            tok = mm([(p[0:64, 0:256], lv[:, k, 0:64], xm[:, k, :], k == 0, k == 7) for k in range(KT)], c.tok, xw, *pfree[i])
            e = act(loT[0:64], p[0:64, 0:256], ACT.Tanh, tok)
            pfree[i] = [e]
            xw = mix(4)
            i, p = ps()
            tok = mm([(p[64:128, 0:256], lv[:, k, 64:128], xm[:, k, :], k == 0, k == 7) for k in range(KT)], xw, *pfree[i])
            e = cp(A, loT[64:128], p[64:128, 0:256], tok)
            pfree[i] = [e]
            xw = mix(5)
            i, p = ps()
            lst = [(p[:, 0:256], lv[:, k, 128:256], xm[:, k, :], k == 0, k == 7) for k in range(KT)]
            lst += [(p[0:32, 256:512], lv[:, k, 256:288], xm[:, k, :], k == 0, k == 7) for k in range(KT)]
            tok = mm(lst, xw, *pfree[i])
            c.free = M.last()
            sg = xx[:, 0:2, :]
            act(sg[:, 0, :], p[:, 0:256], ACT.Sigmoid, tok, V.last())
            e = act(sg[0:32, 1, :], p[0:32, 256:512], ACT.Sigmoid)
            pfree[i] = [e]
            for t in range(NT):
                i, p = ps()
                tok = mm([(p[:, n * 512:(n + 1) * 512], a[:, t * P:(t + 1) * P], b[:, n * 512:(n + 1) * 512], a is not sgb, a is sgb)
                          for n in range(2) for sgb in (sg[0:32, 1, :],) for a, b in ((sg[:, 0, :], g2a), (sgb, g2b))],
                         e, c2.tok, *pfree[i])
                pfree[i] = [cp(V, gt[:, t, :], p, tok)]
            for base, dst, bias in ((0, lw, "w0"), (64, aT, "a0")):
                for half in range(2):
                    i, p = ps()
                    tok = mm([(p[:, n * 256:(n + 1) * 256], lora2[base:base + 64, (4 * half + n) * P:(4 * half + n + 1) * P],
                               loT[base:base + 64, :], True, True) for n in range(4)], A.last(), *pfree[i])
                    for n in range(4):
                        e = act(dst[:, 4 * half + n, :], p[:, n * 256:(n + 1) * 256], ACT.Sigmoid, tok,
                                bias=vcol(bias, 4 * half + n))
                    pfree[i] = [e]
            c2.free = M.last()
            ts(V, flat(lw), flat(lw), -math.exp(-0.5), None, MUL, None, A.last())
            for k in range(KT):
                ts(V, kk[:, k, :], kT[:, k, :], vcol("kk", k), None, MUL, None)
            tt(V, flat(xm), flat(kk), flat(kk), MUL, M.last())
            for half in range(2):
                i, p = ps()
                tok = mm([(p[:, n * 512:(n + 1) * 512], tab["blk"], xm[:, 4 * half + 2 * n:4 * half + 2 * n + 2, :], True, True)
                          for n in range(2)], V.last(), *pfree[i])
                x4 = flat(xx)[:, 1024 * half:1024 * half + 1024]
                ts(V, x4, p, 1e-24, None, MAX, None, tok)
                pfree[i] = [V.last()]
            act(flat(xx), flat(xx), ACT.Sqrt, V.last())
            rec(flat(xx), flat(xx), A.last())
            tt(V, flat(kk), flat(kk), flat(xx), MUL)
            for k in range(KT):
                ts(V, xm[:, k, :], aT[:, k, :], vcol("ka", k), vcol("ka", k), MUL, SUB)
            stt(flat(kT), flat(xm), 1.0, flat(kT), ADD, MUL)
            for k in range(KT):
                stt(xm[:, k, :], rT[:, k, :], vcol("rk", k), kT[:, k, :], MUL, MUL)
            i, p = ps()
            tok = mm([(p[:, t * 512 + 2 * k:t * 512 + 2 * k + 2], xm[:, k, t * P:(t + 1) * P], tab["hnd"], True, True)
                      for t in range(NT) for k in range(KT)], V.last(), *pfree[i])
            pfree[i] = [cp(V, bon, two(p, 16), tok)]
            for k in range(KT):
                V.add(lambda e, k=k: e.tensor_tensor_scan(Lc[:, k, :], tab["rst"], lw[:, k, :], 0.0, MUL, ADD))
            act(flat(xx), flat(Lc), ACT.Exp, V.last())
            tt(V, flat(rT), flat(rT), flat(xx), MUL, A.last())
            cp(V, pc, xx.rearrange("p k (c s) -> p k c s", c=4)[:, :, :, 63])
            tt(V, flat(lw), flat(Lc), flat(lw), SUB)
            act(flat(xm), flat(lw), ACT.Exp, V.last(), M.last())
            act(flat(xx), flat(Lc), ACT.Exp, V.last(), scale=-1.0)
            tt(V, flat(kT), flat(kT), flat(xx), MUL, A.last())
            tt(V, flat(aT), flat(aT), flat(kk), MUL)
            tt(V, flat(aT), flat(aT), flat(xx), MUL)
            stt(flat(kk), flat(kk), -1.0, flat(xm), MUL, MUL)
            bT, aa = aT, kk
            barrier()
            apos[0] = mark
            B = {n: carve(1024) for n in ("X", "Y", "ak", "rb", "rk")}
            for n, big_ in (("N Dm", Lc), ("N2 D2", hT), ("N4 D4", mT)):
                for m, name in enumerate(n.split()):
                    B[name] = flat(big_)[:, 1024 * m:1024 * m + 1024]
            U, B["mv"], B["btok"], B["ktok"], B["y"] = B["N2"], B["D2"], B["N4"], B["D4"], B["X"]
            ms(V, st.rearrange("p k n -> p (k n)"), 0.0)

            def u3(a):
                return a.rearrange("p (u n) -> p u n", u=16)

            def hs(u):
                return 64 * (u // 8), u % 8

            def each(p, lhs, rhs, start=True, stop=True):
                return [(p[64 * c:64 * c + 64, u * 64:(u + 1) * 64], lhs[64 * c:64 * c + 64, u * 64:(u + 1) * 64],
                         rhs[64 * c:64 * c + 64, u * 64:(u + 1) * 64], start, stop) for u in range(16) for c in range(2)]

            def mask(k):
                return bc(tab[k].unsqueeze(1), [P, 16, 64])

            def prod(lhs, rhs, *w):
                i, p = ps()
                tok = mm(each(p, lhs, rhs), *w, *pfree[i])
                return i, p, tok

            for t in range(NT):
                def pair(l_, r_):
                    i, p = ps()
                    lst = []
                    for c in range(2):
                        tk = slice(t * P + 64 * c, t * P + 64 * c + 64)
                        for k in range(KT):
                            for hh in range(2):
                                b = 64 * hh
                                lst.append((p[64 * c:64 * c + 64, hh * 512 + k * 64:hh * 512 + (k + 1) * 64],
                                            l_[b:b + 64, k, tk], r_[b:b + 64, k, tk], True, True))
                    return i, p, mm(lst, V.last(), *pfree[i])

                for dst, l_, r_, m in ((B["N"], bT, aa, "mlt"), (B["Dm"], aa, bT, "mgt"), (B["ak"], kT, aa, "mlt"),
                                       (B["rb"], bT, rT, "mle"), (B["rk"], kT, rT, "mle")):
                    i, p, tok = pair(l_, r_)
                    e = tt(V, u3(dst), u3(p), mask(m), MUL, tok)
                    pfree[i] = [e]
                X, Y, N2, D2, N4, D4 = B["X"], B["Y"], B["N2"], B["D2"], B["N4"], B["D4"]
                tt(V, u3(N2), u3(B["N"]), mask("m16"), MUL)
                tt(V, u3(D2), u3(B["Dm"]), mask("n16"), MUL)
                tt(V, u3(Y), u3(N2), mask("i64"), ADD)
                tt(V, u3(X), u3(D2), mask("i64"), ADD)
                n_, d_, nn, dn = N2, D2, N4, D4
                for step in range(3):
                    i, p, tok = prod(d_, n_, V.last())
                    i2, p2, tok2 = prod(n_, d_)
                    pfree[i] = [cp(A, nn, p, tok)]
                    pfree[i2] = [cp(V, dn, p2, tok2)]
                    i, p, tok = prod(dn, Y, V.last(), A.last())
                    i2, p2, tok2 = prod(nn, X)
                    pfree[i] = [tt(V, Y, Y, p, ADD, tok, tok2)]
                    pfree[i2] = [tt(V, X, X, p2, ADD)]
                    n_, d_, nn, dn = nn, dn, n_, d_
                for lev, (mn, md) in enumerate((("m32", "n32"), ("m64", "n64"))):
                    tt(V, u3(N2), u3(B["N"]), mask(mn), MUL)
                    tt(V, u3(D2), u3(B["Dm"]), mask(md), MUL)
                    i, p, tok = prod(D2, Y, V.last())
                    i2, p2, tok2 = prod(N2, X)
                    pfree[i] = [cp(A, N4, p, tok)]
                    pfree[i2] = [cp(V, D4, p2, tok2)]
                    i, p, tok = prod(X, N4, A.last())
                    i2, p2, tok2 = prod(Y, D4, V.last())
                    pfree[i] = [tt(V, Y, Y, p, ADD, tok, tok2)]
                    pfree[i2] = [tt(V, X, X, p2, ADD)]
                for src, dst in ((bT, B["btok"]), (kT, B["ktok"])):
                    i, p = ps()
                    tok = tr([(p[:, k * P:(k + 1) * P], src[:, k, t * P:(t + 1) * P], idn) for k in range(KT)], *pfree[i])
                    pfree[i] = [cp(A, dst, p, tok, M.last())]
                vtt = vt[:, t, :].rearrange("p (k a n) -> p a k n", k=8, a=2)

                def vu(c, u):
                    hh, k = u // 8, u % 8
                    return vtt[64 * c:64 * c + 64, hh, k, :]

                def blk_(a, c, u):
                    return a[64 * c:64 * c + 64, u * 64:(u + 1) * 64]

                i, p = ps()
                tok = mm([(blk_(p, c, u), blk_(B["ak"], c, u), vu(c, u), True, True) for u in range(16) for c in range(2)],
                         *pfree[i])
                pfree[i] = [cp(V, B["mv"], p, tok)]
                for c in range(2):
                    rows = slice(64 * c, 64 * c + 64)
                    tk = slice(t * P + 64 * c, t * P + 64 * c + 64)
                    i, p = ps()
                    tok = mm([(blk_(p, c, u), aa[64 * (u // 8):64 * (u // 8) + 64, u % 8, tk],
                               st[64 * (u // 8):64 * (u // 8) + 64, u % 8, :], True, True) for k in range(8) for u in (k, 8 + k)],
                             V.last(), *pfree[i])
                    i2, p2 = ps()
                    tok2 = mm([(blk_(p2, c, u), rT[64 * (u // 8):64 * (u // 8) + 64, u % 8, tk],
                                st[64 * (u // 8):64 * (u // 8) + 64, u % 8, :], True, True) for k in range(8) for u in (k, 8 + k)],
                              *pfree[i2])
                    pfree[i] = [tt(V, B["mv"][rows], B["mv"][rows], p[rows], ADD, tok)]
                    pfree[i2] = [cp(A, B["y"][rows], p2[rows], tok2)]
                    i, p = ps()
                    tok = mm([(blk_(p, c, u), blk_(Y, c, u), blk_(B["mv"], c, u), True, True) for u in range(16)], V.last(), *pfree[i])
                    pfree[i] = [cp(V, U[rows], p[rows], tok)]
                    i, p = ps()
                    lst = []
                    for u in range(16):
                        lst.append((blk_(p, c, u), blk_(B["rb"], c, u), blk_(U, c, u), True, False))
                        lst.append((blk_(p, c, u), blk_(B["rk"], c, u), vu(c, u), False, True))
                    i2, p2 = ps()
                    lst2 = []
                    for u in range(16):
                        hh, k = u // 8, u % 8
                        o = p2[64 * hh:64 * hh + 64, k * 64:(k + 1) * 64]
                        hc = slice((2 * k + hh) * 64, (2 * k + hh) * 64 + 64)
                        lst2.append((o, B["btok"][rows, hc], blk_(U, c, u), True, False))
                        lst2.append((o, B["ktok"][rows, hc], vu(c, u), False, True))
                    tok2 = mm(lst2, V.last(), A.last(), *pfree[i2])
                    tok = mm(lst, *pfree[i])
                    s2 = st.rearrange("p k n -> p (k n)")
                    tt(V, s2, s2, p2[:, 0:512], ADD, tok2)
                    pfree[i2] = [V.last()]
                    tt(V, st, st, bc(pc[:, :, 2 * t + c:2 * t + c + 1], [P, 8, 64]), MUL)
                    pfree[i] = [tt(V, B["y"][rows], B["y"][rows], p[rows], ADD, tok)]
                cp(V, hb[:, t, :].rearrange("p (k a n) -> p a k n", k=8, a=2),
                   B["y"].rearrange("p (a k n) -> p a k n", a=2, k=8))
            dmp("wkv", hb)
            r, rtok = rows_in(4)
            h16 = hb.rearrange("p t (h n) -> p (t h) n", h=16)
            sq = flat(rT).rearrange("p (u n) -> p u n", u=32)
            mu, va = carve(32), carve(32)
            red(mu, h16, ADD, M.last())
            ts(V, mu, mu, 1.0 / 64, None, MUL, None)
            tt(V, h16, h16, bc(mu.unsqueeze(2), [P, 32, 64]), SUB)
            tt(V, sq, h16, h16, MUL)
            red(va, sq, ADD)
            rms_scale(va, 64, 64e-5)
            tt(V, h16, h16, bc(va.unsqueeze(2), [P, 32, 64]), MUL)
            tt(V, hb, hb, bc(r[:, 0:1, :], [P, 2, D]), MUL, rtok)
            lnfree[0] = tt(V, hb, hb, bc(r[:, 1:2, :], [P, 2, D]), ADD)
            tt(V, sq, vt.rearrange("p t (h n) -> p (t h) n", h=16),
               bc(bon.rearrange("p t h -> p (t h)").unsqueeze(2), [P, 32, 64]), MUL)
            tt(V, h16, h16, sq, ADD)
            tt(V, hb, hb, gt, MUL)
            oT = kT
            e = to_T(hb, oT, V.last())
            out_proj(T["rw_w_o_2"][0], oT, 3, *e)

        s_o = sem("s_o")
        if stop is None or stop[0] != "l":
            final_norm()
            dmp("x1", x)
            if stop != "fn":
                diff_attention()
                dmp("xa", x)
                if stop != "da":
                    if stop != "rw":
                        moe(0, 2)
                        dmp("xm0", x)
                    if stop != "m0":
                        rwkv()
                        dmp("xr", x)
                        if stop != "rw":
                            moe(1, 5)
        A.dma(out.rearrange("b (t p) d -> p (b t) d", p=P), x, s_o, [V.last()])
        A.items.append((lambda e: None, [(s_o, 16)], None, 0))
        for d in dumps:
            A.items.append((lambda e: None, [d], None, 0))

        block = ctx.enter_context(nc.Block())

        @block.sync
        def _(eng):
            W.emit(eng)

        @block.gpsimd
        def _(eng):
            G.emit(eng)

        @block.scalar
        def _(eng):
            A.emit(eng)

        @block.tensor
        def _(eng):
            M.emit(eng)

        @block.vector
        def _(eng):
            V.emit(eng)


_VECS = (("norm_g", 16), ("qn", 4), ("kvn", 2), ("nb1", 4), ("nb2", 2), ("bm", 64), ("mu", 48), ("w0", 8), ("a0", 8),
         ("kk", 8), ("ka", 8), ("rk", 8))
_ROWS = (("subln", 128), ("lam", 256), ("mb", 72), ("nb2v", 128))


def vec_layout():
    o, out = 0, {}
    for n, w in _VECS:
        out[n] = o
        o += w
    return out


def row_layout():
    o, out = 0, {}
    for n, w in _ROWS:
        out[n] = o
        o += w
    return out


def layout(i):
    def colmaj(a):
        return np.ascontiguousarray(a.reshape(-1, P).T)

    tabs = tables()
    qn = np.zeros((L1, 256), np.float32)
    qn[:, :192] = i["mla_q_norm"]
    v = {
        "norm_g": colmaj(i["norm_g"]), "qn": colmaj(qn), "kvn": colmaj(i["mla_kv_norm"]), "nb1": colmaj(i["nsa_b1"]),
        "nb2": colmaj(np.concatenate([i["nsa_b2"][:, 0], i["nsa_b2"][:, 0]], axis=1)), "bm": colmaj(i["b_merge"]),
        "mu": colmaj(i["rw_mu_2"]), "w0": colmaj(i["rw_w0_2"]), "a0": colmaj(i["rw_a0_2"]), "kk": colmaj(i["rw_k_k_2"]),
        "ka": colmaj(i["rw_k_a_2"]), "rk": colmaj(i["rw_r_k_2"]),
    }
    r = {
        "subln": i["attn_subln_g_2"].reshape(-1), "lam": i["attn_lambda_2"].reshape(-1),
        "mb": np.concatenate([i["moe_rg_b_2"], i["moe_re_b_2"]], axis=1).reshape(-1), "nb2v": i["nsa_b2"][:, 1].reshape(-1),
    }
    vecs = np.concatenate([v[n] for n, _ in _VECS], axis=1)
    rows = np.tile(np.concatenate([r[n] for n, _ in _ROWS])[None], (P, 1))
    pairs = [(i["final_norm_g"], i["final_norm_g"])]
    pairs += [(i["ln1_g_2"][0], i["ln1_b_2"][0]), (i["ln2_g_2"][0], i["ln2_b_2"][0]), (i["ln1_g_2"][1], i["ln1_b_2"][1]),
              (i["rw_lnx_g_2"][0], i["rw_lnx_b_2"][0]), (i["ln2_g_2"][1], i["ln2_b_2"][1])]
    lrows = np.stack([np.tile(np.stack(p)[None], (P, 1, 1)) for p in pairs])
    common = [k for k in tabs if k not in FIRST_TABLES and k[0:2] != "cz"]
    arrays = {
        "x": i["x"], "vecs": vecs, "rows": rows, "lrows": lrows,
        "tcom": np.concatenate([tabs[k] for k in common], axis=1),
        "tfirst": np.concatenate([tabs[k] for k in FIRST_TABLES], axis=1),
        "cz0": tabs["cz0"], "cz1": tabs["cz1"],
        "pos": i["nsa_pos"].transpose(0, 1, 3, 2).reshape(L1, P, 32),
        "wr": np.concatenate([i["moe_rg_w_2"], i["moe_re_w_2"]], axis=2),
        "lora1": np.concatenate([i["rw_w1_2"][0], i["rw_a1_2"][0], i["rw_g1_2"][0]], axis=1),
        "lora2": np.concatenate([i["rw_w2_2"][0], i["rw_a2_2"][0]], axis=0),
    }
    for n in ("w_in", "mla_w_uq", "mla_w_ukv", "nsa_w1", "nsa_w2", "w_branch", "w_merge", "w_out", "attn_w_qkv_2",
              "attn_w_o_2", "rw_w_rkv_2", "rw_w_o_2", "rw_g2_2", "moe_w_gu_2", "moe_w_down_2"):
        arrays[n] = i[n]
    return {k: np.ascontiguousarray(a) for k, a in arrays.items()}


def kernel(**inputs):
    import concourse.bacc as bacc
    from concourse.bass_utils import run_bass_kernel_spmd

    arrays = layout({k: np.asarray(a) for k, a in inputs.items()})
    nc = bacc.Bacc("TRN2", target_bir_lowering=False, num_devices=1)
    T = {k: nc.dram_tensor(f"in_{k}", a.shape, mybir.dt.from_np(a.dtype), kind="ExternalInput").ap() for k, a in arrays.items()}
    out = nc.dram_tensor("out", (1, S, D), F, kind="ExternalOutput").ap()
    program(nc, T, out)
    r = run_bass_kernel_spmd(nc, [{f"in_{k}": a for k, a in arrays.items()}], core_ids=[0])
    return r.results[0]["out"]
```

```python
import math
from contextlib import ExitStack

import numpy as np
import concourse.bass as bass
from concourse import mybir

F = mybir.dt.float32
ALU = mybir.AluOpType
ACT = mybir.ActivationFunctionType
AX = mybir.AxisListType.X
ADD, SUB, MUL, MAX, MIN = ALU.add, ALU.subtract, ALU.mult, ALU.max, ALU.min

P = 128
S = 256
D = 1024
NT = 2
KT = 8
L1 = 2
RING = 4
MORE = 3
CAP = 64
SLOT = 4096
NEG = -1e30
E = 32
ALPHA = 4.0 ** 0.25
HORD = (0, 2, 1, 3)


def tables():
    s = 2.0 ** -(np.arange(8) + 1.0)
    sl_a, sl_c = s[0::2], s[1::2]
    t = np.arange(S)
    dist = t[:, None] - t[None, :]
    cnt = np.zeros((S, S))
    for win, dil in ((128, 1), (512, 4), (2048, 16)):
        cnt += (dist >= 0) & (dist % dil == 0) & (dist <= win)
    lc = np.where(cnt > 0, np.log(np.maximum(cnt, 1)), NEG)
    causal = np.where(dist >= 0, 0.0, NEG)
    out = {}

    def per_tile(name, full):
        for tt in range(NT):
            w = P * (tt + 1)
            out[f"{name}{tt}"] = full[:, tt * P:(tt + 1) * P, :w].transpose(1, 0, 2).reshape(P, 4 * w)

    per_tile("ba", np.stack([np.where(cnt > 0, lc - sl_a[h] * dist, NEG) for h in HORD]))
    per_tile("bc", np.stack([np.where(dist >= 0, -sl_c[h] * dist, NEG) for h in HORD]))
    per_tile("cz", np.stack([causal] * 4))
    dc = t[:, None] - (np.arange(15) * 16 + 31)[None, :]
    cmp_b = np.full((NT, P, 4, 32), NEG)
    for u, h in enumerate(HORD):
        b = np.where(dc >= 0, -sl_c[h] * dc, NEG)
        cmp_b[:, :, u, :15] = b.reshape(NT, P, 15)
    for tt in range(NT):
        out[f"cm{tt}"] = cmp_b[tt].reshape(P, 128)
    strict = (t[:, None] < t[None, :]).astype(np.float64)
    out["st0"] = strict[:P, :]
    out["st1"] = strict[P:, P:]
    inv = 10000.0 ** (-np.arange(16) / 16.0)
    ang = (t[:, None] * inv[None, :]).reshape(NT, P, 16)
    for name, f in (("cos", np.cos), ("sin", np.sin)):
        v = f(ang).transpose(1, 0, 2)
        v = np.repeat(v[:, :, None, :], 4, axis=2).reshape(P, 8, 16)
        out[name] = np.concatenate([v, v], axis=1).reshape(P, 256)
    out["idn"] = np.eye(P)
    i = np.arange(P)
    out["upp"] = (i[:, None] > i[None, :]).astype(float)
    out["one"] = np.ones((P, P))
    out["hnd32"] = (i[:, None] // 64 == np.arange(32)[None, :]).astype(float)
    out["dnh"] = (i[:, None] % 32 == i[None, :] // 64).astype(float)
    out["hnd"] = (i[:, None] // 64 == np.arange(2)[None, :]).astype(float)
    a, b = i[:, None] % 64, np.arange(64)[None, :]
    out["mlt"] = (a < b).astype(float)
    out["mle"] = (a <= b).astype(float)
    out["m16"] = ((a < b) & (a // 16 == b // 16)).astype(float)
    out["n16"] = ((a > b) & (a // 16 == b // 16)).astype(float)
    out["m32"] = ((a < b) & (a // 16 != b // 16) & (a // 32 == b // 32)).astype(float)
    out["n32"] = ((a > b) & (a // 16 != b // 16) & (a // 32 == b // 32)).astype(float)
    out["m64"] = ((a < b) & (a // 32 != b // 32)).astype(float)
    out["n64"] = ((a > b) & (a // 32 != b // 32)).astype(float)
    out["mgt"] = (a > b).astype(float)
    out["i64"] = (a == b).astype(float)
    out["iog"] = np.tile(np.arange(4.0), (P, 1))
    out["ios"] = np.tile(np.arange(64.0), (P, 1))
    out["ioe"] = np.tile(np.arange(32.0), (P, 1))
    out["rst"] = np.tile((np.arange(S) % 64 != 0).astype(float), (P, 1))
    return {k: np.ascontiguousarray(v, np.float32) for k, v in out.items()}


FIRST_TABLES = ("ba0", "ba1", "bc0", "bc1", "cm0", "cm1", "st0", "cos", "sin", "upp")


class Queue:

    def __init__(self, name, sem, chained):
        self.name, self.sem, self.chained = name, sem, chained
        self.items, self.n, self.first = [], 0, []

    def add(self, fn, waits=(), inc=1, chain=None):
        waits = list(waits) + self.first
        self.first = []
        if (self.chained if chain is None else chain) and self.n:
            waits.append((self.sem, self.n))
        self.items.append((fn, waits, self.sem if inc else None, 1))
        self.n += 1 if inc else 0
        return (self.sem, self.n)

    def dma(self, out, in_, sem, waits=()):
        self.items.append((lambda e: e.dma_start(out, in_), list(waits) + self.first, sem, 16))
        self.first = []

    def last(self):
        return (self.sem, self.n)

    def ago(self, k):
        return (self.sem, self.n - k)

    def wait_for(self, eng, waits, seen):
        for w in waits:
            w = w() if callable(w) else w
            if w is None:
                continue
            s, v = w
            if v > seen.get(id(s), 0) and not (s is self.sem and not self.chained):
                eng.wait_ge(s, v)
                seen[id(s)] = v

    def split(self, flag, waits):
        self.outer, self.n0 = self.items, self.n
        self.items = []
        self.fl = (flag, list(waits) + self.first)
        self.first = []

    def other(self):
        self.yes, self.n1 = self.items, self.n
        self.items, self.n = [], self.n0

    def join(self):
        assert self.n == self.n1, (self.name, self.n - self.n0, self.n1 - self.n0)
        self.outer.append((self.fl[0], self.fl[1], (self.yes, self.items), None))
        self.items = self.outer

    def emit(self, eng, items=None, seen=None):
        seen = {} if seen is None else seen
        for fn, waits, sem, by in self.items if items is None else items:
            self.wait_for(eng, waits, seen)
            if by is None:
                flag = eng.value_load(fn, min_val=0, max_val=1)
                a, b = dict(seen), dict(seen)
                with eng.If(flag != 0):
                    self.emit(eng, sem[0], a)
                with eng.Else():
                    self.emit(eng, sem[1], b)
                seen.update({k: min(a[k], b[k]) for k in a if k in b})
                continue
            ins = fn(eng)
            if sem is not None:
                ins.then_inc(sem, by)


class Chunk:

    def __init__(self, ap, tok):
        self.ap, self.tok, self.free = ap, tok, None


def program(nc, T, out, stop=None, dump=None):
    tabs = tables()
    with ExitStack() as ctx:
        def sb(name, w, parts=P):
            return ctx.enter_context(nc.sbuf_tensor(name, [parts, w], F))[:, :]

        def sem(name):
            return ctx.enter_context(nc.semaphore(name))

        V = Queue("vector", sem("sv"), True)
        A = Queue("scalar", sem("sa"), True)
        G = Queue("gpsimd", sem("sg"), True)
        M = Queue("tensor", sem("sm"), False)
        W = Queue("sync", sem("sw"), False)
        queues = (V, A, G, M, W)

        psum = [ctx.enter_context(nc.psum_tensor(f"ps{i}", [P, 1024], F))[:, :] for i in range(4)]
        pfree = [[] for _ in range(4)]
        pnext = [0]

        held = set()

        def ps():
            while pnext[0] % 4 in held:
                pnext[0] += 1
            i = pnext[0] % 4
            pnext[0] += 1
            return i, psum[i]

        def tt(q, o, a, b, op, *w, **k):
            return q.add(lambda e: e.tensor_tensor(o, a, b, op), w, **k)

        def ts(q, o, a, s1, s2, op0, op1, *w, **k):
            if op1 is None:
                return q.add(lambda e: e.tensor_scalar(o, a, s1, None, op0), w, **k)
            return q.add(lambda e: e.tensor_scalar(o, a, s1, s2, op0, op1), w, **k)

        def stt(o, a, s, b, op0, op1, *w, **k):
            return V.add(lambda e: e.scalar_tensor_tensor(out=o, in0=a, scalar=s, in1=b, op0=op0, op1=op1), w, **k)

        def red(o, a, op, *w, **k):
            return V.add(lambda e: e.tensor_reduce(o, a, AX, op), w, **k)

        def rec(o, a, *w, **k):
            return V.add(lambda e: e.reciprocal(o, a), w, **k)

        def cp(q, o, a, *w, **k):
            if q is A:
                return q.add(lambda e: e.activation(o, a, ACT.Copy), w, **k)
            return q.add(lambda e: e.tensor_copy(o, a), w, **k)

        def act(o, a, f, *w, bias=None, scale=1.0, acc=None, **k):
            kw = {"scale": scale}
            if bias is not None:
                kw["bias"] = bias
            if acc is not None:
                kw["accum_out"] = acc
            return A.add(lambda e: e.activation(o, a, f, **kw), w, **k)

        def ms(q, o, v, *w):
            return q.add(lambda e: e.memset(o, v), w)

        def mm(lst, *w):
            tok = None
            for n, (o, l, r, s0, s1) in enumerate(lst):
                end = n == len(lst) - 1
                tok = M.add(lambda e, o=o, l=l, r=r, s0=s0, s1=s1:
                            e.matmul(o, l, r, start=s0, stop=s1, skip_group_check=True),
                            w if n == 0 else (), inc=1 if end else 0)
            return tok

        def tr(lst, *w):
            tok = None
            for n, (o, i, idt) in enumerate(lst):
                end = n == len(lst) - 1
                tok = M.add(lambda e, o=o, i=i, idt=idt: e.transpose(o, i, idt), w if n == 0 else (),
                            inc=1 if end else 0)
            return tok

        def barrier():
            toks = [q.last() for q in queues if q.n and q is not W]
            for q in (V, A, G, M):
                q.first += [t for t in toks if t[0] is not q.sem]

        def bc(ap, shape):
            return ap.to_broadcast(shape)

        ring = [sb(f"ring{i}", SLOT) for i in range(RING)]
        rsem = [sem(f"sr{i}") for i in range(RING + MORE)]
        rcount = [0] * (RING + MORE)
        rwait = [None] * (RING + MORE)
        order = list(range(RING))

        def lend(aps, waits):
            for m, ap in enumerate(aps):
                ring.append(ap)
                rwait[RING + m] = list(waits)
                order.insert(0, RING + m)

        def give_back():
            del ring[RING:]
            order[:] = [k for k in order if k < RING]

        def load(*parts):
            k = order.pop(0)
            order.append(k)
            old = rwait[k]
            for j, (dst, src) in enumerate(parts):
                waits = []
                if j == 0 and old is not None:
                    waits = old if isinstance(old, list) else [lambda: old.free]
                W.dma(dst(ring[k]), src, rsem[k], waits)
                rcount[k] += 16
            rwait[k] = c = Chunk(ring[k], (rsem[k], rcount[k]))
            return c

        def cols(w, kt=KT):
            return lambda s: s[:, 0:kt * w].rearrange("p (k n) -> p k n", k=kt)

        def wsrc(ap, c0, w):
            return ap.rearrange("(k p) n -> p k n", p=P)[:, :, c0:c0 + w]

        def load_cols(ap, c0, w):
            c = load((cols(w, ap.shape[0] // P), wsrc(ap, c0, w)))
            c.v = c.ap[:, 0:ap.shape[0] // P * w].rearrange("p (k n) -> p k n", n=w)
            return c

        x = sb("x", 2 * D).rearrange("p (t d) -> p t d", t=NT)
        hb = sb("hb", 2 * D).rearrange("p (t d) -> p t d", t=NT)
        hT = sb("hT", 2 * D).rearrange("p (k s) -> p k s", k=KT)
        mT = sb("mT", 2 * D).rearrange("p (k s) -> p k s", k=KT)
        small = sb("small", 256)
        arena = sb("arena", 21900)
        apos = [0]

        def carve(w):
            a = arena[:, apos[0]:apos[0] + w]
            apos[0] += w
            assert apos[0] <= 21900, apos[0]
            return a

        s_c, s_f = sem("s_c"), sem("s_f")
        nload = {id(s_c): 0, id(s_f): 0}

        def start_load(dst, src, s=s_f):
            A.dma(dst, src, s)
            nload[id(s)] += 16

        tab = {}
        common = [k for k in tabs if k not in FIRST_TABLES and k[0:2] != "cz"]
        wc = sum(tabs[k].shape[1] for k in common)
        tcom = sb("tcom", wc)
        o = 0
        for k in common:
            tab[k] = tcom[:, o:o + tabs[k].shape[1]]
            o += tabs[k].shape[1]
        for tt_ in range(NT):
            tab[f"cz{tt_}"] = sb(f"cz{tt_}", tabs[f"cz{tt_}"].shape[1])
        vec = sb("vec", T["vecs"].shape[1])
        row = sb("row", T["rows"].shape[1])
        rw36 = sb("rw36", 2 * KT * 36).rearrange("p (l k n) -> p l k n", l=2, k=KT)
        lnr = [sb(f"lnr{i}", 2 * D).rearrange("p (a d) -> p a d", a=2) for i in range(1)]
        s_ln = [sem(f"s_ln{i}") for i in range(1)]
        nln = [0]
        lnfree = [None]

        def rows_in(i):
            w = [lnfree[0]] if lnfree[0] else []
            G.dma(lnr[0], T["lrows"][i], s_ln[0], w)
            nln[0] += 16
            return lnr[0], (s_ln[0], nln[0])

        s_x = sem("s_x")
        A.dma(x, T["x"].rearrange("b (t p) d -> p (b t) d", p=P), s_x)
        start_load(tcom, T["tcom"], s_c)
        start_load(vec, T["vecs"], s_c)
        A.first.append((rsem[1], 16))
        start_load(row, T["rows"])
        for k in FIRST_TABLES:
            tab[k] = carve(tabs[k].shape[1])
        wf = apos[0]
        start_load(arena[:, 0:wf], T["tfirst"])
        for tt_ in range(NT):
            start_load(tab[f"cz{tt_}"], T[f"cz{tt_}"])
        for l in range(2):
            start_load(rw36[:, l], T["wr"][l].rearrange("(k p) n -> p k n", p=P))
        w_uq = [carve(2 * 384).rearrange("p (k n) -> p k n", k=2) for _ in range(L1)]
        w_ukv = [carve(512) for _ in range(L1)]
        w2n = [carve(128).rearrange("p (a n) -> p a n", a=2) for _ in range(L1)]
        posT = [carve(32) for _ in range(L1)]
        for l in range(L1):
            start_load(w_uq[l][:, 0], T["mla_w_uq"][l, 0:P])
            start_load(w_uq[l][0:64, 1], T["mla_w_uq"][l, P:192])
            start_load(w_ukv[l], T["mla_w_ukv"][l])
            start_load(w2n[l], T["nsa_w2"][l].rearrange("a p n -> p a n"))
            start_load(posT[l], T["pos"][l])
        C0, F0 = (s_c, nload[id(s_c)]), (s_f, nload[id(s_f)])
        X0 = (s_x, 16)
        for q in (V, A, G, M):
            q.first += [C0, X0]
        W.first += [C0, X0]
        idn = tab["idn"]

        VO, RO = vec_layout(), row_layout()

        def vcol(name, k=0, parts=slice(0, P)):
            o = VO[name] + k
            return vec[parts, o:o + 1]

        def rrow(name, w, off=0):
            o = RO[name] + off
            return row[:, o:o + w]

        sm_pos = [0]

        def sml(w):
            if sm_pos[0] + w > 256:
                sm_pos[0] = 0
            o = sm_pos[0]
            sm_pos[0] += w
            return small[:, o:o + w]

        def rms_scale(ss, n, eps, *w):
            t = ts(V, ss, ss, 1.0 / n, eps, MUL, ADD, *w)
            t = act(ss, ss, ACT.Sqrt, t)
            return rec(ss, ss, t)

        def to_T(src, dst, *w, scale=None):
            toks = []
            for half in range(2):
                i, p = ps()
                lst = [(p[:, (k % 4) * 256 + t * P:(k % 4) * 256 + t * P + P],
                        src[:, t, k * P:(k + 1) * P], idn) for k in range(4 * half, 4 * half + 4) for t in range(NT)]
                tok = tr(lst, *w, *pfree[i])
                q = V if half else A
                if scale is None:
                    e = cp(q, dst[:, 4 * half:4 * half + 4, :], p.rearrange("p (k s) -> p k s", k=4), tok)
                else:
                    for k in range(4 * half, 4 * half + 4):
                        pk = p[:, (k % 4) * 256:(k % 4) * 256 + 256]
                        if q is V:
                            e = ts(V, dst[:, k, :], pk, scale(k), None, MUL, None, tok)
                        else:
                            e = act(dst[:, k, :], pk, ACT.Copy, tok, scale=scale(k))
                pfree[i] = [e]
                toks.append(e)
            return toks

        def proj_T(lhs, rhs, nk, outs, *w):
            lst = []
            for o, c in outs:
                for k in range(nk):
                    lst.append((o, lhs[:, k, c], rhs[:, k, :], k == 0, k == nk - 1))
            return mm(lst, *w)

        def proj_tok(lhs, rhs, nk, o, c, *w):
            lst = []
            for t in range(NT):
                for k in range(nk):
                    lst.append((o[t], lhs[:, k, t * P:(t + 1) * P], rhs[:, k, c], k == 0, k == nk - 1))
            return mm(lst, *w)

        def silu(dst, src, tmp, *w):
            act(tmp, src, ACT.Sigmoid, *w)
            return tt(V, dst, src, tmp, MUL, A.last())

        def two(p, w):
            return p.rearrange("p (a n) -> p a n", a=2)[:, :, 0:w]

        Sb, Pb, PTb = ([carve(512), carve(1024)] for _ in range(3))
        base_first = apos[0]

        def score_mm(score, *w):
            i, p = ps()
            held.add(i)
            return i, p, mm(score(p), *w, *pfree[i])

        def scores4(t, score, SL, scale, bias, guard, *w):
            i, p, tok = score if isinstance(score, tuple) else score_mm(score, *w)
            s_ = Sb[t][:, 0:4 * SL]
            e = stt(s_.rearrange("p (a n) -> p a n", a=2), two(p, 2 * SL), scale,
                    bias.rearrange("p (a n) -> p a n", a=2), MUL, ADD, tok, A.last())
            pfree[i] = [e]
            held.remove(i)
            mx = sml(4)
            red(mx, s_.rearrange("p (u n) -> p u n", u=4), MAX)
            ts(V, mx, mx, -1.0, 1e29 if guard else None, MUL, MIN if guard else None)
            return mx

        def exps4(t, mx, SL, guard):
            sm = sml(4)
            p4 = Pb[t][:, 0:4 * SL].rearrange("p (u n) -> p u n", u=4)
            e = V.last()
            for u in range(4):
                act(p4[:, u, :], Sb[t][:, u * SL:(u + 1) * SL], ACT.Exp, e, M.last(), bias=mx[:, u:u + 1],
                    acc=sm[:, u:u + 1])
            return p4, sm, A.last()

        def sums4(sm, tok, guard):
            if guard:
                ts(V, sm, sm, 1e-30, None, MAX, None, tok)
            return rec(sm, sm, tok)

        def attn4(score, scale, bias, vals, dst, fill, *w):
            got = {}
            for t in (1, 0):
                mx = scores4(t, score(t), P * (t + 1), scale, bias(t), False, *w)
                got[t] = exps4(t, mx, P * (t + 1), False)
            fill()
            pts = {}
            for t in (1, 0):
                p4, ri, tok = got[t]
                sums4(ri, tok, False)
                i, p = ps()
                tok = tr([(p[:, (u * (t + 1) + s) * P:(u * (t + 1) + s + 1) * P], p4[:, u, s * P:(s + 1) * P], idn)
                          for u in range(4) for s in range(t + 1)], tok, *pfree[i])
                pts[t] = cp(A, PTb[t], p[:, 0:512 * (t + 1)], tok)
                pfree[i] = [pts[t]]
            for t in (1, 0):
                ri, pt = got[t][1], PTb[t]
                i, p = ps()
                lst = []
                for u, h in enumerate(HORD):
                    for s in range(t + 1):
                        lst.append((p[:, u * 64:(u + 1) * 64], pt[:, (u * (t + 1) + s) * P:(u * (t + 1) + s + 1) * P],
                                    vals(h, s), s == 0, s == t))
                tok = mm(lst, pts[t], *pfree[i])
                d4 = dst(t).rearrange("p (j a) n -> p a j n", j=2)
                e = tt(V, d4, p[:, 0:256].rearrange("p (a j n) -> p a j n", a=2, j=2),
                       bc(ri.rearrange("p (a j) -> p a j", a=2).unsqueeze(3), [P, 2, 2, 64]), MUL, tok)
                pfree[i] = [e]
            return e

        def dmp(name, ap):
            if dump is not None and name in dump:
                s_ = sem(f"s_d{name}")
                W.dma(dump[name], ap, s_, [q.last() for q in (V, A, G, M) if q.n])
                dumps.append((s_, 16))
                for q in (V, A, G, M):
                    q.first.append((s_, 16))

        dumps = []

        def first_layer(l):
            apos[0] = base_first
            gate = carve(512).rearrange("p (t n) -> p t n", t=NT)
            y = carve(512).rearrange("p (t n) -> p t n", t=NT)
            sgates = [a.rearrange("p a b -> p (a b)") for a in (mT, hb, lnr[0])]
            yT = [carve(512).rearrange("p (k s) -> p k s", k=2) for _ in range(4)]
            qT = carve(512).rearrange("p (j s) -> p j s", j=2)
            kT = carve(512).rearrange("p (j s) -> p j s", j=2)
            v = carve(512).rearrange("p (t n) -> p t n", t=NT)
            tmp = carve(1024)

            ss = sml(2)
            for t in range(NT):
                act(hb[:, t, :], x[:, t, :], ACT.Square, V.last() if V.n else X0, acc=ss[:, t:t + 1])
            rms_scale(ss, D, 1e-6, A.last())
            for t in range(NT):
                ts(V, hb[:, t, :], x[:, t, :], ss[:, t:t + 1], None, MUL, None)
            hTok = to_T(hb, hT, V.last(), scale=lambda k: vcol("norm_g", 8 * l + k))
            win = T["w_in"][l]

            def tok_major(c, w, c0=0):
                i, p = ps()
                o = p.rearrange("p (t n) -> p t n", t=NT)
                tok = proj_tok(hT, c.v, KT, [o[:, t, 0:w] for t in range(NT)], slice(c0, c0 + w),
                               c.tok, *hTok, *pfree[i])
                return i, two(p, w), tok

            def gate_of(i, src, tok, g):
                e = silu(g, src, tmp[:, 0:512].rearrange("p (t n) -> p t n", t=NT), tok, V.last())
                pfree[i] = [e]

            def heads_T(c, c0, dsts):
                i, p = ps()
                tok = proj_T(c.v, hT, KT, [(p[:, n * 256:(n + 1) * 256], slice(c0 + n * P, c0 + (n + 1) * P))
                                           for n in range(2 * len(dsts))], c.tok, *hTok, *pfree[i])
                for n, d in enumerate(dsts):
                    e = cp(A, d, p[:, n * 512:(n + 1) * 512].rearrange("p (j s) -> p j s", j=2), tok, M.last())
                pfree[i] = [e]
                return e

            def score_qk(q, k, t):
                SL = P * (t + 1)

                def go(p):
                    return [(p[:, hh * 512 + j * SL:hh * 512 + (j + 1) * SL],
                             q[64 * hh:64 * hh + 64, j, t * P:(t + 1) * P],
                             k(hh, j)[:, 0:SL], True, True) for j in range(2) for hh in range(2)]
                return go

            def merge_gate(b, half, dst):
                c = load_cols(T["w_merge"][l, b], 512 * half, 512)

                def step(m):
                    i, p = ps()
                    tok = proj_T(c.v, hT, KT, [(p[:, n * 256:(n + 1) * 256], slice((2 * m + n) * P, (2 * m + n + 1) * P))
                                               for n in range(2)], c.tok, *pfree[i])
                    if m:
                        c.free = M.last()
                    for n in range(2):
                        k = 2 * m + n
                        act(dst[:, k * 256:(k + 1) * 256], p[:, n * 256:(n + 1) * 256], ACT.Sigmoid, tok,
                            bias=vcol("bm", 32 * l + 8 * b + 4 * half + k))
                    pfree[i] = [A.last()]
                return step

            gates_left = [(b, half) for b in range(3) for half in range(2)]

            def fill():
                b, half = gates_left.pop(0)
                step = merge_gate(b, half, sgates[b][:, 1024 * half:1024 * half + 1024])
                step(0)
                step(1)

            def finish_branch(b, gated=False):
                if not gated:
                    tt(V, y, y, gate, MUL)
                i, p = ps()
                tok = tr([(p[:, k * 256 + t * P:k * 256 + t * P + P], y[:, t, k * P:(k + 1) * P], idn)
                          for k in range(2) for t in range(NT)], V.last(), *pfree[i])
                pfree[i] = [cp(A, yT[b], p[:, 0:512].rearrange("p (k s) -> p k s", k=2), tok)]

            def y4(t):
                return y[:, t, :].rearrange("p (h n) -> p h n", h=4)

            c = load_cols(win, 0, 512)
            qe = heads_T(c, 0, (qT, kT))
            c.free = M.last()
            c = load_cols(win, 512, 512)
            i, pv, tok = tok_major(c, 512)
            c.free = M.last()
            ve = cp(V, v, pv[:, :, 0:256], tok)
            gate_of(i, pv[:, :, 256:512], tok, gate)
            for q in (V, M):
                q.first.append(F0)
            attn4(lambda t: score_qk(qT, lambda hh, j: kT[64 * hh:64 * hh + 64, j], t), 0.125, lambda t: tab[f"ba{t}"],
                  lambda h, s: v[:, s, h * 64:(h + 1) * 64], y4, fill, qe, ve)
            dmp(f"y{l}0", y)
            finish_branch(0)

            barrier()
            b0 = apos[0]
            cq = carve(704).rearrange("p (t n) -> p t n", t=NT)
            cT = carve(768).rearrange("p (k s) -> p k s", k=3)
            qk = carve(512).rearrange("p (u n) -> p u n", u=16)
            rp = carve(512).rearrange("p (u n) -> p u n", u=16)
            rT = carve(256).rearrange("p (k s) -> p k s", k=1)
            c = load_cols(win, 1024, 352)
            i, pv, tok = tok_major(c, 352)
            c.free = M.last()
            e = cp(V, cq, pv, tok)
            pfree[i] = [e]
            ss = sml(4)
            for t in range(NT):
                act(tmp[:, 0:192], cq[:, t, 0:192], ACT.Square, e, acc=ss[:, t:t + 1])
                act(tmp[:, 0:128], cq[:, t, 192:320], ACT.Square, acc=ss[:, 2 + t:3 + t])
            ts(V, ss[:, 0:2], ss[:, 0:2], 1.0 / 192, 1e-6, MUL, ADD, A.last())
            ts(V, ss[:, 2:4], ss[:, 2:4], 1.0 / 128, 1e-6, MUL, ADD)
            act(ss, ss, ACT.Sqrt, V.last())
            rec(ss, ss, A.last())
            for t in range(NT):
                ts(V, cq[:, t, 0:192], cq[:, t, 0:192], ss[:, t:t + 1], None, MUL, None)
                ts(V, cq[:, t, 192:320], cq[:, t, 192:320], ss[:, 2 + t:3 + t], None, MUL, None)
            i, p = ps()
            tok = tr([(p[0:m, k * 256 + t * P:k * 256 + t * P + P], cq[:, t, o:o + m], idn)
                      for k, (o, m) in enumerate(((0, 128), (128, 64), (192, 128))) for t in range(NT)],
                     V.last(), *pfree[i])
            ts(V, cT[:, 0, :], p[:, 0:256], vcol("qn", 2 * l), None, MUL, None, tok)
            ts(V, cT[0:64, 1, :], p[0:64, 256:512], vcol("qn", 2 * l + 1, slice(0, 64)), None, MUL, None)
            e = ts(V, cT[:, 2, :], p[:, 512:768], vcol("kvn", l), None, MUL, None)
            pfree[i] = [e]
            i, p = ps()
            lst = []
            for h in range(4):
                j, hh = h // 2, h % 2
                o = p[64 * hh:64 * hh + 64, j * 256:(j + 1) * 256]
                lst.append((o, w_uq[l][:, 0, h * 96:h * 96 + 64], cT[:, 0, :], True, False))
                lst.append((o, w_uq[l][0:64, 1, h * 96:h * 96 + 64], cT[0:64, 1, :], False, True))
            for h in range(4):
                j, hh = h // 2, h % 2
                lst.append((p[64 * hh:64 * hh + 64, 512 + j * 256:512 + (j + 1) * 256],
                            w_ukv[l][:, h * 128:h * 128 + 64], cT[:, 2, :], True, True))
            tok = mm(lst, e, *pfree[i])
            cp(A, qT, p[:, 0:512].rearrange("p (j s) -> p j s", j=2), tok)
            e2 = cp(A, kT, p[:, 512:1024].rearrange("p (j s) -> p j s", j=2))
            pfree[i] = [e2]
            i, p = ps()
            lst = []
            wq4 = w_uq[l].rearrange("p k (h n) -> p k h n", h=4)
            wv4 = w_ukv[l].rearrange("p (h n) -> p h n", h=4)
            for t in range(NT):
                tk = slice(t * P, (t + 1) * P)
                lst.append((p[:, t * P:(t + 1) * P], cT[:, 0, tk], wq4[:, 0, :, 64:96], True, False))
                lst.append((p[:, t * P:(t + 1) * P], cT[0:64, 1, tk], wq4[0:64, 1, :, 64:96], False, True))
            for t in range(NT):
                lst.append((p[:, 512 + t * 256:512 + (t + 1) * 256], cT[:, 2, t * P:(t + 1) * P],
                            wv4[:, :, 64:128], True, True))
            tok = mm(lst, *pfree[i])
            cp(V, qk[:, 0:8, :], p[:, 0:256].rearrange("p (u n) -> p u n", u=8), tok)
            ve = cp(V, v, p[:, 512:1024].rearrange("p (t n) -> p t n", t=NT))
            pfree[i] = [ve]
            for t in range(NT):
                cp(V, qk[:, 8 + 4 * t:12 + 4 * t, :], bc(cq[:, t, 320:352].unsqueeze(1), [P, 4, 32]))
            cos = tab["cos"].rearrange("p (u n) -> p u n", u=16)
            sin = tab["sin"].rearrange("p (u n) -> p u n", u=16)
            t1 = tmp[:, 0:256].rearrange("p (u n) -> p u n", u=16)
            x1, x2 = qk[:, :, 0:16], qk[:, :, 16:32]
            tt(V, rp[:, :, 0:16], x1, cos, MUL)
            tt(V, t1, x2, sin, MUL)
            tt(V, rp[:, :, 0:16], rp[:, :, 0:16], t1, SUB)
            tt(V, rp[:, :, 16:32], x1, sin, MUL)
            tt(V, t1, x2, cos, MUL)
            e = tt(V, rp[:, :, 16:32], rp[:, :, 16:32], t1, ADD)
            i, p = ps()
            rpf = rp.rearrange("p u n -> p (u n)")
            tok = tr([(p[:, k * 256 + t * P:k * 256 + t * P + P], rpf[:, (k * 2 + t) * P:(k * 2 + t + 1) * P], idn)
                      for k in range(2) for t in range(NT)], e, *pfree[i])
            cp(V, rT[:, 0, :], p[:, 0:256], tok)
            krm = tmp.rearrange("p (h s) -> p h s", h=4)
            ms(V, tmp, 0.0)
            for h in range(4):
                cp(V, krm[32 * h:32 * h + 32, h, :], p[32 * h:32 * h + 32, 256:512])
            e = V.last()
            pfree[i] = [e]
            def score_b(t):
                SL = P * (t + 1)
                tk = slice(t * P, (t + 1) * P)

                def go(p):
                    lst = []
                    for j in range(2):
                        for hh in range(2):
                            o = p[:, hh * 512 + j * SL:hh * 512 + (j + 1) * SL]
                            lst.append((o, qT[64 * hh:64 * hh + 64, j, tk], kT[64 * hh:64 * hh + 64, j, 0:SL], True, False))
                            lst.append((o, rT[:, 0, tk], krm[:, 2 * j + hh, 0:SL], False, True))
                    return lst
                return go
            attn4(score_b, 96.0 ** -0.5, lambda t: tab[f"cz{t}"], lambda h, s: v[:, s, h * 64:(h + 1) * 64],
                  y4, fill, e, e2, ve)
            barrier()
            apos[0] = b0

            c = load_cols(win, 1376, 512)
            i, pv, tok = tok_major(c, 256)
            gate_of(i, pv, tok, gate)
            dmp(f"y{l}1", y)
            finish_branch(1)
            qe = heads_T(c, 256, (qT,))
            c.free = M.last()
            kcv = carve(256)
            ksd, kwd = carve(256), carve(256)
            vs, vw = (carve(128).rearrange("p (t n) -> p t n", t=NT) for _ in range(2))
            cg = carve(24).rearrange("p (t n) -> p t n", t=NT)
            blk = carve(480).rearrange("p (q n) -> p q n", q=32)
            hid = carve(64).rearrange("p (a n) -> p a n", a=2)
            kcd = carve(32)
            vcb = carve(256)
            ob = carve(512).rearrange("p (t n) -> p t n", t=NT)
            c = load_cols(win, 1888, 396)
            i, p = ps()
            lst = [(p[:, 0:256], c.v[:, k, 0:128], hT[:, k, :], k == 0, k == 7) for k in range(KT)]
            for n, c0 in enumerate((128, 256)):
                for hh in range(2):
                    lst += [(p[64 * hh:64 * hh + 64, 512 + n * 256:768 + n * 256], c.v[:, k, c0:c0 + 64], hT[:, k, :],
                             k == 0, k == 7) for k in range(KT)]
            tok = mm(lst, c.tok, *hTok, *pfree[i])
            cp(V, kcv, p[:, 0:256], tok)
            cp(V, ksd, p[:, 512:768])
            e = cp(V, kwd, p[:, 768:1024])
            pfree[i] = [e]
            i, p = ps()
            lst = []
            for t in range(NT):
                for c0, w, o0 in ((192, 64, 0), (320, 76, 64)):
                    lst += [(p[:, t * 512 + o0:t * 512 + o0 + w], hT[:, k, t * P:(t + 1) * P], c.v[:, k, c0:c0 + w],
                             k == 0, k == 7) for k in range(KT)]
            tok = mm(lst, *pfree[i])
            c.free = M.last()
            o = p.rearrange("p (t n) -> p t n", t=NT)
            cp(V, vs, o[:, :, 0:64], tok)
            cp(V, vw, o[:, :, 64:128])
            act(cg, o[:, :, 128:140], ACT.Exp, V.last(), scale=-1.0)
            pfree[i] = [A.last()]
            ts(V, cg, cg, 1.0, None, ADD, None, A.last())
            rec(cg, cg)
            c = load(*[((lambda a: lambda s: s[64 * a:64 * a + 64, :].rearrange("d (q c) -> d q c", q=32))(a),
                        T["nsa_w1"][l, a].rearrange("(q d) c -> d q c", d=64)) for a in range(2)])
            w1v = c.ap.rearrange("d (q c) -> d q c", q=32)
            for q_ in range(2):
                win_ap = kcv[:, 16 * q_:16 * q_ + 240].rearrange("p (n q) -> p q n", q=16)
                tt(V, blk[:, 16 * q_:16 * q_ + 16, :], win_ap, bc(posT[l][:, 16 * q_:16 * q_ + 16].unsqueeze(2), [P, 16, 15]), ADD)
            i, p = ps()
            tok = mm([(p[:, a * 512:a * 512 + 15], w1v[64 * a:64 * a + 64, q, :], blk[64 * a:64 * a + 64, q, :],
                       q == 0, q == 31) for q in range(32) for a in range(2)], c.tok, V.last(), *pfree[i])
            c.free = M.last()
            ms(V, hid, 0.0, tok)
            g1, g2 = tmp[:, 0:32].rearrange("p (a n) -> p a n", a=2), tmp[:, 32:64].rearrange("p (a n) -> p a n", a=2)
            g1, g2 = g1[:, :, 0:15], g2[:, :, 0:15]
            h15 = hid[:, :, 0:15]
            for a in range(2):
                ts(V, h15[:, a, :], p[:, a * 512:a * 512 + 15], vcol("nb1", 2 * l + a), None, ADD, None)
            pfree[i] = [V.last()]
            tt(V, g1, h15, h15, MUL)
            ts(V, g1, g1, 0.044715, 1.0, MUL, ADD)
            tt(V, g1, g1, h15, MUL)
            act(g2, g1, ACT.Exp, V.last(), scale=-2.0 * 0.7978845608028654)
            ts(V, g2, g2, 1.0, None, ADD, None, A.last())
            rec(g2, g2)
            tt(V, h15, h15, g2, MUL)
            i, p = ps()
            lst = [(p[64 * hh:64 * hh + 64, 0:32], w2n[l][:, 0, :], hid[:, 0, :], True, True) for hh in range(2)]
            lst += [(p[32 * u:32 * u + 32, 512:576], hid[:, 1, :], w2n[l][:, 1, :], True, True) for u in range(4)]
            tok = mm(lst, V.last(), *pfree[i])
            ts(V, kcd, p[:, 0:32], vcol("nb2", l), None, ADD, None, tok)
            ms(V, vcb, 0.0)
            for u in range(4):
                tt(V, vcb[32 * u:32 * u + 32, u * 64:u * 64 + 64], p[32 * u:32 * u + 32, 512:576],
                   rrow("nb2v", 64, 64 * l)[32 * u:32 * u + 32], ADD)
            pfree[i] = [V.last()]
            kve = V.last()
            got = {}
            for t in (1, 0):
                tk = slice(t * P, (t + 1) * P)

                def score_c(p, tk=tk):
                    return [(p[:, hh * 512 + j * 32:hh * 512 + j * 32 + 32], qT[64 * hh:64 * hh + 64, j, tk],
                             kcd[64 * hh:64 * hh + 64, :], True, True) for j in range(2) for hh in range(2)]
                mx = scores4(t, score_c, 32, 0.125, tab[f"cm{t}"], True, qe, kve)
                got[t] = exps4(t, mx, 32, True)
            fill()
            for t in (1, 0):
                p4, ri, tok = got[t]
                sums4(ri, tok, True)
                i, p = ps()
                tok = tr([(p[:, 0:P], Pb[t][:, 0:P], idn)], tok, *pfree[i])
                e = cp(A, PTb[t][:, 0:P], p[:, 0:P], tok)
                pfree[i] = [e]
                i, p = ps()
                tok = mm([(p[:, 0:256], PTb[t][:, 0:P], vcb, True, True)], e, *pfree[i])
                d4 = y[:, t, :].rearrange("p (j a n) -> p a j n", j=2, a=2)
                pfree[i] = [tt(V, d4, p[:, 0:256].rearrange("p (a j n) -> p a j n", a=2, j=2),
                               bc(ri.rearrange("p (a j) -> p a j", a=2).unsqueeze(3), [P, 2, 2, 64]), MUL, tok)]
            y8 = y.rearrange("p t (h n) -> p (t h) n", h=4)
            o4 = ob.rearrange("p t (h n) -> p (t h) n", h=4)
            gg = [cg.rearrange("p t (h g) -> p (t h) g", g=3)[:, :, g:g + 1] for g in range(3)]
            tt(V, y8, y8, bc(gg[0], [P, 8, 64]), MUL)
            for n, (kd, vv) in enumerate(((ksd, vs), (kwd, vw))):
                attn4(lambda t: score_qk(qT, lambda hh, j: kd[64 * hh:64 * hh + 64, :], t), 0.125, lambda t: tab[f"bc{t}"],
                      lambda h, s: vv[:, s, :], lambda t: ob[:, t, :].rearrange("p (h n) -> p h n", h=4), fill, qe, kve)
                tt(V, o4, o4, bc(gg[1 + n], [P, 8, 64]), MUL)
                tt(V, y8, y8, o4, ADD)
            c = load_cols(win, 2284, 512)
            i, pv, tok = tok_major(c, 256)
            gate_of(i, pv, tok, gate)
            dmp(f"y{l}2", y)
            finish_branch(2)
            barrier()
            apos[0] = b0

            qe = heads_T(c, 256, (qT,))
            c.free = M.last()
            c = load_cols(win, 2796, 512)
            ke = heads_T(c, 0, (kT,))
            i, pv, tok = tok_major(c, 256, 256)
            c.free = M.last()
            ve = cp(V, v, pv, tok)
            pfree[i] = [ve]
            c = load_cols(win, 3308, 256)
            i, pv, tok = tok_major(c, 256)
            c.free = M.last()
            gate_of(i, pv, tok, gate)
            zb = [carve(1024), carve(512)]
            sp = [Sb[1], Sb[0]]
            lg = [Pb[1], Pb[0]]
            for s in range(2):
                w = S - s * P
                i, p = ps()
                tok = mm([(p[:, hh * 512 + j * w:hh * 512 + (j + 1) * w], kT[64 * hh:64 * hh + 64, j, s * P:(s + 1) * P],
                           qT[64 * hh:64 * hh + 64, j, s * P:S], True, True) for j in range(2) for hh in range(2)],
                         qe, ke, *pfree[i])
                z3 = zb[s].rearrange("p (a n) -> p a n", a=2)
                e = ts(V, z3, two(p, 2 * w), 0.125, None, MUL, None, tok)
                pfree[i] = [e]
                act(lg[s], zb[s], ACT.Abs, e)
                act(lg[s], lg[s], ACT.Exp, scale=-1.0)
                act(lg[s], lg[s], ACT.Ln, bias=1.0)
                e = stt(sp[s], zb[s], 0.0, lg[s], MAX, ADD, A.last())
                tt(V, zb[s], zb[s], sp[s], SUB)
                sp4 = sp[s].rearrange("p (u n) -> p u n", u=4)
                tt(V, sp4, sp4, bc(tab[f"st{s}"].unsqueeze(1), [P, 4, w]), MUL)
            fill()
            i, p = ps()
            lst = []
            for u in range(4):
                o = p[:, u * 256:(u + 1) * 256]
                lst.append((o, tab["upp"], sp[0][:, u * 256:(u + 1) * 256], True, False))
                lst.append((o[:, P:256], tab["one"], sp[1][:, u * P:(u + 1) * P], False, True))
            i2, p2 = ps()
            tok = mm(lst, V.last(), *pfree[i])
            tok2 = mm([(p2[:, 0:512], tab["upp"], sp[1], True, True)], *pfree[i2])
            tt(V, zb[0], zb[0], p, SUB, tok)
            pfree[i] = [V.last()]
            tt(V, zb[1], zb[1], p2[:, 0:512], SUB, tok2)
            pfree[i2] = [V.last()]
            for s in range(2):
                w = S - s * P
                act(lg[s], zb[s], ACT.Exp, V.last())
                l4 = lg[s].rearrange("p (u n) -> p u n", u=4)
                tt(V, l4, l4, bc(tab[f"st{s}"].unsqueeze(1), [P, 4, w]), MUL, A.last())
            i, p = ps()
            lst = []
            for t in range(NT):
                for u, h in enumerate(HORD):
                    for s in range(t + 1):
                        w = S - s * P
                        a = lg[s][:, u * w + (t - s) * P:u * w + (t - s + 1) * P]
                        lst.append((p[:, t * 512 + h * 64:t * 512 + (h + 1) * 64], a, v[:, s, h * 64:(h + 1) * 64], s == 0, s == t))
            tok = mm(lst, V.last(), *pfree[i])
            tt(V, y, two(p, 256), gate, MUL, tok)
            pfree[i] = [V.last()]
            finish_branch(3, True)
            for b in range(4):
                cb = load_cols(T["w_branch"][l, b], 0, D)
                for half in range(2):
                    i2, p2 = ps()
                    tok2 = proj_T(cb.v, yT[b], 2, [(p2[:, n * 256:(n + 1) * 256], slice((4 * half + n) * P, (4 * half + n + 1) * P))
                                                   for n in range(4)], cb.tok, A.last(), *pfree[i2])
                    cb.free = M.last()
                    if b < 3:
                        sg = sgates[b][:, 1024 * half:1024 * half + 1024]
                    else:
                        sg = sg3[half]
                    e = tt(V, sg, sg, p2, MUL, tok2)
                    pfree[i2] = [e]
                    m3 = sgates[0][:, 1024 * half:1024 * half + 1024]
                    if b:
                        lnfree[0] = tt(V, m3, m3, sg, ADD)
                if b == 0:
                    sg3 = [tmp, Pb[1]]
                    for half in range(2):
                        step = merge_gate(3, half, sg3[half])
                        step(0)
                        step(1)
            dmp(f"mT{l}", mT)
            for half in range(2):
                c = load_cols(T["w_out"][l], 512 * half, 512)
                i, p = ps()
                o = p.rearrange("p (t n) -> p t n", t=NT)
                tok = proj_tok(mT, c.v, KT, [o[:, t, :] for t in range(NT)], slice(0, 512), c.tok, V.last(), *pfree[i])
                c.free = M.last()
                xs = x[:, :, 512 * half:512 * half + 512]
                pfree[i] = [tt(V, xs, xs, o, ADD, tok)]
            barrier()

        for l in range(L1):
            first_layer(l)
            if stop == f"l{l}":
                break

        def final_norm():
            r, rt = rows_in(0)
            ss = sml(2)
            for t in range(NT):
                act(hb[:, t, :], x[:, t, :], ACT.Square, acc=ss[:, t:t + 1])
            rms_scale(ss, D, 1e-6, A.last())
            for t in range(NT):
                lnfree[0] = stt(x[:, t, :], x[:, t, :], ss[:, t:t + 1], r[:, 0, :], MUL, MUL, rt)

        def layer_norm(src, rows, *w, tiles=(0, 1)):
            r, rt = rows
            ss = sml(2 * NT).rearrange("p (a t) -> p a t", a=2)
            ta, tb = [(V.sem, 0)] * NT, [(V.sem, 0)] * NT
            for t in tiles:
                e = stt(x[:, t, :], x[:, t, :], ALPHA, src(t), MUL, ADD, *w)
                ta[t] = act(hb[:, t, :], x[:, t, :], ACT.Copy, e, acc=ss[:, 0, t:t + 1])
            for t in tiles:
                e = ts(V, ss[:, 0, t:t + 1], ss[:, 0, t:t + 1], -1.0 / D, None, MUL, None, ta[t])
                tb[t] = act(hb[:, t, :], x[:, t, :], ACT.Square, e, bias=ss[:, 0, t:t + 1], acc=ss[:, 1, t:t + 1])
            for t in tiles:
                e = ts(V, ss[:, 1, t:t + 1], ss[:, 1, t:t + 1], 1.0 / D, 1e-5, MUL, ADD, tb[t])
                ta[t] = act(ss[:, 1, t:t + 1], ss[:, 1, t:t + 1], ACT.Sqrt, e)
            for t in tiles:
                rec(ss[:, 1, t:t + 1], ss[:, 1, t:t + 1], ta[t])
                stt(x[:, t, :], x[:, t, :], ss[:, 0, t:t + 1], r[:, 0, :], ADD, MUL, rt)
                lnfree[0] = stt(x[:, t, :], x[:, t, :], ss[:, 1, t:t + 1], r[:, 1, :], MUL, ADD)
            return V.last()

        def tile_T(t, src, dst, *w):
            i, p = ps()
            tok = tr([(p[:, k * P:(k + 1) * P], src[:, t, k * P:(k + 1) * P], idn) for k in range(KT)], *w, *pfree[i])
            d = dst[:, :, t * P:(t + 1) * P]
            pfree[i] = [cp(q, d[:, 4 * h:4 * h + 4], p[:, 512 * h:512 * h + 512].rearrange("p (k s) -> p k s", k=4), tok)
                        for h, q in enumerate((A, V))]
            return pfree[i]

        def diff_attention():
            apos[0] = 0
            qT = carve(2048).rearrange("p (h s) -> p h s", h=8)
            kT = carve(2048).rearrange("p (h s) -> p h s", h=8)
            v = carve(2048).rearrange("p (t n) -> p t n", t=NT)
            o = carve(2048).rearrange("p (t n) -> p t n", t=NT)
            oT = carve(2048).rearrange("p (k s) -> p k s", k=KT)
            for buf in (Sb, Pb, PTb):
                buf[:] = [carve(512), carve(1024)]
            tmp = carve(256)
            wq = T["attn_w_qkv_2"][0]
            xe = to_T(x, hT, V.last())
            lam = sml(4)
            for n in range(2):
                tt(V, tmp[:, 0:64], rrow("lam", 64, 128 * n), rrow("lam", 64, 128 * n + 64), MUL)
                red(lam[:, n:n + 1], tmp[:, 0:64], ADD)
            act(lam[:, 0:2], lam[:, 0:2], ACT.Exp, V.last())
            tt(V, lam[:, 2:3], lam[:, 1:2], lam[:, 0:1], SUB, A.last())
            lneg = carve(1)
            ts(V, lneg, lam[:, 2:3], 0.2, None, SUB, None)
            sub = carve(128)
            ts(V, sub, rrow("subln", 128), 0.8, None, MUL, None)
            ready = [[], []]

            def proj_qk(d, c0, half):
                c = load_cols(wq, c0 + 512 * half, 512)
                i, p = ps()
                tok = proj_T(c.v, hT, KT, [(p[:, m * 256:(m + 1) * 256], slice(m * P, (m + 1) * P)) for m in range(4)],
                             c.tok, *xe, *pfree[i])
                c.free = M.last()
                pfree[i] = [cp(A, d[:, 4 * half:4 * half + 4, :], p.rearrange("p (h s) -> p h s", h=4), tok)]
                ready[half] += pfree[i]

            def proj_v(half):
                c = load_cols(wq, 2048 + 512 * half, 512)
                i, p = ps()
                o3 = p.rearrange("p (t n) -> p t n", t=NT)
                tok = proj_tok(hT, c.v, KT, [o3[:, t, :] for t in range(NT)], slice(0, 512), c.tok, *pfree[i])
                c.free = M.last()
                pfree[i] = [cp(A, v[:, :, 512 * half:512 * half + 512], o3, tok)]

            def score(g, t):
                SL = P * (t + 1)

                def go(p):
                    return [(p[:, cc * 512 + hl * SL:cc * 512 + (hl + 1) * SL],
                             qT[64 * cc:64 * cc + 64, 2 * g + hl, t * P:(t + 1) * P],
                             kT[64 * cc:64 * cc + 64, 2 * g + hl, 0:SL], True, True)
                            for hl in range(2) for cc in range(2)]
                return go

            def front(g, t):
                SL = P * (t + 1)
                mx = scores4(t, scored.pop((g, t)), SL, 0.125, tab[f"cz{t}"], False)
                return exps4(t, mx, SL, False)

            def back(g, t, p4, ri, tok):
                SL = P * (t + 1)
                sums4(ri, tok, False)
                ts(V, ri[:, 2:4], ri[:, 2:4], lneg, None, MUL, None)
                s4 = Sb[t][:, 0:4 * SL].rearrange("p (u n) -> p u n", u=4)
                tt(V, s4, p4, bc(ri.unsqueeze(2), [P, 4, SL]), MUL)
                a = Sb[t][:, 0:2 * SL]
                e = tt(V, a, a, Sb[t][:, 2 * SL:4 * SL], ADD)
                i, p = ps()
                tok = tr([(p[:, n * P:(n + 1) * P], a[:, n * P:(n + 1) * P], idn) for n in range(2 * (t + 1))],
                         e, *pfree[i])
                pt = PTb[t][:, 0:2 * SL]
                e = cp(A, pt, p[:, 0:2 * SL], tok)
                pfree[i] = [e]
                i, p = ps()
                lst = []
                for hl in range(2):
                    for s in range(t + 1):
                        n = hl * (t + 1) + s
                        h = 2 * g + hl
                        lst.append((p[:, hl * P:(hl + 1) * P], pt[:, n * P:(n + 1) * P], v[:, s, h * P:(h + 1) * P], s == 0, s == t))
                tok = mm(lst, e, *pfree[i])
                pfree[i] = [cp(A, o[:, t, 2 * g * P:(2 * g + 2) * P], p[:, 0:256], tok)]

            units = [(g, t) for g in range(4) for t in (1, 0)]
            got = {}
            among = {0: lambda: proj_v(0), 1: lambda: proj_qk(qT, 0, 1), 2: lambda: proj_qk(kT, 1024, 1), 3: lambda: proj_v(1)}
            proj_qk(qT, 0, 0)
            proj_qk(kT, 1024, 0)
            scored = {units[0]: score_mm(score(*units[0]), *ready[0])}
            for n, un in enumerate(units):
                if n in among:
                    among[n]()
                if n + 1 < len(units):
                    nx = units[n + 1]
                    scored[nx] = score_mm(score(*nx), *ready[nx[0] // 2])
                got[un] = front(*un)
                if n:
                    back(*units[n - 1], *got[units[n - 1]])

            def head_norm(t):
                o8 = o[:, t, :].rearrange("p (h n) -> p h n", h=8)
                h8 = hb[:, t, :].rearrange("p (h n) -> p h n", h=8)
                ss = sml(8)
                tt(V, h8, o8, o8, MUL, A.last())
                red(ss, h8, ADD)
                rms_scale(ss, 128, 1e-5)
                tt(V, o8, o8, bc(ss.unsqueeze(2), [P, 8, 128]), MUL)
                return tt(V, o8, o8, bc(sub.unsqueeze(1), [P, 8, 128]), MUL)

            def part(t):
                def go():
                    wt = tile_T(t, o, oT, head_norm(t))
                    if t:
                        back(*units[-1], *got[units[-1]])
                    return wt
                return go

            out_proj(T["attn_w_o_2"][0], oT, 1, [(t, part(t)) for t in (1, 0)])

        def out_proj(w, srcT, lni, parts):
            cs = [load_cols(w, 512 * half, 512) for half in range(2)]
            got = []
            for t, ready in parts:
                wt = ready()
                i, p = ps()
                tok = mm([(p[:, 512 * half:512 * half + 512], srcT[:, k, t * P:(t + 1) * P], cs[half].v[:, k, :], k == 0, k == KT - 1)
                          for half in range(2) for k in range(KT)], cs[0].tok, cs[1].tok, *wt, *pfree[i])
                got.append((t, i, p, tok))
                held.add(i)
            for c in cs:
                c.free = M.last()
            rows = rows_in(lni)
            for t, i, p, tok in got:
                e = layer_norm(lambda t: p, rows, tok, tiles=(t,))
                pfree[i] = [e]
                held.remove(i)
                tile_T(t, x, hT, e)
            barrier()

        def route(l, gates, sel):
            i, p = ps()
            tok = proj_tok(hT, rw36[:, l], KT, [p[:, t * 512:t * 512 + 36] for t in range(NT)], slice(0, 36), *pfree[i])
            lo = carve(72).rearrange("p (t n) -> p t n", t=NT)
            e = tt(V, lo, two(p, 36), bc(rrow("mb", 36, 36 * l).unsqueeze(1), [P, 2, 36]), ADD, tok)
            pfree[i] = [e]
            gl, el = lo[:, :, 0:4], lo[:, :, 4:36]
            ex = carve(64).rearrange("p (t n) -> p t n", t=NT)
            eq = carve(64).rearrange("p (t n) -> p t n", t=NT)
            k1 = carve(64).rearrange("p (t n) -> p t n", t=NT)
            mx, gp, ix, m1, m2 = (carve(2) for _ in range(5))

            def col(a, n):
                return bc(a.unsqueeze(2), [P, 2, n])

            def first_of(dst, val, n, iota, m):
                tt(V, eq[:, :, 0:n], val, col(m, n), ALU.is_ge)
                ts(V, eq[:, :, 0:n], eq[:, :, 0:n], -1000.0, 1000.0, MUL, ADD)
                tt(V, eq[:, :, 0:n], eq[:, :, 0:n], bc(iota.unsqueeze(1), [P, 2, n]), ADD)
                red(ix, eq[:, :, 0:n], MIN)
                tt(V, dst, bc(iota.unsqueeze(1), [P, 2, n]), col(ix, n), ALU.is_equal)

            red(mx, gl, MAX)
            g4 = ex[:, :, 0:4]
            tt(V, g4, gl, col(mx, 4), SUB)
            act(g4, g4, ACT.Exp, V.last())
            red(gp, g4, ADD, A.last())
            rec(gp, gp)
            oh = carve(8).rearrange("p (t n) -> p t n", t=NT)
            first_of(oh, gl, 4, tab["iog"], mx)
            ts(V, oh, oh, -2 * NEG, NEG, MUL, ADD)
            oh8 = bc(oh.rearrange("p t g -> p (t g)").unsqueeze(2), [P, 8, 8])
            el8 = lambda a: a.rearrange("p t (g n) -> p (t g) n", g=4)
            em = carve(64).rearrange("p (t n) -> p t n", t=NT)
            ec = carve(64).rearrange("p (t n) -> p t n", t=NT)
            cp(V, ec, el)
            tt(V, el8(em), el8(ec), oh8, MIN)
            red(m1, em, MAX)
            o1 = k1
            first_of(o1, em, 32, tab["ioe"], m1)
            e2 = carve(64).rearrange("p (t n) -> p t n", t=NT)
            stt(e2.rearrange("p t n -> p (t n)"), o1.rearrange("p t n -> p (t n)"), 2 * NEG, em.rearrange("p t n -> p (t n)"), MUL, ADD)
            red(m2, e2, MAX)
            o2 = ex
            first_of(o2, e2, 32, tab["ioe"], m2)
            tt(V, m2, m2, m1, SUB)
            act(m2, m2, ACT.Exp, V.last())
            ts(V, m1, m2, 1.0, None, ADD, None, A.last())
            rec(m1, m1)
            tt(V, m1, m1, gp, MUL)
            tt(V, m2, m2, m1, MUL)
            tt(V, sel, o1, o2, ADD)
            tt(V, o1, o1, col(m1, 32), MUL)
            tt(V, o2, o2, col(m2, 32), MUL)
            tt(V, gates, o1, o2, ADD)

        def moe(l, lni):
            apos[0] = 0
            acc = mT.rearrange("p k s -> p (k s)").rearrange("p (t d) -> p t d", t=NT)
            gates = carve(64).rearrange("p (t n) -> p t n", t=NT)
            sel = carve(64).rearrange("p (t n) -> p t n", t=NT)
            pos = carve(64).rearrange("p (t n) -> p t n", t=NT)
            flag = carve(16).bitcast(mybir.dt.int32)
            pad = carve(1)
            xe = [carve(1024) for _ in range(2)]
            ogT = [carve(256) for _ in range(2)]
            oh, og = carve(256), carve(256)
            scratch = apos[0]
            gu = [carve(512), carve(512)]
            hs_ = [carve(256).rearrange("p (k n) -> p k n", k=4) for _ in range(2)]
            sg = [carve(256).rearrange("p (k n) -> p k n", k=4) for _ in range(2)]
            yb = carve(1024)
            end = apos[0]
            apos[0] = scratch
            hid = [carve(1024), carve(1024)]
            dsg = carve(1024)
            apos[0] = end
            lend([carve(SLOT) for _ in range(MORE)], [q.last() for q in (V, A, G, M)])
            apos[0] = scratch
            ms(G, acc, 0.0)
            route(l, gates, sel)
            dmp(f"g{l}", gates)
            i, p = ps()
            tok = mm([(p[:, 0:32], tab["st1"], sel[:, 0, :], True, True),
                      (p[:, 32:64], tab["st1"], sel[:, 1, :], True, False),
                      (p[:, 32:64], tab["one"], sel[:, 0, :], False, True),
                      (p[:, 64:96], tab["one"], sel[:, 0, :], True, False),
                      (p[:, 64:96], tab["one"], sel[:, 1, :], False, True)], V.last(), *pfree[i])
            ts(V, pos, sel, -1000.0, 1000.0, MUL, ADD)
            tt(V, pos, pos, p[:, 0:64].rearrange("p (t n) -> p t n", t=NT), ADD, tok)
            cnt = sml(16)
            red(cnt, p[:, 64:96].rearrange("p (q a) -> p q a", a=2), MAX)
            pfree[i] = [V.last()]
            ts(V, cnt, cnt, CAP + 0.5, None, ALU.is_gt, None)
            fl = cp(V, flag, cnt)
            barrier()
            pg, pt = psum[2], psum[3]
            oh4, og4 = (a.rearrange("p (t e n) -> p t e n", t=NT, e=2) for a in (oh, og))

            def places(pr, *w):
                pr = min(pr, E // 2 - 1)
                e2 = slice(2 * pr, 2 * pr + 2)
                tt(V, oh4, bc(pos[:, :, e2].unsqueeze(3), [P, 2, 2, CAP]),
                   bc(tab["ios"].unsqueeze(1).unsqueeze(1), [P, 2, 2, CAP]), ALU.is_equal, *w)
                tt(V, og4, oh4, bc(gates[:, :, e2].unsqueeze(3), [P, 2, 2, CAP]), MUL)

            def gather(pr, buf, buf2, *w):
                lst = [(buf[:, k * P:(k + 1) * P], x[:, t, k * P:(k + 1) * P], oh[:, t * P:(t + 1) * P], t == 0, t == 1)
                       for k in range(KT) for t in range(NT)]
                tok = mm(lst, *w)
                tok2 = tr([(buf2[:, t * P:(t + 1) * P], og[:, t * P:(t + 1) * P], idn) for t in range(NT)])
                d = xe[pr % 2]
                cp(A, d[:, 0:512], buf[:, 0:512], tok)
                cp(V, d[:, 512:1024], buf[:, 512:1024], tok)
                cp(A, ogT[pr % 2], buf2[:, 0:256], tok2)
                places(pr + 1, tok2)

            places(0)
            gather(0, psum[0], psum[1], V.last())
            for pr in range(E // 2):
                gu_c, dn_c = [], []
                for a in range(2):
                    wg = T["moe_w_gu_2"][l, 2 * pr + a]
                    gu_c.append([load_cols(wg, 0, 512), load_cols(wg, 512, 512)])
                for a in range(2):
                    dn_c.append(load_cols(T["moe_w_down_2"][l, 2 * pr + a], 0, D))
                m0 = M.n
                v_all, a_all = V.last(), A.last()
                v_in = V.ago(4) if pr else v_all
                for q in (V, A, M):
                    q.split(flag[0:1, pr:pr + 1], [fl])

                v_hid = v_in
                for a in range(2):
                    c0, c1 = gu_c[a]
                    lst = [(dst[:, n * 256:(n + 1) * 256], c.v[:, k, n * P:(n + 1) * P], hT[:, k, :], k == 0, k == KT - 1)
                           for dst, c in ((pg, c0), (pt, c1)) for n in range(4) for k in range(KT)]
                    tok = mm(lst, c0.tok, c1.tok, v_hid, a_all)
                    act(dsg, pg, ACT.Sigmoid, tok, V.last())
                    tt(V, hid[a], dsg, pg, MUL, A.last())
                    v_hid = tt(V, hid[a], hid[a], pt, MUL)
                if pr + 1 < E // 2:
                    gather(pr + 1, psum[0], psum[1], v_all)
                a_xe, v_xe = A.last(), V.last()
                for a in range(2):
                    h3 = hid[a].rearrange("p (k s) -> p k s", k=4)
                    for t in range(NT):
                        tok = mm([(psum[t][:, n * 512:(n + 1) * 512], h3[:, k, t * P:(t + 1) * P],
                                   dn_c[a].v[:, k, n * 512:(n + 1) * 512], k == 0, k == 3) for n in range(2) for k in range(4)],
                                 dn_c[a].tok, a_xe, v_xe if a == 0 else V.ago(1))
                        stt(acc[:, t, :], psum[t], gates[:, t, 2 * pr + a:2 * pr + a + 1], acc[:, t, :], MUL, ADD, tok)
                for _ in range(2):
                    mm([(pg[0:1, 0:1], idn[:, 0:1], idn[:, 0:1], True, True)], V.last())
                for _ in range(4):
                    act(pad[0:1], tab["one"][0:1, 0:1], ACT.Copy)

                for q in (V, A, M):
                    q.other()
                xp = xe[pr % 2].rearrange("p (k n) -> p k n", k=KT)
                for a in range(2):
                    c0, c1 = gu_c[a]
                    o = pg[:, 512 * a:512 * a + 512]
                    lst = [(o[64 * m:64 * m + 64, :], xp[:, k, a * CAP:(a + 1) * CAP], c.v[:, k, :], k == 0, k == KT - 1)
                           for k in range(KT) for m, c in enumerate((c0, c1))]
                    tok = mm(lst, c0.tok, c1.tok, v_in, a_all)
                    cp(A, gu[a], o, tok)
                a_gu = A.last()
                if pr + 1 < E // 2:
                    gather(pr + 1, pt, psum[1], v_all)
                for a in range(2):
                    o = psum[0][:, 512 * a:512 * a + 512]
                    tok = tr([(o[:, k * P:(k + 1) * P], gu[a][:, k * P:(k + 1) * P], idn) for k in range(4)], a_gu, v_all)
                    o4 = o.rearrange("p (k n) -> p k n", k=4)
                    act(sg[a], o4[:, :, 0:64], ACT.Sigmoid, tok)
                    tt(V, sg[a], sg[a], o4[:, :, 0:64], MUL, A.last())
                    tt(V, hs_[a], sg[a], o4[:, :, 64:128], MUL)
                v_hs = V.last()
                for n in range(2):
                    h = slice(n * 512, (n + 1) * 512)
                    tok = mm([(pg[64 * a:64 * a + 64, h], hs_[a][:, k, :], dn_c[a].v[:, k, h], k == 0, k == 3)
                              for k in range(4) for a in range(2)], dn_c[0].tok, dn_c[1].tok, v_hs)
                    cp(A, yb[:, h], pg[:, h], tok)
                for n in range(2):
                    h = slice(n * 512, (n + 1) * 512)
                    tok = mm([(psum[n][:, 512 * t:512 * t + 512], ogT[pr % 2][:, t * P:(t + 1) * P], yb[:, h], True, True)
                              for t in range(NT)], A.ago(1 - n))
                    for t in range(NT):
                        tt(V, acc[:, t, h], acc[:, t, h], psum[n][:, 512 * t:512 * t + 512], ADD, tok)
                for q in (V, A, M):
                    q.join()
                for a in range(2):
                    for c in gu_c[a]:
                        c.free = (M.sem, m0 + 1 + a)
                    dn_c[a].free = M.last()
            give_back()
            for k in range(4):
                pfree[k] = [V.last(), A.last()]
            dmp(f"moe{l}", acc)
            layer_norm(lambda t: acc[:, t, :], rows_in(lni))
            barrier()

        def rwkv():
            apos[0] = 0

            def big():
                return carve(2048).rearrange("p (k s) -> p k s", k=KT)

            def flat(a):
                return a.rearrange("p k s -> p (k s)")

            rT, kT, kk, aT, Lc = (big() for _ in range(5))
            vt = carve(2048).rearrange("p (t n) -> p t n", t=NT)
            gt = carve(2048).rearrange("p (t n) -> p t n", t=NT)
            bon = carve(32).rearrange("p (t h) -> p t h", t=NT)
            pc = carve(32).rearrange("p (k c) -> p k c", k=KT)
            st = carve(512).rearrange("p (k n) -> p k n", k=KT)
            mark = apos[0]
            xx, xa_, lw = (big() for _ in range(3))
            xb_, xc_ = mT, hb.rearrange("p t d -> p (t d)").rearrange("p (k s) -> p k s", k=KT)
            loT, om = carve(256), carve(8)
            xe = to_T(x, hT, V.last())
            ts(V, xx[:, :, 0:1], hT[:, :, 0:1], -1.0, None, MUL, None, *xe)
            tt(V, xx[:, :, 1:S], hT[:, :, 0:S - 1], hT[:, :, 1:S], SUB)

            def mix(i, dst, *w):
                for k in range(KT):
                    tok = stt(dst[:, k, :], xx[:, k, :], vcol("mu", 8 * i + k), hT[:, k, :], MUL, ADD, *w)
                return tok

            def proj(n, xw, src, d):
                for half in range(2):
                    c = load_cols(T["rw_w_rkv_2"][0, n], 512 * half, 512)
                    i, p = ps()
                    tok = proj_T(c.v, src, KT, [(p[:, m * 256:(m + 1) * 256], slice(m * P, (m + 1) * P)) for m in range(4)],
                                 c.tok, xw, *pfree[i])
                    c.free = tok
                    pfree[i] = [cp(A, d[:, 4 * half:4 * half + 4, :], p.rearrange("p (k s) -> p k s", k=4), tok)]
                return tok

            xk, xw, xa = mix(1, xa_), mix(3, xb_), mix(4, xc_)
            tk_ = proj(1, xk, xa_, kT)
            c = load((cols(288), T["lora1"].rearrange("(k p) n -> p k n", p=P)))
            lv = c.ap[:, 0:KT * 288].rearrange("p (k n) -> p k n", k=KT)
            c2 = load((lambda s: s[:, 0:1024], T["lora2"]), (lambda s: s[:, 1024:2048], T["rw_g2_2"][0, 0:128]),
                      (lambda s: s[0:32, 2048:3072], T["rw_g2_2"][0, 128:160]))
            lora2, g2a, g2b = c2.ap[:, 0:1024], c2.ap[:, 1024:2048], c2.ap[0:32, 2048:3072]
            i, p = ps()
            tw = mm([(p[0:64, 0:256], lv[:, k, 0:64], xb_[:, k, :], k == 0, k == 7) for k in range(KT)], c.tok, xw, *pfree[i])
            ta = mm([(p[64:128, 512:768], lv[:, k, 64:128], xc_[:, k, :], k == 0, k == 7) for k in range(KT)], xa)
            act(loT[0:64], p[0:64, 0:256], ACT.Tanh, tw)
            e = cp(A, loT[64:128], p[64:128, 512:768], ta)
            pfree[i] = [e]
            for k in range(KT):
                tkk = act(kk[:, k, :], kT[:, k, :], ACT.Copy, scale=vcol("kk", k))
            xr = mix(0, xa_, tk_)
            for base, dst, bias in ((0, lw, "w0"), (64, aT, "a0")):
                for half in range(2):
                    i, p = ps()
                    tok = mm([(p[:, n * 256:(n + 1) * 256], lora2[base:base + 64, (4 * half + n) * P:(4 * half + n + 1) * P],
                               loT[base:base + 64, :], True, True) for n in range(4)], e, c2.tok, *pfree[i])
                    for n in range(4):
                        t_ = act(dst[:, 4 * half + n, :], p[:, n * 256:(n + 1) * 256], ACT.Sigmoid, tok,
                                 bias=vcol(bias, 4 * half + n))
                    pfree[i] = [t_]
            tq = tt(V, flat(Lc), flat(kk), flat(kk), MUL, tkk)
            xg = mix(5, xb_, tw)
            xv = mix(2, xc_, ta)
            tr_ = proj(0, xr, xa_, rT)
            tr_e = A.last()
            i, p = ps()
            tok = mm([(p[32 * (k % 4):32 * (k % 4) + 32, 512 * (k // 4):512 * (k // 4) + 256], tab["hnd32"], Lc[:, k, :], True, True)
                      for k in range(KT)], tq, *pfree[i])
            ln = xx[:, 0:2, :]
            ts(V, ln, two(p, 256), 1e-24, None, MAX, None, tok)
            pfree[i] = [V.last()]
            act(ln, ln, ACT.Sqrt, V.last())
            tl = rec(ln, ln, A.last())
            tsum = tok
            i, p = ps()
            lst = [(p[:, 0:256], lv[:, k, 128:256], xb_[:, k, :], k == 0, k == 7) for k in range(KT)]
            lst += [(p[0:32, 256:512], lv[:, k, 256:288], xb_[:, k, :], k == 0, k == 7) for k in range(KT)]
            tg = tok = mm(lst, xg, *pfree[i])
            c.free = M.last()
            sg = xx[:, 2:4, :]
            act(sg[:, 0, :], p[:, 0:256], ACT.Sigmoid, tok, xv)
            e = act(sg[0:32, 1, :], p[0:32, 256:512], ACT.Sigmoid)
            pfree[i] = [e]
            kk4 = kk.rearrange("p (h n) s -> p n h s", h=2)
            for n0 in range(0, 4, 2):
                i, p = ps()
                tok = mm([(p[:, n * 512 + half * 256:n * 512 + half * 256 + 256], tab["dnh"][32 * (n0 + n):32 * (n0 + n) + 32, :],
                           ln[32 * (n0 + n):32 * (n0 + n) + 32, half, :], True, True) for half in range(2) for n in range(2)],
                         tl, *pfree[i])
                pfree[i] = [tt(V, kk4[:, n0:n0 + 2], kk4[:, n0:n0 + 2], p.rearrange("p (n h s) -> p n h s", n=2, h=2), MUL, tok)]
            tkk = V.last()
            for t in range(NT):
                i, p = ps()
                tok = mm([(p[:, n * 512:(n + 1) * 512], a[:, t * P:(t + 1) * P], b[:, n * 512:(n + 1) * 512], a is not sgb, a is sgb)
                          for n in range(2) for sgb in (sg[0:32, 1, :],) for a, b in ((sg[:, 0, :], g2a), (sgb, g2b))],
                         e, *pfree[i])
                pfree[i] = [cp(A, gt[:, t, :], p, tok)]
            c2.free = M.last()
            tg2 = M.last()
            for half in range(2):
                c = load_cols(T["rw_w_rkv_2"][0, 2], 512 * half, 512)
                i, p = ps()
                o3 = p.rearrange("p (t n) -> p t n", t=NT)
                tok = proj_tok(xc_, c.v, KT, [o3[:, t, :] for t in range(NT)], slice(0, 512), c.tok, xv, *pfree[i])
                c.free = M.last()
                pfree[i] = [cp(A, vt[:, :, 512 * half:512 * half + 512], o3, tok)]
            spare_k = [order.pop(0) for _ in range(3)]
            spare = [ring[k] for k in spare_k]
            for k in spare_k[0:2]:
                zero = ms(G, ring[k], 0.0, lambda old=rwait[k]: old.free)
            ts(V, om, vec[:, VO["ka"]:VO["ka"] + 8], -1.0, 1.0, MUL, ADD)
            for k in range(KT):
                ts(V, xb_[:, k, :], aT[:, k, :], vcol("ka", k), om[:, k:k + 1], MUL, ADD, t_, tg)
            tt(V, flat(kT), flat(xb_), flat(kT), MUL)
            for k in range(KT):
                stt(xa_[:, k, :], rT[:, k, :], vcol("rk", k), kT[:, k, :], MUL, MUL, tr_e)
            i, p = ps()
            tok = mm([(p[:, t * 512 + 2 * k:t * 512 + 2 * k + 2], xa_[:, k, t * P:(t + 1) * P], tab["hnd"], True, True)
                      for t in range(NT) for k in range(KT)], V.last(), *pfree[i])
            for k in range(KT):
                V.add(lambda e, k=k: e.tensor_tensor_scan(Lc[:, k, :], tab["rst"], lw[:, k, :], 0.0, MUL, ADD), [tsum])
            dec = -math.exp(-0.5)
            t1 = tt(V, flat(lw), flat(Lc), flat(lw), SUB)
            pfree[i] = [cp(V, bon, two(p, 16), tok)]
            e1 = act(flat(xx), flat(Lc), ACT.Exp, t1, tg2, scale=dec)
            e3 = act(flat(xb_), flat(Lc), ACT.Exp, scale=-dec)
            e2 = act(flat(lw), flat(lw), ACT.Exp, scale=dec)
            tt(V, flat(aT), flat(aT), flat(kk), MUL)
            tt(V, flat(rT), flat(rT), flat(xx), MUL, e1)
            cp(V, pc, xx.rearrange("p k (c s) -> p k c s", c=4)[:, :, :, 63])
            tt(V, flat(kT), flat(kT), flat(xb_), MUL, e3)
            tt(V, flat(aT), flat(aT), flat(xb_), MUL)
            stt(flat(kk), flat(kk), -1.0, flat(lw), MUL, MUL, e2)
            barrier()
            bT, aa = aT, kk
            apos[0] = mark

            def u3(a):
                return a.rearrange("p (u n) -> p u n", n=64)

            def half_of(a, c):
                return a.rearrange("p (u c n) -> p c u n", c=2, n=64)[64 * c:64 * c + 64, c]

            def rows_of(a, c):
                return u3(a)[64 * c:64 * c + 64]

            hbf = hb.rearrange("p t d -> p (t d)")
            own = carve(5120)
            lf, hf, mf = flat(Lc), flat(hT), flat(mT)
            ones = [own[:, 1024 * m:1024 * m + 1024] for m in range(5)]
            ones.append(lnr[0][:, 0, :])
            stb = carve(1024)
            B = []
            for t in range(NT):
                d = {"nd": (hbf if t else spare[2][:, 0:2048]), "P": (hf if t else spare[2][:, 2048:4096]), "Q": (mf if t else lf)}
                for two_, names in (("nd", "ND"), ("P", "nY"), ("Q", "dX")):
                    for m in range(2):
                        d[names[m]] = d[two_][:, 1024 * m:1024 * m + 1024]
                for k in ("rb", "rk", "ak"):
                    d[k] = ones.pop(0)
                B.append(d)
            bd = [spare[m // 2][:, 2048 * (m % 2):2048 * (m % 2) + 2048] for m in range(4)]
            ms(V, st.rearrange("p k n -> p (k n)"), 0.0)
            ms(V, stb, 0.0)

            def mask(k, parts=slice(0, P)):
                return bc(tab[k][parts].unsqueeze(1), [parts.stop - parts.start, 16, 64])

            def spread(q, dst, src, t, *w):
                d5 = dst.rearrange("p (k c a n) -> p a k c n", k=KT, c=2, a=2)
                for hh in range(2):
                    h = slice(64 * hh, 64 * hh + 64)
                    tok = cp(q, d5[h, hh], src[h, :, t * P:(t + 1) * P].rearrange("p k (c n) -> p k c n", c=2), *w)
                return tok

            def pair(dst, lhs, rhs, t, m, *w):
                i, p = ps()
                r4 = rhs.rearrange("p (k c n) -> p k c n", k=KT, c=2)
                tok = mm([(p[64 * c:64 * c + 64, k * P:(k + 1) * P], lhs[:, k, t * P + 64 * c:t * P + 64 * c + 64],
                           r4[:, k, c, :], True, True) for k in range(KT) for c in range(2)], *w, *pfree[i])
                pfree[i] = [tt(V, u3(dst), u3(p), mask(m), MUL, tok)]
                return tok

            free = [zero] * 4
            place = (dict(a=0, b=2, r=1), dict(a=3, b=0, r=2))
            for t in range(NT):
                d, pl = B[t], place[t]
                ta = spread(A, bd[pl["a"]], aa, t, free[pl["a"]])
                tb = spread(A, bd[pl["b"]], bT, t, free[pl["b"]])
                t_r = spread(V, bd[pl["r"]], rT, t, free[pl["r"]])
                pair(d["N"], bT, bd[pl["a"]], t, "mlt", ta)
                free[pl["a"]] = pair(d["ak"], kT, bd[pl["a"]], t, "mlt")
                free[pl["b"]] = pair(d["D"], aa, bd[pl["b"]], t, "mgt", tb)
                pair(d["rb"], bT, bd[pl["r"]], t, "mle", t_r)
                free[pl["r"]] = pair(d["rk"], kT, bd[pl["r"]], t, "mle")
            for t in range(NT):
                d = B[t]
                d["nb"], d["db"] = (bd[1], bd[3]) if t == 0 else (bd[0], bd[2])
                fr = (free[1], free[3]) if t == 0 else (free[0], free[2])
                for src, dst, one, m, big_, f in ((d["N"], d["n"], d["Y"], "m16", d["nb"], fr[0]),
                                                  (d["D"], d["d"], d["X"], "n16", d["db"], fr[1])):
                    tok = tt(V, u3(dst), u3(src), mask(m), MUL)
                    for c in range(2):
                        tok2 = cp(A, half_of(big_, c), rows_of(dst, c), tok, f)
                    tt(V, u3(one), u3(dst), mask("i64"), ADD)
                d["bd"] = tok2
                d["st"] = V.last()

            def prod(lhs, rhs, g, *w):
                i, p = ps()
                r4 = rhs.rearrange("p (m u n) -> p u m n", m=2, n=64)
                o4 = p.rearrange("p (u m n) -> p u m n", m=2, n=64)
                tok = mm([(o4[:, u - 8 * g], lhs[:, u * P:(u + 1) * P], r4[:, u], True, True)
                          for u in range(8 * g, 8 * g + 8)], *w, *pfree[i])
                return i, p.rearrange("p (u m n) -> p m u n", m=2, n=64), tok

            for step in range(4):
                for t in range(NT):
                    d = B[t]
                    w = [d["bd"], d["st"]]
                    for g in range(2):
                        us = slice(8 * g, 8 * g + 8)
                        got = [prod(d["db"], d["P"], g, *w), prod(d["nb"], d["Q"], g)]
                        both = got[1][2]
                        for (i, p, tok), pw, inv, big_ in zip(got, "nd", "YX", ("nb", "db")):
                            if step < 3:
                                tn = cp(V, u3(d[pw])[:, us], p[:, 0], tok)
                            if step:
                                tn_ = tt(V, u3(d[inv])[:, us], u3(d[inv])[:, us], p[:, 1], ADD, tok)
                            d["st"] = V.last()
                            pfree[i] = [V.last()]
                            if step < 3:
                                for c in range(2):
                                    d["bd"] = cp(A, half_of(d[big_], c)[:, us], rows_of(d[pw], c)[:, us], tn, both)
                            else:
                                d["bd"] = both
            for mn, md in (("m32", "n32"), (None, "n64")):
                for t in range(NT):
                    d = B[t]
                    for c in range(2):
                        h = slice(64 * c, 64 * c + 64)
                        tt(V, half_of(d["db"], c), rows_of(d["D"], c), mask(md, h), MUL, d["bd"])
                        if mn:
                            tt(V, half_of(d["nb"], c), rows_of(d["N"], c), mask(mn, h), MUL)
                    d["m"] = V.last()
                for t in range(NT):
                    d = B[t]
                    w = [d["m"], d["st"]]
                    for g in range(2):
                        us = slice(8 * g, 8 * g + 8)
                        i, p, tok = prod(d["db"], d["P"], g, *w)
                        pfree[i] = [cp(V, u3(d["n"])[:, us], p[:, 1], tok)]
                        for c in range(2):
                            d["b"] = cp(A, half_of(d["db"], c)[:, us], rows_of(d["X"], c)[:, us], tok)
                        if mn:
                            i, p, tok = prod(d["nb"], d["Q"], g)
                            pfree[i] = [cp(V, u3(d["d"])[:, us], p[:, 1], tok)]
                            for c in range(2):
                                d["b"] = cp(A, half_of(d["nb"], c)[:, us], rows_of(d["Y"], c)[:, us], tok)
                        d["c"] = V.last()
                for t in range(NT):
                    d = B[t]
                    got = []
                    for g in range(2):
                        us = slice(8 * g, 8 * g + 8)
                        got = [("Y",) + prod(d["db"], d["P"], g, d["b"], d["c"])]
                        if mn:
                            got.append(("X",) + prod(d["nb"], d["Q"], g))
                        for inv, i, p, tok in got:
                            pfree[i] = [tt(V, u3(d[inv])[:, us], u3(d[inv])[:, us], p[:, 0], ADD, tok)]
                    d["st"], d["bd"] = V.last(), M.last()
            for t in range(NT):
                d = B[t]
                d["mv"], d["U"], d["btok"], d["ktok"] = d["n"], d["X"], d["d"], bd[t][:, 0:1024]
                for src, dst in ((bT, d["btok"]), (kT, d["ktok"])):
                    i, p = ps()
                    tok = tr([(p[:, k * P:(k + 1) * P], src[:, k, t * P:(t + 1) * P], idn) for k in range(KT)],
                             V.last(), A.last(), *pfree[i])
                    pfree[i] = [cp(A, dst, p, tok)]

            def blk_(a, c, u):
                return a[64 * c:64 * c + 64, u * 64:(u + 1) * 64]

            for t in range(NT):
                d = B[t]
                i, p = ps()
                tok = mm([(blk_(p, c, u), blk_(d["ak"], c, u), blk_(vt[:, t, :], c, u), True, True)
                          for u in range(16) for c in range(2)], V.last(), *pfree[i])
                pfree[i] = [cp(V, d["mv"], p, tok)]
            lnfree[0] = V.last()
            barrier()
            s3 = stb.rearrange("p (k a n) -> p k a n", k=KT, a=2)
            r, rtok = rows_in(4)

            def norm_ops(t):
                y = hb[:, t, :]
                h16 = y.rearrange("p (h n) -> p h n", h=16)
                sq = B[0]["ak"]
                s16 = sq.rearrange("p (h n) -> p h n", h=16)
                mu, va = carve(16), carve(16)

                def wide(a):
                    return bc(a.unsqueeze(2), [P, 16, 64])

                def last():
                    lnfree[0] = tt(V, y, y, r[:, 1, :], ADD)

                return [lambda: red(mu, h16, ADD), lambda: ts(V, mu, mu, 1.0 / 64, None, MUL, None),
                        lambda: tt(V, h16, h16, wide(mu), SUB), lambda: tt(V, sq, y, y, MUL), lambda: red(va, s16, ADD),
                        lambda: rms_scale(va, 64, 64e-5), lambda: tt(V, h16, h16, wide(va), MUL),
                        lambda: tt(V, y, y, r[:, 0, :], MUL, rtok), last,
                        lambda: tt(V, s16, vt[:, t, :].rearrange("p (h n) -> p h n", h=16), wide(bon[:, t, :]), MUL),
                        lambda: tt(V, y, y, sq, ADD), lambda: tt(V, y, y, gt[:, t, :], MUL)]

            norms = [norm_ops(t) for t in range(NT)]

            def some(t, n):
                for _ in range(n if t else 0):
                    if norms[0]:
                        norms[0].pop(0)()

            v_s = a_s = None
            for t in range(NT):
                d, v_, y = B[t], vt[:, t, :], hb[:, t, :]
                mv, U = d["mv"], d["U"]
                for c in range(2):
                    rows = slice(64 * c, 64 * c + 64)
                    tk = slice(t * P + 64 * c, t * P + 64 * c + 64)
                    i, p = ps()
                    tok = mm([(p[rows, k * P:(k + 1) * P], aa[:, k, tk], stb[:, k * P:(k + 1) * P], True, True)
                              for k in range(KT)], v_s, a_s, *pfree[i])
                    i2, p2 = ps()
                    tok2 = mm([(p2[rows, k * P:(k + 1) * P], rT[:, k, tk], stb[:, k * P:(k + 1) * P], True, True)
                               for k in range(KT)], *pfree[i2])
                    pfree[i] = [tt(V, mv[rows], mv[rows], p[rows], ADD, tok)]
                    v_mv = V.last()
                    pfree[i2] = [cp(A, y[rows], p2[rows], tok2)]
                    a_y = A.last()
                    some(t, 1)
                    i, p = ps()
                    tok = mm([(blk_(p, c, u), blk_(d["Y"], c, u), blk_(mv, c, u), True, True) for u in range(16)],
                             v_mv, *pfree[i])
                    pfree[i] = [cp(V, U[rows], p[rows], tok)]
                    v_u = V.last()
                    some(t, 3)
                    i2, p2 = ps()
                    lst2 = []
                    for u in range(16):
                        k, hh = u // 2, u % 2
                        o = p2[64 * hh:64 * hh + 64, k * 64:(k + 1) * 64]
                        lst2.append((o, blk_(d["btok"], c, u), blk_(U, c, u), True, False))
                        lst2.append((o, blk_(d["ktok"], c, u), blk_(v_, c, u), False, True))
                    tok2 = mm(lst2, v_u, *pfree[i2])
                    s2 = st.rearrange("p k n -> p (k n)")
                    tt(V, s2, s2, p2[:, 0:512], ADD, tok2)
                    pfree[i2] = [V.last()]
                    e = tt(V, st, st, bc(pc[:, :, 2 * t + c:2 * t + c + 1], [P, 8, 64]), MUL)
                    cp(A, s3[64:128, :, 1], st[64:128], e)
                    v_s = cp(V, s3[0:64, :, 0], st[0:64])
                    a_s = A.last()
                    some(t, 2)
                    i, p = ps()
                    lst = []
                    for u in range(16):
                        lst.append((blk_(p, c, u), blk_(d["rb"], c, u), blk_(U, c, u), True, False))
                        lst.append((blk_(p, c, u), blk_(d["rk"], c, u), blk_(v_, c, u), False, True))
                    tok = mm(lst, *pfree[i])
                    pfree[i] = [tt(V, y[rows], y[rows], p[rows], ADD, tok, a_y)]
                for k in spare_k[:2] if t else spare_k[2:]:
                    rwait[k] = [V.last(), A.last(), M.last()]
                    order.append(k)
            dmp("wkv", hb)
            def part(t):
                def go():
                    for f in norms[t]:
                        f()
                    return tile_T(t, hb, kT, V.last())
                return go

            out_proj(T["rw_w_o_2"][0], kT, 3, [(t, part(t)) for t in range(NT)])

        s_o = sem("s_o")
        if stop is None or stop[0] != "l":
            final_norm()
            dmp("x1", x)
            if stop != "fn":
                diff_attention()
                dmp("xa", x)
                if stop != "da":
                    if stop != "rw":
                        moe(0, 2)
                        dmp("xm0", x)
                    if stop != "m0":
                        rwkv()
                        dmp("xr", x)
                        if stop != "rw":
                            moe(1, 5)
        A.dma(out.rearrange("b (t p) d -> p (b t) d", p=P), x, s_o, [V.last()])
        A.items.append((lambda e: None, [(s_o, 16)], None, 0))
        for d in dumps:
            A.items.append((lambda e: None, [d], None, 0))

        block = ctx.enter_context(nc.Block())

        @block.sync
        def _(eng):
            W.emit(eng)

        @block.gpsimd
        def _(eng):
            G.emit(eng)

        @block.scalar
        def _(eng):
            A.emit(eng)

        @block.tensor
        def _(eng):
            M.emit(eng)

        @block.vector
        def _(eng):
            V.emit(eng)


_VECS = (("norm_g", 16), ("qn", 4), ("kvn", 2), ("nb1", 4), ("nb2", 2), ("bm", 64), ("mu", 48), ("w0", 8), ("a0", 8),
         ("kk", 8), ("ka", 8), ("rk", 8))
_ROWS = (("subln", 128), ("lam", 256), ("mb", 72), ("nb2v", 128))


def vec_layout():
    o, out = 0, {}
    for n, w in _VECS:
        out[n] = o
        o += w
    return out


def row_layout():
    o, out = 0, {}
    for n, w in _ROWS:
        out[n] = o
        o += w
    return out


def layout(i):
    def colmaj(a):
        return np.ascontiguousarray(a.reshape(-1, P).T)

    tabs = tables()
    qn = np.zeros((L1, 256), np.float32)
    qn[:, :192] = i["mla_q_norm"]
    v = {
        "norm_g": colmaj(i["norm_g"]), "qn": colmaj(qn), "kvn": colmaj(i["mla_kv_norm"]), "nb1": colmaj(i["nsa_b1"]),
        "nb2": colmaj(np.concatenate([i["nsa_b2"][:, 0], i["nsa_b2"][:, 0]], axis=1)), "bm": colmaj(i["b_merge"]),
        "mu": colmaj(i["rw_mu_2"]), "w0": colmaj(i["rw_w0_2"]), "a0": colmaj(i["rw_a0_2"]), "kk": colmaj(i["rw_k_k_2"]),
        "ka": colmaj(i["rw_k_a_2"]), "rk": colmaj(i["rw_r_k_2"]),
    }
    r = {
        "subln": i["attn_subln_g_2"].reshape(-1), "lam": i["attn_lambda_2"].reshape(-1),
        "mb": np.concatenate([i["moe_rg_b_2"], i["moe_re_b_2"]], axis=1).reshape(-1), "nb2v": i["nsa_b2"][:, 1].reshape(-1),
    }
    vecs = np.concatenate([v[n] for n, _ in _VECS], axis=1)
    rows = np.tile(np.concatenate([r[n] for n, _ in _ROWS])[None], (P, 1))
    pairs = [(i["final_norm_g"], i["final_norm_g"])]
    pairs += [(i["ln1_g_2"][0], i["ln1_b_2"][0]), (i["ln2_g_2"][0], i["ln2_b_2"][0]), (i["ln1_g_2"][1], i["ln1_b_2"][1]),
              (i["rw_lnx_g_2"][0], i["rw_lnx_b_2"][0]), (i["ln2_g_2"][1], i["ln2_b_2"][1])]
    lrows = np.stack([np.tile(np.stack(p)[None], (P, 1, 1)) for p in pairs])
    common = [k for k in tabs if k not in FIRST_TABLES and k[0:2] != "cz"]
    arrays = {
        "x": i["x"], "vecs": vecs, "rows": rows, "lrows": lrows,
        "tcom": np.concatenate([tabs[k] for k in common], axis=1),
        "tfirst": np.concatenate([tabs[k] for k in FIRST_TABLES], axis=1),
        "cz0": tabs["cz0"], "cz1": tabs["cz1"],
        "pos": i["nsa_pos"].transpose(0, 1, 3, 2).reshape(L1, P, 32),
        "wr": np.concatenate([i["moe_rg_w_2"], i["moe_re_w_2"]], axis=2),
        "lora1": np.concatenate([i["rw_w1_2"][0], i["rw_a1_2"][0], i["rw_g1_2"][0]], axis=1),
        "lora2": np.concatenate([i["rw_w2_2"][0], i["rw_a2_2"][0]], axis=0),
    }
    for n in ("w_in", "mla_w_uq", "mla_w_ukv", "nsa_w1", "nsa_w2", "w_branch", "w_merge", "w_out", "attn_w_qkv_2",
              "attn_w_o_2", "rw_w_rkv_2", "rw_w_o_2", "rw_g2_2", "moe_w_gu_2", "moe_w_down_2"):
        arrays[n] = i[n]
    return {k: np.ascontiguousarray(a) for k, a in arrays.items()}


def kernel(**inputs):
    import concourse.bacc as bacc
    from concourse.bass_utils import run_bass_kernel_spmd

    arrays = layout({k: np.asarray(a) for k, a in inputs.items()})
    nc = bacc.Bacc("TRN2", target_bir_lowering=False, num_devices=1)
    T = {k: nc.dram_tensor(f"in_{k}", a.shape, mybir.dt.from_np(a.dtype), kind="ExternalInput").ap() for k, a in arrays.items()}
    out = nc.dram_tensor("out", (1, S, D), F, kind="ExternalOutput").ap()
    program(nc, T, out)
    r = run_bass_kernel_spmd(nc, [{f"in_{k}": a for k, a in arrays.items()}], core_ids=[0])
    return r.results[0]["out"]
```

```python
import math
from contextlib import ExitStack

import numpy as np
import concourse.bass as bass
from concourse import mybir

F = mybir.dt.float32
ALU = mybir.AluOpType
ACT = mybir.ActivationFunctionType
AX = mybir.AxisListType.X
ADD, SUB, MUL, MAX, MIN = ALU.add, ALU.subtract, ALU.mult, ALU.max, ALU.min

P = 128
S = 256
D = 1024
NT = 2
KT = 8
L1 = 2
RING = 4
MORE = 4
CAP = 64
SLOT = 4096
NEG = -1e30
E = 32
ALPHA = 4.0 ** 0.25
HORD = (0, 2, 1, 3)


def tables():
    s = 2.0 ** -(np.arange(8) + 1.0)
    sl_a, sl_c = s[0::2], s[1::2]
    t = np.arange(S)
    dist = t[:, None] - t[None, :]
    cnt = np.zeros((S, S))
    for win, dil in ((128, 1), (512, 4), (2048, 16)):
        cnt += (dist >= 0) & (dist % dil == 0) & (dist <= win)
    lc = np.where(cnt > 0, np.log(np.maximum(cnt, 1)), NEG)
    causal = np.where(dist >= 0, 0.0, NEG)
    out = {}

    def per_tile(name, full):
        for tt in range(NT):
            w = P * (tt + 1)
            out[f"{name}{tt}"] = full[:, tt * P:(tt + 1) * P, :w].transpose(1, 0, 2).reshape(P, 4 * w)

    per_tile("ba", np.stack([np.where(cnt > 0, lc - sl_a[h] * dist, NEG) for h in HORD]))
    per_tile("bc", np.stack([np.where(dist >= 0, -sl_c[h] * dist, NEG) for h in HORD]))
    per_tile("cz", np.stack([causal] * 4))
    dc = t[:, None] - (np.arange(15) * 16 + 31)[None, :]
    cmp_b = np.full((NT, P, 4, 32), NEG)
    for u, h in enumerate(HORD):
        b = np.where(dc >= 0, -sl_c[h] * dc, NEG)
        cmp_b[:, :, u, :15] = b.reshape(NT, P, 15)
    for tt in range(NT):
        out[f"cm{tt}"] = cmp_b[tt].reshape(P, 128)
    strict = (t[:, None] < t[None, :]).astype(np.float64)
    out["st0"] = strict[:P, :]
    out["st1"] = strict[P:, P:]
    inv = 10000.0 ** (-np.arange(16) / 16.0)
    ang = (t[:, None] * inv[None, :]).reshape(NT, P, 16)
    for name, f in (("cos", np.cos), ("sin", np.sin)):
        v = f(ang).transpose(1, 0, 2)
        v = np.repeat(v[:, :, None, :], 4, axis=2).reshape(P, 8, 16)
        out[name] = np.concatenate([v, v], axis=1).reshape(P, 256)
    out["idn"] = np.eye(P)
    i = np.arange(P)
    out["upp"] = (i[:, None] > i[None, :]).astype(float)
    out["one"] = np.ones((P, P))
    out["hnd32"] = (i[:, None] // 64 == np.arange(32)[None, :]).astype(float)
    out["dnh"] = (i[:, None] % 32 == i[None, :] // 64).astype(float)
    out["hnd"] = (i[:, None] // 64 == np.arange(2)[None, :]).astype(float)
    a, b = i[:, None] % 64, np.arange(64)[None, :]
    out["mlt"] = (a < b).astype(float)
    out["mle"] = (a <= b).astype(float)
    out["m16"] = ((a < b) & (a // 16 == b // 16)).astype(float)
    out["n16"] = ((a > b) & (a // 16 == b // 16)).astype(float)
    out["m32"] = ((a < b) & (a // 16 != b // 16) & (a // 32 == b // 32)).astype(float)
    out["n32"] = ((a > b) & (a // 16 != b // 16) & (a // 32 == b // 32)).astype(float)
    out["m64"] = ((a < b) & (a // 32 != b // 32)).astype(float)
    out["n64"] = ((a > b) & (a // 32 != b // 32)).astype(float)
    out["mgt"] = (a > b).astype(float)
    out["i64"] = (a == b).astype(float)
    out["iog"] = np.tile(np.arange(4.0), (P, 1))
    out["ios"] = np.tile(np.arange(64.0), (P, 1))
    out["ioe"] = np.tile(np.arange(32.0), (P, 1))
    out["rst"] = np.tile((np.arange(S) % 64 != 0).astype(float), (P, 1))
    return {k: np.ascontiguousarray(v, np.float32) for k, v in out.items()}


FIRST_TABLES = ("ba0", "ba1", "bc0", "bc1", "cm0", "cm1", "st0", "cos", "sin", "upp")


class Queue:

    def __init__(self, name, sem, chained):
        self.name, self.sem, self.chained = name, sem, chained
        self.items, self.n, self.first, self.ways = [], 0, [], []

    def add(self, fn, waits=(), inc=1, chain=None):
        waits = list(waits) + self.first
        self.first = []
        if (self.chained if chain is None else chain) and self.n:
            waits.append((self.sem, self.n))
        self.items.append((fn, waits, self.sem if inc else None, 1))
        self.n += 1 if inc else 0
        return (self.sem, self.n)

    def dma(self, out, in_, sem, waits=()):
        self.items.append((lambda e: e.dma_start(out, in_), list(waits) + self.first, sem, 16))
        self.first = []

    def last(self):
        return (self.sem, self.n)

    def ago(self, k):
        return (self.sem, self.n - k)

    def wait_for(self, eng, waits, seen):
        for w in waits:
            w = w() if callable(w) else w
            if w is None:
                continue
            s, v = w
            if v > seen.get(id(s), 0) and not (s is self.sem and not self.chained):
                eng.wait_ge(s, v)
                seen[id(s)] = v

    def split(self, flag, waits):
        self.ways.append({"outer": self.items, "n0": self.n, "flag": (flag, list(waits) + self.first)})
        self.items, self.first = [], []

    def other(self):
        f = self.ways[-1]
        f["yes"], f["n1"] = self.items, self.n
        self.items, self.n = [], f["n0"]

    def join(self):
        f = self.ways.pop()
        assert self.n == f["n1"], (self.name, self.n - f["n0"], f["n1"] - f["n0"])
        f["outer"].append((f["flag"][0], f["flag"][1], (f["yes"], self.items), None))
        self.items = f["outer"]

    def emit(self, eng, items=None, seen=None):
        seen = {} if seen is None else seen
        for fn, waits, sem, by in self.items if items is None else items:
            self.wait_for(eng, waits, seen)
            if by is None:
                flag = eng.value_load(fn, min_val=0, max_val=1)
                a, b = dict(seen), dict(seen)
                with eng.If(flag != 0):
                    self.emit(eng, sem[0], a)
                with eng.Else():
                    self.emit(eng, sem[1], b)
                seen.update({k: min(a[k], b[k]) for k in a if k in b})
                continue
            ins = fn(eng)
            if sem is not None:
                ins.then_inc(sem, by)


class Chunk:

    def __init__(self, ap, tok):
        self.ap, self.tok, self.free = ap, tok, None


def program(nc, T, out, stop=None, dump=None):
    tabs = tables()
    with ExitStack() as ctx:
        def sb(name, w, parts=P):
            return ctx.enter_context(nc.sbuf_tensor(name, [parts, w], F))[:, :]

        def sem(name):
            return ctx.enter_context(nc.semaphore(name))

        V = Queue("vector", sem("sv"), True)
        A = Queue("scalar", sem("sa"), True)
        G = Queue("gpsimd", sem("sg"), True)
        M = Queue("tensor", sem("sm"), False)
        W = Queue("sync", sem("sw"), False)
        queues = (V, A, G, M, W)

        psum = [ctx.enter_context(nc.psum_tensor(f"ps{i}", [P, 1024], F))[:, :] for i in range(4)]
        pfree = [[] for _ in range(4)]
        pnext = [0]

        held = set()

        def ps():
            while pnext[0] % 4 in held:
                pnext[0] += 1
            i = pnext[0] % 4
            pnext[0] += 1
            return i, psum[i]

        def tt(q, o, a, b, op, *w, **k):
            return q.add(lambda e: e.tensor_tensor(o, a, b, op), w, **k)

        def ts(q, o, a, s1, s2, op0, op1, *w, **k):
            if op1 is None:
                return q.add(lambda e: e.tensor_scalar(o, a, s1, None, op0), w, **k)
            return q.add(lambda e: e.tensor_scalar(o, a, s1, s2, op0, op1), w, **k)

        def stt(o, a, s, b, op0, op1, *w, **k):
            return V.add(lambda e: e.scalar_tensor_tensor(out=o, in0=a, scalar=s, in1=b, op0=op0, op1=op1), w, **k)

        def red(o, a, op, *w, **k):
            return V.add(lambda e: e.tensor_reduce(o, a, AX, op), w, **k)

        def rec(o, a, *w, **k):
            return V.add(lambda e: e.reciprocal(o, a), w, **k)

        def cp(q, o, a, *w, **k):
            if q is A:
                return q.add(lambda e: e.activation(o, a, ACT.Copy), w, **k)
            return q.add(lambda e: e.tensor_copy(o, a), w, **k)

        def act(o, a, f, *w, bias=None, scale=1.0, acc=None, **k):
            kw = {"scale": scale}
            if bias is not None:
                kw["bias"] = bias
            if acc is not None:
                kw["accum_out"] = acc
            return A.add(lambda e: e.activation(o, a, f, **kw), w, **k)

        def ms(q, o, v, *w):
            return q.add(lambda e: e.memset(o, v), w)

        def mm(lst, *w):
            tok = None
            for n, (o, l, r, s0, s1) in enumerate(lst):
                end = n == len(lst) - 1
                tok = M.add(lambda e, o=o, l=l, r=r, s0=s0, s1=s1:
                            e.matmul(o, l, r, start=s0, stop=s1, skip_group_check=True),
                            w if n == 0 else (), inc=1 if end else 0)
            return tok

        def tr(lst, *w):
            tok = None
            for n, (o, i, idt) in enumerate(lst):
                end = n == len(lst) - 1
                tok = M.add(lambda e, o=o, i=i, idt=idt: e.transpose(o, i, idt), w if n == 0 else (),
                            inc=1 if end else 0)
            return tok

        def barrier():
            toks = [q.last() for q in queues if q.n and q is not W]
            for q in (V, A, G, M):
                q.first += [t for t in toks if t[0] is not q.sem]

        def bc(ap, shape):
            return ap.to_broadcast(shape)

        ring = [sb(f"ring{i}", SLOT) for i in range(RING)]
        rsem = [sem(f"sr{i}") for i in range(RING + MORE)]
        rcount = [0] * (RING + MORE)
        rwait = [None] * (RING + MORE)
        order = list(range(RING))

        def lend(aps, waits):
            for m, ap in enumerate(aps):
                ring.append(ap)
                rwait[RING + m] = list(waits)
                order.append(RING + m)

        def give_back():
            del ring[RING:]
            order[:] = [k for k in order if k < RING]

        def load(*parts):
            k = order.pop(0)
            order.append(k)
            old = rwait[k]
            for j, (dst, src) in enumerate(parts):
                waits = []
                if j == 0 and old is not None:
                    waits = old if isinstance(old, list) else [lambda: old.free]
                W.dma(dst(ring[k]), src, rsem[k], waits)
                rcount[k] += 16
            rwait[k] = c = Chunk(ring[k], (rsem[k], rcount[k]))
            if sum(rcount) == 2 * 16:
                for dst, src, s_ in later:
                    W.dma(dst, src, s_)
            return c

        def cols(w, kt=KT):
            return lambda s: s[:, 0:kt * w].rearrange("p (k n) -> p k n", k=kt)

        def wsrc(ap, c0, w):
            return ap.rearrange("(k p) n -> p k n", p=P)[:, :, c0:c0 + w]

        def load_cols(ap, c0, w):
            c = load((cols(w, ap.shape[0] // P), wsrc(ap, c0, w)))
            c.v = c.ap[:, 0:ap.shape[0] // P * w].rearrange("p (k n) -> p k n", n=w)
            return c

        x = sb("x", 2 * D).rearrange("p (t d) -> p t d", t=NT)
        hb = sb("hb", 2 * D).rearrange("p (t d) -> p t d", t=NT)
        hT = sb("hT", 2 * D).rearrange("p (k s) -> p k s", k=KT)
        mT = sb("mT", 2 * D).rearrange("p (k s) -> p k s", k=KT)
        small = sb("small", 256)
        arena = sb("arena", 21900)
        apos = [0]

        def carve(w):
            a = arena[:, apos[0]:apos[0] + w]
            apos[0] += w
            assert apos[0] <= 21900, apos[0]
            return a

        s_c, s_f = sem("s_c"), sem("s_f")
        nload = {id(s_c): 0, id(s_f): 0}

        later = []

        def start_load(dst, src, s=s_f):
            if s is s_c:
                A.dma(dst, src, s)
            else:
                later.append((dst, src, s))
            nload[id(s)] += 16

        tab = {}
        common = [k for k in tabs if k not in FIRST_TABLES and k[0:2] != "cz"]
        wc = sum(tabs[k].shape[1] for k in common)
        tcom = sb("tcom", wc)
        o = 0
        for k in common:
            tab[k] = tcom[:, o:o + tabs[k].shape[1]]
            o += tabs[k].shape[1]
        for tt_ in range(NT):
            tab[f"cz{tt_}"] = sb(f"cz{tt_}", tabs[f"cz{tt_}"].shape[1])
        vec = sb("vec", T["vecs"].shape[1])
        row = sb("row", T["rows"].shape[1])
        rw36 = sb("rw36", 2 * KT * 36).rearrange("p (l k n) -> p l k n", l=2, k=KT)
        lnr = [sb(f"lnr{i}", 2 * D).rearrange("p (a d) -> p a d", a=2) for i in range(1)]
        s_ln = [sem(f"s_ln{i}") for i in range(1)]
        nln = [0]
        lnfree = [None]

        def rows_in(i):
            w = [lnfree[0]] if lnfree[0] else []
            G.dma(lnr[0], T["lrows"][i], s_ln[0], w)
            nln[0] += 16
            return lnr[0], (s_ln[0], nln[0])

        s_x = sem("s_x")
        A.dma(x, T["x"].rearrange("b (t p) d -> p (b t) d", p=P), s_x)
        start_load(tcom, T["tcom"], s_c)
        start_load(vec, T["vecs"], s_c)
        start_load(row, T["rows"])
        for k in FIRST_TABLES:
            tab[k] = carve(tabs[k].shape[1])
        wf = apos[0]
        start_load(arena[:, 0:wf], T["tfirst"])
        for tt_ in range(NT):
            start_load(tab[f"cz{tt_}"], T[f"cz{tt_}"])
        for l in range(2):
            start_load(rw36[:, l], T["wr"][l].rearrange("(k p) n -> p k n", p=P))
        w_uq = [carve(2 * 384).rearrange("p (k n) -> p k n", k=2) for _ in range(L1)]
        w_ukv = [carve(512) for _ in range(L1)]
        w2n = [carve(128).rearrange("p (a n) -> p a n", a=2) for _ in range(L1)]
        posT = [carve(32) for _ in range(L1)]
        for l in range(L1):
            start_load(w_uq[l][:, 0], T["mla_w_uq"][l, 0:P])
            start_load(w_uq[l][0:64, 1], T["mla_w_uq"][l, P:192])
            start_load(w_ukv[l], T["mla_w_ukv"][l])
            start_load(w2n[l], T["nsa_w2"][l].rearrange("a p n -> p a n"))
            start_load(posT[l], T["pos"][l])
        C0, F0 = (s_c, nload[id(s_c)]), (s_f, nload[id(s_f)])
        X0 = (s_x, 16)
        for q in (V, A, G, M):
            q.first += [C0, X0]
        W.first += [C0, X0]
        idn = tab["idn"]

        VO, RO = vec_layout(), row_layout()

        def vcol(name, k=0, parts=slice(0, P)):
            o = VO[name] + k
            return vec[parts, o:o + 1]

        def rrow(name, w, off=0):
            o = RO[name] + off
            return row[:, o:o + w]

        sm_pos = [0]

        def sml(w):
            if sm_pos[0] + w > 256:
                sm_pos[0] = 0
            o = sm_pos[0]
            sm_pos[0] += w
            return small[:, o:o + w]

        def rms_scale(ss, n, eps, *w):
            t = ts(V, ss, ss, 1.0 / n, eps, MUL, ADD, *w)
            t = act(ss, ss, ACT.Sqrt, t)
            return rec(ss, ss, t)

        def to_T(src, dst, *w, scale=None):
            toks = []
            for half in range(2):
                i, p = ps()
                lst = [(p[:, (k % 4) * 256 + t * P:(k % 4) * 256 + t * P + P],
                        src[:, t, k * P:(k + 1) * P], idn) for k in range(4 * half, 4 * half + 4) for t in range(NT)]
                tok = tr(lst, *w, *pfree[i])
                q = V if half else A
                if scale is None:
                    e = cp(q, dst[:, 4 * half:4 * half + 4, :], p.rearrange("p (k s) -> p k s", k=4), tok)
                else:
                    for k in range(4 * half, 4 * half + 4):
                        pk = p[:, (k % 4) * 256:(k % 4) * 256 + 256]
                        if q is V:
                            e = ts(V, dst[:, k, :], pk, scale(k), None, MUL, None, tok)
                        else:
                            e = act(dst[:, k, :], pk, ACT.Copy, tok, scale=scale(k))
                pfree[i] = [e]
                toks.append(e)
            return toks

        def proj_T(lhs, rhs, nk, outs, *w):
            lst = []
            for o, c in outs:
                for k in range(nk):
                    lst.append((o, lhs[:, k, c], rhs[:, k, :], k == 0, k == nk - 1))
            return mm(lst, *w)

        def proj_tok(lhs, rhs, nk, o, c, *w):
            lst = []
            for t in range(NT):
                for k in range(nk):
                    lst.append((o[t], lhs[:, k, t * P:(t + 1) * P], rhs[:, k, c], k == 0, k == nk - 1))
            return mm(lst, *w)

        def silu(dst, src, tmp, *w):
            act(tmp, src, ACT.Sigmoid, *w)
            return tt(V, dst, src, tmp, MUL, A.last())

        def two(p, w):
            return p.rearrange("p (a n) -> p a n", a=2)[:, :, 0:w]

        Sb, Pb, PTb = ([carve(512), carve(1024)] for _ in range(3))
        base_first = apos[0]

        def score_mm(score, *w):
            i, p = ps()
            held.add(i)
            return i, p, mm(score(p), *w, *pfree[i])

        def scores4(t, score, SL, scale, bias, guard, *w):
            i, p, tok = score if isinstance(score, tuple) else score_mm(score, *w)
            s_ = Sb[t][:, 0:4 * SL]
            e = stt(s_.rearrange("p (a n) -> p a n", a=2), two(p, 2 * SL), scale,
                    bias.rearrange("p (a n) -> p a n", a=2), MUL, ADD, tok, A.last())
            pfree[i] = [e]
            held.remove(i)
            mx = sml(4)
            red(mx, s_.rearrange("p (u n) -> p u n", u=4), MAX)
            ts(V, mx, mx, -1.0, 1e29 if guard else None, MUL, MIN if guard else None)
            return mx

        def exps4(t, mx, SL, guard):
            sm = sml(4)
            p4 = Pb[t][:, 0:4 * SL].rearrange("p (u n) -> p u n", u=4)
            e = V.last()
            for u in range(4):
                act(p4[:, u, :], Sb[t][:, u * SL:(u + 1) * SL], ACT.Exp, e, M.last(), bias=mx[:, u:u + 1],
                    acc=sm[:, u:u + 1])
            return p4, sm, A.last()

        def sums4(sm, tok, guard):
            if guard:
                ts(V, sm, sm, 1e-30, None, MAX, None, tok)
            return rec(sm, sm, tok)

        def attn4(score, scale, bias, vals, dst, fill, *w):
            got = {}
            for t in (1, 0):
                mx = scores4(t, score(t), P * (t + 1), scale, bias(t), False, *w)
                got[t] = exps4(t, mx, P * (t + 1), False)
            fill()
            pts = {}
            for t in (1, 0):
                p4, ri, tok = got[t]
                sums4(ri, tok, False)
                i, p = ps()
                tok = tr([(p[:, (u * (t + 1) + s) * P:(u * (t + 1) + s + 1) * P], p4[:, u, s * P:(s + 1) * P], idn)
                          for u in range(4) for s in range(t + 1)], tok, *pfree[i])
                pts[t] = cp(A, PTb[t], p[:, 0:512 * (t + 1)], tok)
                pfree[i] = [pts[t]]
            for t in (1, 0):
                ri, pt = got[t][1], PTb[t]
                i, p = ps()
                lst = []
                for u, h in enumerate(HORD):
                    for s in range(t + 1):
                        lst.append((p[:, u * 64:(u + 1) * 64], pt[:, (u * (t + 1) + s) * P:(u * (t + 1) + s + 1) * P],
                                    vals(h, s), s == 0, s == t))
                tok = mm(lst, pts[t], *pfree[i])
                d4 = dst(t).rearrange("p (j a) n -> p a j n", j=2)
                e = tt(V, d4, p[:, 0:256].rearrange("p (a j n) -> p a j n", a=2, j=2),
                       bc(ri.rearrange("p (a j) -> p a j", a=2).unsqueeze(3), [P, 2, 2, 64]), MUL, tok)
                pfree[i] = [e]
            return e

        def dmp(name, ap):
            if dump is not None and name in dump:
                s_ = sem(f"s_d{name}")
                W.dma(dump[name], ap, s_, [q.last() for q in (V, A, G, M) if q.n])
                dumps.append((s_, 16))
                for q in (V, A, G, M):
                    q.first.append((s_, 16))

        dumps = []

        hready = [[], []]

        def norm_in(l, t, *w):
            ss = sml(1)
            act(hb[:, t, :], x[:, t, :], ACT.Square, *w, acc=ss)
            rms_scale(ss, D, 1e-6, A.last())
            e = ts(V, hb[:, t, :], x[:, t, :], ss, None, MUL, None)
            i, p = ps()
            tok = tr([(p[:, k * P:(k + 1) * P], hb[:, t, k * P:(k + 1) * P], idn) for k in range(KT)], e, *pfree[i])
            for k in range(KT):
                d, g = hT[:, k, t * P:(t + 1) * P], vcol("norm_g", 8 * l + k)
                if k < 4:
                    act(d, p[:, k * P:(k + 1) * P], ACT.Copy, tok, scale=g)
                else:
                    ts(V, d, p[:, k * P:(k + 1) * P], g, None, MUL, None, tok)
            pfree[i] = [A.last(), V.last()]
            hready[l] += pfree[i]

        def first_layer(l):
            apos[0] = base_first
            gate = carve(512).rearrange("p (t n) -> p t n", t=NT)
            y = carve(512).rearrange("p (t n) -> p t n", t=NT)
            sgates = [a.rearrange("p a b -> p (a b)") for a in (mT, hb, lnr[0])]
            yT = [carve(512).rearrange("p (k s) -> p k s", k=2) for _ in range(4)]
            qT = carve(512).rearrange("p (j s) -> p j s", j=2)
            kT = carve(512).rearrange("p (j s) -> p j s", j=2)
            v = carve(512).rearrange("p (t n) -> p t n", t=NT)
            tmp = carve(1024)

            hTok = hready[l]
            win = T["w_in"][l]

            def tok_major(c, w, c0=0):
                i, p = ps()
                o = p.rearrange("p (t n) -> p t n", t=NT)
                tok = proj_tok(hT, c.v, KT, [o[:, t, 0:w] for t in range(NT)], slice(c0, c0 + w),
                               c.tok, *hTok, *pfree[i])
                return i, two(p, w), tok

            def gate_of(i, src, tok, g):
                e = silu(g, src, tmp[:, 0:512].rearrange("p (t n) -> p t n", t=NT), tok, V.last())
                pfree[i] = [e]

            def heads_T(c, c0, dsts):
                i, p = ps()
                tok = proj_T(c.v, hT, KT, [(p[:, n * 256:(n + 1) * 256], slice(c0 + n * P, c0 + (n + 1) * P))
                                           for n in range(2 * len(dsts))], c.tok, *hTok, *pfree[i])
                for n, d in enumerate(dsts):
                    e = cp(A, d, p[:, n * 512:(n + 1) * 512].rearrange("p (j s) -> p j s", j=2), tok, M.last())
                pfree[i] = [e]
                return e

            def score_qk(q, k, t):
                SL = P * (t + 1)

                def go(p):
                    return [(p[:, hh * 512 + j * SL:hh * 512 + (j + 1) * SL],
                             q[64 * hh:64 * hh + 64, j, t * P:(t + 1) * P],
                             k(hh, j)[:, 0:SL], True, True) for j in range(2) for hh in range(2)]
                return go

            def merge_gate(b, half, dst):
                c = load_cols(T["w_merge"][l, b], 512 * half, 512)

                def step(m):
                    i, p = ps()
                    tok = proj_T(c.v, hT, KT, [(p[:, n * 256:(n + 1) * 256], slice((2 * m + n) * P, (2 * m + n + 1) * P))
                                               for n in range(2)], c.tok, *pfree[i])
                    if m:
                        c.free = M.last()
                    for n in range(2):
                        k = 2 * m + n
                        act(dst[:, k * 256:(k + 1) * 256], p[:, n * 256:(n + 1) * 256], ACT.Sigmoid, tok,
                            bias=vcol("bm", 32 * l + 8 * b + 4 * half + k))
                    pfree[i] = [A.last()]
                return step

            gates_left = [(b, half) for b in range(4) for half in range(2)]
            steps = []

            def fill(n=2):
                for _ in range(n):
                    if not steps:
                        b, half = gates_left.pop(0)
                        g = merge_gate(b, half, sgates[b][:, 1024 * half:1024 * half + 1024])
                        steps.extend((lambda: g(0), lambda: g(1)))
                    steps.pop(0)()

            def finish_branch(b, gated=False):
                if not gated:
                    tt(V, y, y, gate, MUL)
                i, p = ps()
                tok = tr([(p[:, k * 256 + t * P:k * 256 + t * P + P], y[:, t, k * P:(k + 1) * P], idn)
                          for k in range(2) for t in range(NT)], V.last(), *pfree[i])
                pfree[i] = [cp(A, yT[b], p[:, 0:512].rearrange("p (k s) -> p k s", k=2), tok)]

            def merge(b):
                cb = load_cols(T["w_branch"][l, b], 0, D)
                for half in range(2):
                    i2, p2 = ps()
                    tok2 = proj_T(cb.v, yT[b], 2, [(p2[:, n * 256:(n + 1) * 256], slice((4 * half + n) * P, (4 * half + n + 1) * P))
                                                   for n in range(4)], cb.tok, A.last(), *pfree[i2])
                    cb.free = M.last()
                    sg = sgates[b][:, 1024 * half:1024 * half + 1024]
                    pfree[i2] = [tt(V, sg, sg, p2, MUL, tok2)]
                    if b:
                        m3 = sgates[0][:, 1024 * half:1024 * half + 1024]
                        lnfree[0] = tt(V, m3, m3, sg, ADD)

            def y4(t):
                return y[:, t, :].rearrange("p (h n) -> p h n", h=4)

            c = load_cols(win, 0, 512)
            qe = heads_T(c, 0, (qT, kT))
            c.free = M.last()
            c = load_cols(win, 512, 512)
            i, pv, tok = tok_major(c, 512)
            c.free = M.last()
            ve = cp(V, v, pv[:, :, 0:256], tok)
            gate_of(i, pv[:, :, 256:512], tok, gate)
            for q in (V, M):
                q.first.append(F0)
            attn4(lambda t: score_qk(qT, lambda hh, j: kT[64 * hh:64 * hh + 64, j], t), 0.125, lambda t: tab[f"ba{t}"],
                  lambda h, s: v[:, s, h * 64:(h + 1) * 64], y4, fill, qe, ve)
            dmp(f"y{l}0", y)
            finish_branch(0)

            barrier()
            qTc = carve(512).rearrange("p (j s) -> p j s", j=2)
            b0 = apos[0]
            cq = carve(704).rearrange("p (t n) -> p t n", t=NT)
            cT = carve(768).rearrange("p (k s) -> p k s", k=3)
            qk = carve(512).rearrange("p (u n) -> p u n", u=16)
            rp = carve(512).rearrange("p (u n) -> p u n", u=16)
            rT = carve(256).rearrange("p (k s) -> p k s", k=1)
            c = load_cols(win, 1024, 352)
            i, pv, tok = tok_major(c, 352)
            c.free = M.last()
            e = cp(V, cq, pv, tok)
            pfree[i] = [e]
            cg_ = load_cols(win, 1376, 512)
            ig, pvg, tokg = tok_major(cg_, 256)
            held.add(ig)
            ss = sml(4)
            for t in range(NT):
                act(tmp[:, 0:192], cq[:, t, 0:192], ACT.Square, e, acc=ss[:, t:t + 1])
                act(tmp[:, 0:128], cq[:, t, 192:320], ACT.Square, acc=ss[:, 2 + t:3 + t])
            ts(V, ss[:, 0:2], ss[:, 0:2], 1.0 / 192, 1e-6, MUL, ADD, A.last())
            ts(V, ss[:, 2:4], ss[:, 2:4], 1.0 / 128, 1e-6, MUL, ADD)
            act(ss, ss, ACT.Sqrt, V.last())
            rec(ss, ss, A.last())
            for t in range(NT):
                ts(V, cq[:, t, 0:192], cq[:, t, 0:192], ss[:, t:t + 1], None, MUL, None)
                ts(V, cq[:, t, 192:320], cq[:, t, 192:320], ss[:, 2 + t:3 + t], None, MUL, None)
            i, p = ps()
            tok = tr([(p[0:m, k * 256 + t * P:k * 256 + t * P + P], cq[:, t, o:o + m], idn)
                      for k, (o, m) in enumerate(((0, 128), (128, 64), (192, 128))) for t in range(NT)],
                     V.last(), *pfree[i])
            ts(V, cT[:, 0, :], p[:, 0:256], vcol("qn", 2 * l), None, MUL, None, tok)
            ts(V, cT[0:64, 1, :], p[0:64, 256:512], vcol("qn", 2 * l + 1, slice(0, 64)), None, MUL, None)
            e = ts(V, cT[:, 2, :], p[:, 512:768], vcol("kvn", l), None, MUL, None)
            pfree[i] = [e]
            gate_of(ig, pvg, tokg, gate)
            held.remove(ig)
            i, p = ps()
            lst = []
            for h in range(4):
                j, hh = h // 2, h % 2
                o = p[64 * hh:64 * hh + 64, j * 256:(j + 1) * 256]
                lst.append((o, w_uq[l][:, 0, h * 96:h * 96 + 64], cT[:, 0, :], True, False))
                lst.append((o, w_uq[l][0:64, 1, h * 96:h * 96 + 64], cT[0:64, 1, :], False, True))
            for h in range(4):
                j, hh = h // 2, h % 2
                lst.append((p[64 * hh:64 * hh + 64, 512 + j * 256:512 + (j + 1) * 256],
                            w_ukv[l][:, h * 128:h * 128 + 64], cT[:, 2, :], True, True))
            tok = mm(lst, e, *pfree[i])
            cp(A, qT, p[:, 0:512].rearrange("p (j s) -> p j s", j=2), tok)
            e2 = cp(A, kT, p[:, 512:1024].rearrange("p (j s) -> p j s", j=2))
            pfree[i] = [e2]
            i, p = ps()
            lst = []
            wq4 = w_uq[l].rearrange("p k (h n) -> p k h n", h=4)
            wv4 = w_ukv[l].rearrange("p (h n) -> p h n", h=4)
            for t in range(NT):
                tk = slice(t * P, (t + 1) * P)
                lst.append((p[:, t * P:(t + 1) * P], cT[:, 0, tk], wq4[:, 0, :, 64:96], True, False))
                lst.append((p[:, t * P:(t + 1) * P], cT[0:64, 1, tk], wq4[0:64, 1, :, 64:96], False, True))
            for t in range(NT):
                lst.append((p[:, 512 + t * 256:512 + (t + 1) * 256], cT[:, 2, t * P:(t + 1) * P],
                            wv4[:, :, 64:128], True, True))
            tok = mm(lst, *pfree[i])
            qec = heads_T(cg_, 256, (qTc,))
            cg_.free = M.last()
            cp(V, qk[:, 0:8, :], p[:, 0:256].rearrange("p (u n) -> p u n", u=8), tok)
            ve = cp(V, v, p[:, 512:1024].rearrange("p (t n) -> p t n", t=NT))
            pfree[i] = [ve]
            for t in range(NT):
                cp(V, qk[:, 8 + 4 * t:12 + 4 * t, :], bc(cq[:, t, 320:352].unsqueeze(1), [P, 4, 32]))
            cos = tab["cos"].rearrange("p (u n) -> p u n", u=16)
            sin = tab["sin"].rearrange("p (u n) -> p u n", u=16)
            t1 = tmp[:, 0:256].rearrange("p (u n) -> p u n", u=16)
            x1, x2 = qk[:, :, 0:16], qk[:, :, 16:32]
            tt(V, rp[:, :, 0:16], x1, cos, MUL)
            tt(V, t1, x2, sin, MUL)
            tt(V, rp[:, :, 0:16], rp[:, :, 0:16], t1, SUB)
            tt(V, rp[:, :, 16:32], x1, sin, MUL)
            tt(V, t1, x2, cos, MUL)
            e = tt(V, rp[:, :, 16:32], rp[:, :, 16:32], t1, ADD)
            i, p = ps()
            rpf = rp.rearrange("p u n -> p (u n)")
            tok = tr([(p[:, k * 256 + t * P:k * 256 + t * P + P], rpf[:, (k * 2 + t) * P:(k * 2 + t + 1) * P], idn)
                      for k in range(2) for t in range(NT)], e, *pfree[i])
            cp(V, rT[:, 0, :], p[:, 0:256], tok)
            krm = tmp.rearrange("p (h s) -> p h s", h=4)
            ms(V, tmp, 0.0)
            for h in range(4):
                cp(V, krm[32 * h:32 * h + 32, h, :], p[32 * h:32 * h + 32, 256:512])
            e = V.last()
            pfree[i] = [e]
            def score_b(t):
                SL = P * (t + 1)
                tk = slice(t * P, (t + 1) * P)

                def go(p):
                    lst = []
                    for j in range(2):
                        for hh in range(2):
                            o = p[:, hh * 512 + j * SL:hh * 512 + (j + 1) * SL]
                            lst.append((o, qT[64 * hh:64 * hh + 64, j, tk], kT[64 * hh:64 * hh + 64, j, 0:SL], True, False))
                            lst.append((o, rT[:, 0, tk], krm[:, 2 * j + hh, 0:SL], False, True))
                    return lst
                return go
            attn4(score_b, 96.0 ** -0.5, lambda t: tab[f"cz{t}"], lambda h, s: v[:, s, h * 64:(h + 1) * 64],
                  y4, fill, e, e2, ve)
            dmp(f"y{l}1", y)
            finish_branch(1)
            barrier()
            apos[0] = b0

            qT_own, qT, qe = qT, qTc, qec
            kcv = carve(256)
            ksd, kwd = carve(256), carve(256)
            vs, vw = (carve(128).rearrange("p (t n) -> p t n", t=NT) for _ in range(2))
            cg = carve(24).rearrange("p (t n) -> p t n", t=NT)
            blk = carve(960).rearrange("p (q a n) -> p q a n", q=32, a=2)
            zb_ = ms(G, blk.rearrange("p q a n -> p (q a n)"), 0.0)
            hid = carve(64).rearrange("p (a n) -> p a n", a=2)
            kcd = carve(32)
            vcb = carve(256)
            ob = carve(512).rearrange("p (t n) -> p t n", t=NT)
            c = load_cols(win, 1888, 396)
            i, p = ps()
            lst = [(p[:, 0:256], c.v[:, k, 0:128], hT[:, k, :], k == 0, k == 7) for k in range(KT)]
            for n, c0 in enumerate((128, 256)):
                for hh in range(2):
                    lst += [(p[64 * hh:64 * hh + 64, 512 + n * 256:768 + n * 256], c.v[:, k, c0:c0 + 64], hT[:, k, :],
                             k == 0, k == 7) for k in range(KT)]
            tok = mm(lst, c.tok, *hTok, *pfree[i])
            cp(V, kcv, p[:, 0:256], tok)
            cp(V, ksd, p[:, 512:768])
            e = cp(V, kwd, p[:, 768:1024])
            pfree[i] = [e]
            i, p = ps()
            lst = []
            for t in range(NT):
                for c0, w, o0 in ((192, 64, 0), (320, 76, 64)):
                    lst += [(p[:, t * 512 + o0:t * 512 + o0 + w], hT[:, k, t * P:(t + 1) * P], c.v[:, k, c0:c0 + w],
                             k == 0, k == 7) for k in range(KT)]
            tok = mm(lst, *pfree[i])
            c.free = M.last()
            o = p.rearrange("p (t n) -> p t n", t=NT)
            cp(V, vs, o[:, :, 0:64], tok)
            kv_e = cp(V, vw, o[:, :, 64:128])
            act(cg, o[:, :, 128:140], ACT.Exp, V.last(), scale=-1.0)
            pfree[i] = [A.last()]
            ts(V, cg, cg, 1.0, None, ADD, None, A.last())
            rec(cg, cg)
            c = load(*[((lambda a: lambda s: s[64 * a:64 * a + 64, :].rearrange("d (q c) -> d q c", q=32))(a),
                        T["nsa_w1"][l, a].rearrange("(q d) c -> d q c", d=64)) for a in range(2)])
            w1v = c.ap.rearrange("d (q c) -> d q c", q=32)
            for q_ in range(2):
                for a in range(2):
                    h = slice(64 * a, 64 * a + 64)
                    win_ap = kcv[h, 16 * q_:16 * q_ + 240].rearrange("p (n q) -> p q n", q=16)
                    tt(V, blk[h, 16 * q_:16 * q_ + 16, a, :], win_ap,
                       bc(posT[l][h, 16 * q_:16 * q_ + 16].unsqueeze(2), [64, 16, 15]), ADD, zb_)
            i, p = ps()
            tok = mm([(p[0:30, 0:P], blk[:, q].rearrange("p a n -> p (a n)"), w1v[:, q, :], q == 0, q == 31) for q in range(32)],
                     c.tok, V.last(), *pfree[i])
            c.free = M.last()
            e = cp(V, tmp[0:30, 64:192], p[0:30, 0:P], tok)
            tok = tr([(p[:, 512:542], tmp[0:30, 64:192], idn[0:30, 0:30])], e)
            ms(V, hid, 0.0, tok)
            g1, g2 = tmp[:, 0:32].rearrange("p (a n) -> p a n", a=2), tmp[:, 32:64].rearrange("p (a n) -> p a n", a=2)
            g1, g2 = g1[:, :, 0:15], g2[:, :, 0:15]
            h15 = hid[:, :, 0:15]
            for a in range(2):
                ts(V, h15[:, a, :], p[:, 512 + a * 15:512 + a * 15 + 15], vcol("nb1", 2 * l + a), None, ADD, None)
            pfree[i] = [V.last()]
            tt(V, g1, h15, h15, MUL)
            ts(V, g1, g1, 0.044715, 1.0, MUL, ADD)
            tt(V, g1, g1, h15, MUL)
            act(g2, g1, ACT.Exp, V.last(), scale=-2.0 * 0.7978845608028654)
            ts(V, g2, g2, 1.0, None, ADD, None, A.last())
            rec(g2, g2)
            tt(V, h15, h15, g2, MUL)
            hid_ = V.last()
            y8 = y.rearrange("p t (h n) -> p (t h) n", h=4)
            o4 = ob.rearrange("p t (h n) -> p (t h) n", h=4)
            gg = [cg.rearrange("p t (h g) -> p (t h) g", g=3)[:, :, g:g + 1] for g in range(3)]
            attn4(lambda t: score_qk(qT, lambda hh, j: ksd[64 * hh:64 * hh + 64, :], t), 0.125, lambda t: tab[f"bc{t}"],
                  lambda h, s: vs[:, s, :], y4, fill, qe, kv_e)
            tt(V, y8, y8, bc(gg[1], [P, 8, 64]), MUL)
            i, p = ps()
            lst = [(p[64 * hh:64 * hh + 64, 0:32], w2n[l][:, 0, :], hid[:, 0, :], True, True) for hh in range(2)]
            lst += [(p[32 * u:32 * u + 32, 512:576], hid[:, 1, :], w2n[l][:, 1, :], True, True) for u in range(4)]
            tok = mm(lst, hid_, *pfree[i])
            ts(V, kcd, p[:, 0:32], vcol("nb2", l), None, ADD, None, tok)
            ms(V, vcb, 0.0)
            for u in range(4):
                tt(V, vcb[32 * u:32 * u + 32, u * 64:u * 64 + 64], p[32 * u:32 * u + 32, 512:576],
                   rrow("nb2v", 64, 64 * l)[32 * u:32 * u + 32], ADD)
            pfree[i] = [V.last()]
            kve = V.last()
            got = {}
            for t in (1, 0):
                tk = slice(t * P, (t + 1) * P)

                def score_c(p, tk=tk):
                    return [(p[:, hh * 512 + j * 32:hh * 512 + j * 32 + 32], qT[64 * hh:64 * hh + 64, j, tk],
                             kcd[64 * hh:64 * hh + 64, :], True, True) for j in range(2) for hh in range(2)]
                mx = scores4(t, score_c, 32, 0.125, tab[f"cm{t}"], True, qe, kve)
                got[t] = exps4(t, mx, 32, True)
            fill(2)
            for t in (1, 0):
                p4, ri, tok = got[t]
                sums4(ri, tok, True)
                i, p = ps()
                tok = tr([(p[:, 0:P], Pb[t][:, 0:P], idn)], tok, *pfree[i])
                e = cp(A, PTb[t][:, 0:P], p[:, 0:P], tok)
                pfree[i] = [e]
                i, p = ps()
                tok = mm([(p[:, 0:256], PTb[t][:, 0:P], vcb, True, True)], e, *pfree[i])
                d4 = ob[:, t, :].rearrange("p (j a n) -> p a j n", j=2, a=2)
                pfree[i] = [tt(V, d4, p[:, 0:256].rearrange("p (a j n) -> p a j n", a=2, j=2),
                               bc(ri.rearrange("p (a j) -> p a j", a=2).unsqueeze(3), [P, 2, 2, 64]), MUL, tok)]
            tt(V, o4, o4, bc(gg[0], [P, 8, 64]), MUL)
            tt(V, y8, y8, o4, ADD)
            attn4(lambda t: score_qk(qT, lambda hh, j: kwd[64 * hh:64 * hh + 64, :], t), 0.125, lambda t: tab[f"bc{t}"],
                  lambda h, s: vw[:, s, :], lambda t: ob[:, t, :].rearrange("p (h n) -> p h n", h=4), fill, qe, kv_e)
            tt(V, o4, o4, bc(gg[2], [P, 8, 64]), MUL)
            tt(V, y8, y8, o4, ADD)
            c = load_cols(win, 2284, 512)
            i, pv, tok = tok_major(c, 256)
            gate_of(i, pv, tok, gate)
            dmp(f"y{l}2", y)
            finish_branch(2)
            barrier()
            apos[0] = b0

            qT = qT_own
            sgates.append(carve(2048))
            qe = heads_T(c, 256, (qT,))
            c.free = M.last()
            c = load_cols(win, 2796, 512)
            ke = heads_T(c, 0, (kT,))
            i, pv, tok = tok_major(c, 256, 256)
            c.free = M.last()
            ve = cp(V, v, pv, tok)
            pfree[i] = [ve]
            c = load_cols(win, 3308, 256)
            i, pv, tok = tok_major(c, 256)
            c.free = M.last()
            gate_of(i, pv, tok, gate)
            zb = [carve(1024), carve(512)]
            sp = [Sb[1], Sb[0]]
            lg = [Pb[1], Pb[0]]
            for s in range(2):
                w = S - s * P
                i, p = ps()
                tok = mm([(p[:, hh * 512 + j * w:hh * 512 + (j + 1) * w], kT[64 * hh:64 * hh + 64, j, s * P:(s + 1) * P],
                           qT[64 * hh:64 * hh + 64, j, s * P:S], True, True) for j in range(2) for hh in range(2)],
                         qe, ke, *pfree[i])
                z3 = zb[s].rearrange("p (a n) -> p a n", a=2)
                e = ts(V, z3, two(p, 2 * w), 0.125, None, MUL, None, tok)
                pfree[i] = [e]
                stt(lg[s], zb[s], -1.0, zb[s], MUL, MAX)
                act(lg[s], lg[s], ACT.Exp, V.last(), scale=-1.0)
            fill(4)
            for s in range(2):
                w = S - s * P
                act(lg[s], lg[s], ACT.Ln, bias=1.0)
                e = stt(sp[s], zb[s], 0.0, lg[s], MAX, ADD, A.last())
                tt(V, zb[s], zb[s], sp[s], SUB)
                sp4 = sp[s].rearrange("p (u n) -> p u n", u=4)
                tt(V, sp4, sp4, bc(tab[f"st{s}"].unsqueeze(1), [P, 4, w]), MUL)
            merge(0)
            i, p = ps()
            lst = []
            for u in range(4):
                o = p[:, u * 256:(u + 1) * 256]
                lst.append((o, tab["upp"], sp[0][:, u * 256:(u + 1) * 256], True, False))
                lst.append((o[:, P:256], tab["one"], sp[1][:, u * P:(u + 1) * P], False, True))
            i2, p2 = ps()
            tok = mm(lst, V.last(), *pfree[i])
            tok2 = mm([(p2[:, 0:512], tab["upp"], sp[1], True, True)], *pfree[i2])
            tt(V, zb[0], zb[0], p, SUB, tok)
            pfree[i] = [V.last()]
            tt(V, zb[1], zb[1], p2[:, 0:512], SUB, tok2)
            pfree[i2] = [V.last()]
            e = V.last()
            for s in range(2):
                act(lg[s], zb[s], ACT.Exp, e)
            lgt = A.last()
            fill(2)
            merge(1)
            merge(2)
            for s in range(2):
                w = S - s * P
                l4 = lg[s].rearrange("p (u n) -> p u n", u=4)
                tt(V, l4, l4, bc(tab[f"st{s}"].unsqueeze(1), [P, 4, w]), MUL, lgt)
            i, p = ps()
            lst = []
            for t in range(NT):
                for u, h in enumerate(HORD):
                    for s in range(t + 1):
                        w = S - s * P
                        a = lg[s][:, u * w + (t - s) * P:u * w + (t - s + 1) * P]
                        lst.append((p[:, t * 512 + h * 64:t * 512 + (h + 1) * 64], a, v[:, s, h * 64:(h + 1) * 64], s == 0, s == t))
            tok = mm(lst, V.last(), *pfree[i])
            tt(V, y, two(p, 256), gate, MUL, tok)
            pfree[i] = [V.last()]
            finish_branch(3, True)
            merge(3)
            m_all = V.last()
            dmp(f"mT{l}", mT)
            cs = [load_cols(T["w_out"][l], 512 * half, 512) for half in range(2)]
            got = []
            for t in range(NT):
                i, p = ps()
                tok = mm([(p[:, 512 * half:512 * half + 512], mT[:, k, t * P:(t + 1) * P], cs[half].v[:, k, :], k == 0, k == KT - 1)
                          for half in range(2) for k in range(KT)], cs[0].tok, cs[1].tok, m_all, *pfree[i])
                got.append((t, i, p, tok))
            for c in cs:
                c.free = M.last()
            rows = rows_in(0) if l else None
            for t, i, p, tok in got:
                e = tt(V, x[:, t, :], x[:, t, :], p, ADD, tok)
                pfree[i] = [e]
                if l == 0:
                    norm_in(1, t, e)
                else:
                    final_norm(t, rows, e)
            barrier()

        def final_norm(t, rows, *w):
            r, rt = rows
            ss = sml(1)
            act(hb[:, t, :], x[:, t, :], ACT.Square, *w, acc=ss)
            rms_scale(ss, D, 1e-6, A.last())
            lnfree[0] = stt(x[:, t, :], x[:, t, :], ss, r[:, 0, :], MUL, MUL, rt)
            tile_T(t, x, hT, V.last())

        def layer_norm(src, rows, *w, tiles=(0, 1)):
            r, rt = rows
            ss = sml(2 * NT).rearrange("p (a t) -> p a t", a=2)
            ta, tb = [(V.sem, 0)] * NT, [(V.sem, 0)] * NT
            for t in tiles:
                e = stt(x[:, t, :], x[:, t, :], ALPHA, src(t), MUL, ADD, *w)
                ta[t] = act(hb[:, t, :], x[:, t, :], ACT.Copy, e, acc=ss[:, 0, t:t + 1])
            for t in tiles:
                e = ts(V, ss[:, 0, t:t + 1], ss[:, 0, t:t + 1], -1.0 / D, None, MUL, None, ta[t])
                tb[t] = act(hb[:, t, :], x[:, t, :], ACT.Square, e, bias=ss[:, 0, t:t + 1], acc=ss[:, 1, t:t + 1])
            for t in tiles:
                e = ts(V, ss[:, 1, t:t + 1], ss[:, 1, t:t + 1], 1.0 / D, 1e-5, MUL, ADD, tb[t])
                ta[t] = act(ss[:, 1, t:t + 1], ss[:, 1, t:t + 1], ACT.Sqrt, e)
            for t in tiles:
                rec(ss[:, 1, t:t + 1], ss[:, 1, t:t + 1], ta[t])
                stt(x[:, t, :], x[:, t, :], ss[:, 0, t:t + 1], r[:, 0, :], ADD, MUL, rt)
                lnfree[0] = stt(x[:, t, :], x[:, t, :], ss[:, 1, t:t + 1], r[:, 1, :], MUL, ADD)
            return V.last()

        def tile_T(t, src, dst, *w):
            i, p = ps()
            tok = tr([(p[:, k * P:(k + 1) * P], src[:, t, k * P:(k + 1) * P], idn) for k in range(KT)], *w, *pfree[i])
            d = dst[:, :, t * P:(t + 1) * P]
            pfree[i] = [cp(q, d[:, 4 * h:4 * h + 4], p[:, 512 * h:512 * h + 512].rearrange("p (k s) -> p k s", k=4), tok)
                        for h, q in enumerate((A, V))]
            return pfree[i]

        for t in range(NT):
            norm_in(0, t, X0)
        for l in range(L1):
            first_layer(l)
            if stop == f"l{l}":
                break

        def diff_attention():
            apos[0] = 0
            qT = carve(2048).rearrange("p (h s) -> p h s", h=8)
            kT = carve(2048).rearrange("p (h s) -> p h s", h=8)
            v = carve(2048).rearrange("p (t n) -> p t n", t=NT)
            o = carve(2048).rearrange("p (t n) -> p t n", t=NT)
            oT = carve(2048).rearrange("p (k s) -> p k s", k=KT)
            for buf in (Sb, Pb, PTb):
                buf[:] = [carve(512), carve(1024)]
            S2, P2 = ([carve(512), carve(1024)] for _ in range(2))

            def turn():
                for buf, other in ((Sb, S2), (Pb, P2)):
                    buf[:], other[:] = list(other), list(buf)

            tmp = carve(256)
            wq = T["attn_w_qkv_2"][0]
            xe = []
            lam = sml(4)
            for n in range(2):
                tt(V, tmp[:, 0:64], rrow("lam", 64, 128 * n), rrow("lam", 64, 128 * n + 64), MUL)
                red(lam[:, n:n + 1], tmp[:, 0:64], ADD)
            act(lam[:, 0:2], lam[:, 0:2], ACT.Exp, V.last())
            tt(V, lam[:, 2:3], lam[:, 1:2], lam[:, 0:1], SUB, A.last())
            lneg = carve(1)
            ts(V, lneg, lam[:, 2:3], 0.2, None, SUB, None)
            sub = carve(128)
            ts(V, sub, rrow("subln", 128), 0.8, None, MUL, None)
            ready = [[], []]

            def proj_qk(d, c0, half):
                c = load_cols(wq, c0 + 512 * half, 512)
                i, p = ps()
                tok = proj_T(c.v, hT, KT, [(p[:, m * 256:(m + 1) * 256], slice(m * P, (m + 1) * P)) for m in range(4)],
                             c.tok, *xe, *pfree[i])
                c.free = M.last()
                pfree[i] = [cp(A, d[:, 4 * half:4 * half + 4, :], p.rearrange("p (h s) -> p h s", h=4), tok)]
                ready[half] += pfree[i]

            def proj_v(half):
                c = load_cols(wq, 2048 + 512 * half, 512)
                i, p = ps()
                o3 = p.rearrange("p (t n) -> p t n", t=NT)
                tok = proj_tok(hT, c.v, KT, [o3[:, t, :] for t in range(NT)], slice(0, 512), c.tok, *pfree[i])
                c.free = M.last()
                pfree[i] = [cp(A, v[:, :, 512 * half:512 * half + 512], o3, tok)]

            def score(g, t):
                SL = P * (t + 1)

                def go(p):
                    return [(p[:, cc * 512 + hl * SL:cc * 512 + (hl + 1) * SL],
                             qT[64 * cc:64 * cc + 64, 2 * g + hl, t * P:(t + 1) * P],
                             kT[64 * cc:64 * cc + 64, 2 * g + hl, 0:SL], True, True)
                            for hl in range(2) for cc in range(2)]
                return go

            def front(g, t):
                SL = P * (t + 1)
                mx = scores4(t, scored.pop((g, t)), SL, 0.125, tab[f"cz{t}"], False)
                return exps4(t, mx, SL, False)

            def back(g, t, p4, ri, tok):
                SL = P * (t + 1)
                sums4(ri, tok, False)
                ts(V, ri[:, 2:4], ri[:, 2:4], lneg, None, MUL, None)
                s4 = Sb[t][:, 0:4 * SL].rearrange("p (u n) -> p u n", u=4)
                tt(V, s4, p4, bc(ri.unsqueeze(2), [P, 4, SL]), MUL)
                a = Sb[t][:, 0:2 * SL]
                e = tt(V, a, a, Sb[t][:, 2 * SL:4 * SL], ADD)
                i, p = ps()
                tok = tr([(p[:, n * P:(n + 1) * P], a[:, n * P:(n + 1) * P], idn) for n in range(2 * (t + 1))],
                         e, *pfree[i])
                pt = PTb[t][:, 0:2 * SL]
                e = cp(A, pt, p[:, 0:2 * SL], tok)
                pfree[i] = [e]
                i, p = ps()
                lst = []
                for hl in range(2):
                    for s in range(t + 1):
                        n = hl * (t + 1) + s
                        h = 2 * g + hl
                        lst.append((p[:, hl * P:(hl + 1) * P], pt[:, n * P:(n + 1) * P], v[:, s, h * P:(h + 1) * P], s == 0, s == t))
                tok = mm(lst, e, *pfree[i])
                pfree[i] = [cp(A, o[:, t, 2 * g * P:(2 * g + 2) * P], p[:, 0:256], tok)]

            units = [(g, t) for g in range(4) for t in (1, 0)]
            got = {}
            among = {0: lambda: proj_v(0), 1: lambda: proj_qk(qT, 0, 1), 2: lambda: proj_qk(kT, 1024, 1), 3: lambda: proj_v(1)}
            proj_qk(qT, 0, 0)
            proj_qk(kT, 1024, 0)
            scored = {units[0]: score_mm(score(*units[0]), *ready[0])}
            for n, un in enumerate(units):
                if n in among:
                    among[n]()
                if n + 1 < len(units):
                    nx = units[n + 1]
                    scored[nx] = score_mm(score(*nx), *ready[nx[0] // 2])
                if n and n % 2 == 0:
                    turn()
                got[un] = front(*un)
                if n > 1:
                    turn()
                    back(*units[n - 2], *got[units[n - 2]])
                    turn()
            back(*units[-2], *got[units[-2]])

            def head_norm(t):
                o8 = o[:, t, :].rearrange("p (h n) -> p h n", h=8)
                h8 = hb[:, t, :].rearrange("p (h n) -> p h n", h=8)
                ss = sml(8)
                tt(V, h8, o8, o8, MUL, A.last())
                red(ss, h8, ADD)
                rms_scale(ss, 128, 1e-5)
                tt(V, o8, o8, bc(ss.unsqueeze(2), [P, 8, 128]), MUL)
                return tt(V, o8, o8, bc(sub.unsqueeze(1), [P, 8, 128]), MUL)

            def part(t):
                def go():
                    wt = tile_T(t, o, oT, head_norm(t))
                    if t:
                        back(*units[-1], *got[units[-1]])
                    return wt
                return go

            out_proj(T["attn_w_o_2"][0], oT, 1, [(t, part(t)) for t in (1, 0)])

        def out_proj(w, srcT, lni, parts):
            cs = [load_cols(w, 512 * half, 512) for half in range(2)]
            got = []
            for t, ready in parts:
                wt = ready()
                i, p = ps()
                tok = mm([(p[:, 512 * half:512 * half + 512], srcT[:, k, t * P:(t + 1) * P], cs[half].v[:, k, :], k == 0, k == KT - 1)
                          for half in range(2) for k in range(KT)], cs[0].tok, cs[1].tok, *wt, *pfree[i])
                got.append((t, i, p, tok))
                held.add(i)
            for c in cs:
                c.free = M.last()
            rows = rows_in(lni)
            for t, i, p, tok in got:
                e = layer_norm(lambda t: p, rows, tok, tiles=(t,))
                pfree[i] = [e]
                held.remove(i)
                tile_T(t, x, hT, e)
            barrier()

        def route(l, gates, sel):
            i, p = ps()
            tok = proj_tok(hT, rw36[:, l], KT, [p[:, t * 512:t * 512 + 36] for t in range(NT)], slice(0, 36), *pfree[i])
            lo = carve(72).rearrange("p (t n) -> p t n", t=NT)
            e = tt(V, lo, two(p, 36), bc(rrow("mb", 36, 36 * l).unsqueeze(1), [P, 2, 36]), ADD, tok)
            pfree[i] = [e]
            gl, el = lo[:, :, 0:4], lo[:, :, 4:36]
            ex = carve(64).rearrange("p (t n) -> p t n", t=NT)
            eq = carve(64).rearrange("p (t n) -> p t n", t=NT)
            k1 = carve(64).rearrange("p (t n) -> p t n", t=NT)
            mx, gp, ix, m1, m2 = (carve(2) for _ in range(5))

            def col(a, n):
                return bc(a.unsqueeze(2), [P, 2, n])

            def first_of(dst, val, n, iota, m):
                tt(V, eq[:, :, 0:n], val, col(m, n), ALU.is_ge)
                ts(V, eq[:, :, 0:n], eq[:, :, 0:n], -1000.0, 1000.0, MUL, ADD)
                tt(V, eq[:, :, 0:n], eq[:, :, 0:n], bc(iota.unsqueeze(1), [P, 2, n]), ADD)
                red(ix, eq[:, :, 0:n], MIN)
                tt(V, dst, bc(iota.unsqueeze(1), [P, 2, n]), col(ix, n), ALU.is_equal)

            red(mx, gl, MAX)
            g4 = ex[:, :, 0:4]
            tt(V, g4, gl, col(mx, 4), SUB)
            act(g4, g4, ACT.Exp, V.last())
            red(gp, g4, ADD, A.last())
            rec(gp, gp)
            oh = carve(8).rearrange("p (t n) -> p t n", t=NT)
            first_of(oh, gl, 4, tab["iog"], mx)
            ts(V, oh, oh, -2 * NEG, NEG, MUL, ADD)
            oh8 = bc(oh.rearrange("p t g -> p (t g)").unsqueeze(2), [P, 8, 8])
            el8 = lambda a: a.rearrange("p t (g n) -> p (t g) n", g=4)
            em = carve(64).rearrange("p (t n) -> p t n", t=NT)
            ec = carve(64).rearrange("p (t n) -> p t n", t=NT)
            cp(V, ec, el)
            tt(V, el8(em), el8(ec), oh8, MIN)
            red(m1, em, MAX)
            o1 = k1
            first_of(o1, em, 32, tab["ioe"], m1)
            e2 = carve(64).rearrange("p (t n) -> p t n", t=NT)
            stt(e2.rearrange("p t n -> p (t n)"), o1.rearrange("p t n -> p (t n)"), 2 * NEG, em.rearrange("p t n -> p (t n)"), MUL, ADD)
            red(m2, e2, MAX)
            o2 = ex
            first_of(o2, e2, 32, tab["ioe"], m2)
            tt(V, m2, m2, m1, SUB)
            act(m2, m2, ACT.Exp, V.last())
            ts(V, m1, m2, 1.0, None, ADD, None, A.last())
            rec(m1, m1)
            tt(V, m1, m1, gp, MUL)
            tt(V, m2, m2, m1, MUL)
            tt(V, sel, o1, o2, ADD)
            tt(V, o1, o1, col(m1, 32), MUL)
            tt(V, o2, o2, col(m2, 32), MUL)
            tt(V, gates, o1, o2, ADD)

        def moe(l, lni):
            apos[0] = 0
            acc = mT.rearrange("p k s -> p (k s)").rearrange("p (t d) -> p t d", t=NT)
            gates = carve(64).rearrange("p (t n) -> p t n", t=NT)
            sel = carve(64).rearrange("p (t n) -> p t n", t=NT)
            pos = carve(64).rearrange("p (t n) -> p t n", t=NT)
            flag, flag2 = (carve(16).bitcast(mybir.dt.int32) for _ in range(2))
            io2 = carve(P)
            pad = carve(1)
            xe = [carve(1024) for _ in range(2)]
            ogT = [carve(256) for _ in range(2)]
            oh, og = carve(256), carve(256)
            scratch = apos[0]
            gu = [carve(512), carve(512)]
            hs_ = [carve(256).rearrange("p (k n) -> p k n", k=4) for _ in range(2)]
            sg = [carve(256).rearrange("p (k n) -> p k n", k=4) for _ in range(2)]
            end = apos[0]
            apos[0] = scratch
            yb = carve(1024)
            apos[0] = scratch
            hid = [carve(1024), carve(1024)]
            hm = [a[:, 0:512].rearrange("p (k n) -> p k n", k=4) for a in hid]
            xm_ = [hb[:, a, :].rearrange("p (k n) -> p k n", k=KT) for a in range(2)]
            long_ = lnr[0].rearrange("p a d -> p (a d)")
            oh2, og2, ogT2 = (long_[:, 512 * m:512 * m + 512] for m in range(3))
            oh24, og24 = (a.rearrange("p (t e n) -> p t e n", t=NT, e=2) for a in (oh2, og2))
            assert apos[0] == end
            lend([carve(SLOT) for _ in range(MORE)], [q.last() for q in (V, A, G, M)])
            apos[0] = scratch
            ms(G, acc, 0.0)
            route(l, gates, sel)
            dmp(f"g{l}", gates)
            i, p = ps()
            tok = mm([(p[:, 0:32], tab["st1"], sel[:, 0, :], True, True),
                      (p[:, 32:64], tab["st1"], sel[:, 1, :], True, False),
                      (p[:, 32:64], tab["one"], sel[:, 0, :], False, True),
                      (p[:, 64:96], tab["one"], sel[:, 0, :], True, False),
                      (p[:, 64:96], tab["one"], sel[:, 1, :], False, True)], V.last(), *pfree[i])
            ts(V, pos, sel, -1000.0, 1000.0, MUL, ADD)
            tt(V, pos, pos, p[:, 0:64].rearrange("p (t n) -> p t n", t=NT), ADD, tok)
            cnt = sml(16)
            red(cnt, p[:, 64:96].rearrange("p (q a) -> p q a", a=2), MAX)
            pfree[i] = [V.last()]
            cp(V, io2[:, 0:CAP], tab["ios"])
            ts(V, io2[:, CAP:P], tab["ios"], float(CAP), None, ADD, None)
            cnt2 = sml(16)
            ts(V, cnt2, cnt, P + 0.5, None, ALU.is_gt, None)
            cp(V, flag2, cnt2)
            ts(V, cnt, cnt, CAP + 0.5, None, ALU.is_gt, None)
            fl = cp(V, flag, cnt)
            barrier()
            pg, pt = psum[2], psum[3]
            oh4, og4 = (a.rearrange("p (t e n) -> p t e n", t=NT, e=2) for a in (oh, og))

            def places(pr, *w):
                pr = min(pr, E // 2 - 1)
                e2 = slice(2 * pr, 2 * pr + 2)
                tt(V, oh4, bc(pos[:, :, e2].unsqueeze(3), [P, 2, 2, CAP]),
                   bc(tab["ios"].unsqueeze(1).unsqueeze(1), [P, 2, 2, CAP]), ALU.is_equal, *w)
                tt(V, og4, oh4, bc(gates[:, :, e2].unsqueeze(3), [P, 2, 2, CAP]), MUL)

            def gather(pr, buf, half, *w):
                if pr == E // 2:
                    return None
                return mm([(buf[:, k * P:(k + 1) * P], x[:, t, k * P:(k + 1) * P], oh[:, t * P:(t + 1) * P], t == 0, t == 1)
                           for k in range(4 * half, 4 * half + 4) for t in range(NT)], *w)

            def gathered(pr, buf, buf2, toks):
                if pr == E // 2:
                    return
                tok2 = tr([(buf2[:, t * P:(t + 1) * P], og[:, t * P:(t + 1) * P], idn) for t in range(NT)])
                for half, q in enumerate((A, V)):
                    cp(q, xe[pr % 2][:, 512 * half:512 * half + 512], buf[:, 512 * half:512 * half + 512], toks[half])
                cp(A, ogT[pr % 2], buf2[:, 0:256], tok2)
                places(pr + 1, tok2)

            places(0)
            g_ = [gather(0, psum[0], half, V.last()) for half in range(2)]
            gathered(0, psum[0], psum[1], g_)
            for pr in range(E // 2):
                gu_c, dn_c = [], []
                for a in range(2):
                    wg = T["moe_w_gu_2"][l, 2 * pr + a]
                    gu_c.append([load_cols(wg, 0, 512), load_cols(wg, 512, 512)])
                for a in range(2):
                    dn_c.append(load_cols(T["moe_w_down_2"][l, 2 * pr + a], 0, D))
                m0 = M.n
                v_all, a_all = V.last(), A.last()
                v_in = V.ago(4) if pr else v_all
                for q in (V, A, M):
                    q.split(flag[0:1, pr:pr + 1], [fl])
                    q.split(flag2[0:1, pr:pr + 1], [])

                v_hid = []
                for a in range(2):
                    c0, c1 = gu_c[a]
                    bufs = (psum[0], psum[1]) if a else (pg, pt)
                    lst = [(dst[:, n * 256:(n + 1) * 256], c.v[:, k, n * P:(n + 1) * P], hT[:, k, :], k == 0, k == KT - 1)
                           for dst, c in zip(bufs, (c0, c1)) for n in range(4) for k in range(KT)]
                    if a == 0:
                        mm(lst[:8], c0.tok, c1.tok, v_in, a_all)
                        lst = lst[8:]
                    tok = mm(lst, c0.tok, c1.tok, v_all if a else v_in, a_all)
                    act(hid[a], bufs[0], ACT.Sigmoid, tok, V.last())
                    tt(V, hid[a], hid[a], bufs[0], MUL, A.last())
                    v_hid.append(tt(V, hid[a], hid[a], bufs[1], MUL))
                g_ = [gather(pr + 1, pg, half, v_hid[0]) for half in range(2)]
                gathered(pr + 1, pg, pt, g_)
                a_xe, v_xe = A.last(), V.last()
                for a in range(2):
                    h3 = hid[a].rearrange("p (k s) -> p k s", k=4)
                    for t in range(NT):
                        buf = (pg, pt)[t] if a else psum[t]
                        tok = mm([(buf[:, n * 512:(n + 1) * 512], h3[:, k, t * P:(t + 1) * P],
                                   dn_c[a].v[:, k, n * 512:(n + 1) * 512], k == 0, k == 3) for n in range(2) for k in range(4)],
                                 dn_c[a].tok, v_hid[1], *((a_xe, v_xe) if a else ()))
                        stt(acc[:, t, :], buf, gates[:, t, 2 * pr + a:2 * pr + a + 1], acc[:, t, :], MUL, ADD, tok)
                for _ in range(2):
                    mm([(pg[0:1, 0:1], idn[:, 0:1], idn[:, 0:1], True, True)], V.last())
                for _ in range(5):
                    act(pad[0:1], tab["one"][0:1, 0:1], ACT.Copy)

                for q in (V, A, M):
                    q.other()
                e2 = slice(2 * pr, 2 * pr + 2)
                tt(V, oh24, bc(pos[:, :, e2].unsqueeze(3), [P, 2, 2, P]),
                   bc(io2.unsqueeze(1).unsqueeze(1), [P, 2, 2, P]), ALU.is_equal)
                e = tt(V, og24, oh24, bc(gates[:, :, e2].unsqueeze(3), [P, 2, 2, P]), MUL)
                lst = [(buf[:, k * P:(k + 1) * P], x[:, t, k * P:(k + 1) * P], oh24[:, t, a, :], t == 0, t == 1)
                       for a, buf in enumerate((pg, pt)) for k in range(KT) for t in range(NT)]
                lst += [(psum[0][:, (2 * a + t) * P:(2 * a + t + 1) * P], og24[:, t, a, :], idn, True, True)
                        for a in range(2) for t in range(NT)]
                tok = mm(lst, e, v_all, a_all)
                a_x = [cp(A, xm_[a], (pg, pt)[a].rearrange("p (k n) -> p k n", k=KT), tok) for a in range(2)]
                a_og = cp(A, ogT2, psum[0][:, 0:512], tok)
                v_hm = []
                for a in range(2):
                    c0, c1 = gu_c[a]
                    buf = pg if a else psum[1]
                    lst = [(buf[:, 512 * m + n * P:512 * m + (n + 1) * P], c.v[:, k, n * P:(n + 1) * P], xm_[a][:, k, :],
                            k == 0, k == KT - 1) for m, c in enumerate((c0, c1)) for n in range(4) for k in range(KT)]
                    tok = mm(lst, c0.tok, c1.tok, a_x[a])
                    b3 = [buf[:, 512 * m:512 * m + 512].rearrange("p (k n) -> p k n", k=4) for m in range(2)]
                    act(hm[a], b3[0], ACT.Sigmoid, tok)
                    tt(V, hm[a], hm[a], b3[0], MUL, A.last())
                    v_hm.append(tt(V, hm[a], hm[a], b3[1], MUL))
                g_ = [gather(pr + 1, pt, half, a_og) for half in range(2)]
                gathered(pr + 1, pt, psum[0], g_)
                a_xe, v_xe = A.last(), V.last()
                for a, buf in enumerate((psum[1], pg)):
                    tok = mm([(buf[:, n * 512:(n + 1) * 512], hm[a][:, k, :], dn_c[a].v[:, k, n * 512:(n + 1) * 512], k == 0, k == 3)
                              for n in range(2) for k in range(4)], dn_c[a].tok, v_hm[1])
                    cp(A, hb[:, a, :], buf, tok)
                for t, buf in enumerate((psum[0], pt)):
                    tok = mm([(buf[:, n * 512:(n + 1) * 512], ogT2[:, (2 * a + t) * P:(2 * a + t + 1) * P], hb[:, a, n * 512:(n + 1) * 512],
                               a == 0, a == 1) for n in range(2) for a in range(2)], A.last(), a_xe, v_xe)
                    tt(V, acc[:, t, :], acc[:, t, :], buf, ADD, tok)
                for _ in range(2):
                    mm([(pg[0:1, 0:1], idn[:, 0:1], idn[:, 0:1], True, True)], V.last())
                for q in (V, A, M):
                    q.join()

                for q in (V, A, M):
                    q.other()
                act(pad[0:1], tab["one"][0:1, 0:1], ACT.Copy)
                xp = xe[pr % 2].rearrange("p (k n) -> p k n", k=KT)
                for a in range(2):
                    c0, c1 = gu_c[a]
                    o = pg[:, 512 * a:512 * a + 512]
                    lst = [(o[64 * m:64 * m + 64, :], xp[:, k, a * CAP:(a + 1) * CAP], c.v[:, k, :], k == 0, k == KT - 1)
                           for k in range(KT) for m, c in enumerate((c0, c1))]
                    if a == 0:
                        mm(lst[:8], c0.tok, c1.tok, v_in, a_all)
                        lst = lst[8:]
                    tok = mm(lst, c0.tok, c1.tok, v_in, a_all)
                    cp(A, gu[a], o, tok)
                toks, g_ = [], []
                for a in range(2):
                    o = psum[0][:, 512 * a:512 * a + 512]
                    toks.append(tr([(o[:, k * P:(k + 1) * P], gu[a][:, k * P:(k + 1) * P], idn) for k in range(4)], A.ago(1 - a), v_all))
                    g_.append(gather(pr + 1, pt, a))
                for a in range(2):
                    o4 = psum[0][:, 512 * a:512 * a + 512].rearrange("p (k n) -> p k n", k=4)
                    act(sg[a], o4[:, :, 0:64], ACT.Sigmoid, toks[a])
                    tt(V, sg[a], sg[a], o4[:, :, 0:64], MUL, A.last())
                    tt(V, hs_[a], sg[a], o4[:, :, 64:128], MUL)
                v_hs = V.last()
                gathered(pr + 1, pt, psum[1], g_)
                for n in range(2):
                    h = slice(n * 512, (n + 1) * 512)
                    tok = mm([(pg[64 * a:64 * a + 64, h], hs_[a][:, k, :], dn_c[a].v[:, k, h], k == 0, k == 3)
                              for k in range(4) for a in range(2)], dn_c[0].tok, dn_c[1].tok, v_hs)
                    cp(A, yb[:, h], pg[:, h], tok)
                for n in range(2):
                    h = slice(n * 512, (n + 1) * 512)
                    tok = mm([(psum[n][:, 512 * t:512 * t + 512], ogT[pr % 2][:, t * P:(t + 1) * P], yb[:, h], True, True)
                              for t in range(NT)], A.ago(1 - n))
                    for t in range(NT):
                        tt(V, acc[:, t, h], acc[:, t, h], psum[n][:, 512 * t:512 * t + 512], ADD, tok)
                for q in (V, A, M):
                    q.join()
                for a in range(2):
                    for c in gu_c[a]:
                        c.free = (M.sem, m0 + 2 + a)
                    dn_c[a].free = M.last()
            give_back()
            for k in range(4):
                pfree[k] = [V.last(), A.last()]
            dmp(f"moe{l}", acc)
            lnfree[0] = V.last()
            layer_norm(lambda t: acc[:, t, :], rows_in(lni))
            barrier()

        def rwkv():
            apos[0] = 0

            def big():
                return carve(2048).rearrange("p (k s) -> p k s", k=KT)

            def flat(a):
                return a.rearrange("p k s -> p (k s)")

            rT, kT, kk, aT, Lc = (big() for _ in range(5))
            vt = carve(2048).rearrange("p (t n) -> p t n", t=NT)
            gt = carve(2048).rearrange("p (t n) -> p t n", t=NT)
            bon = carve(32).rearrange("p (t h) -> p t h", t=NT)
            pc = carve(32).rearrange("p (k c) -> p k c", k=KT)
            st = carve(512).rearrange("p (k n) -> p k n", k=KT)
            mark = apos[0]
            xx, xa_, lw = (big() for _ in range(3))
            xb_, xc_ = mT, hb.rearrange("p t d -> p (t d)").rearrange("p (k s) -> p k s", k=KT)
            loT, om = carve(256), carve(8)
            xe = to_T(x, hT, V.last())
            ts(V, xx[:, :, 0:1], hT[:, :, 0:1], -1.0, None, MUL, None, *xe)
            tt(V, xx[:, :, 1:S], hT[:, :, 0:S - 1], hT[:, :, 1:S], SUB)

            def mix(i, dst, *w):
                for k in range(KT):
                    tok = stt(dst[:, k, :], xx[:, k, :], vcol("mu", 8 * i + k), hT[:, k, :], MUL, ADD, *w)
                return tok

            def proj(n, xw, src, d):
                for half in range(2):
                    c = load_cols(T["rw_w_rkv_2"][0, n], 512 * half, 512)
                    i, p = ps()
                    tok = proj_T(c.v, src, KT, [(p[:, m * 256:(m + 1) * 256], slice(m * P, (m + 1) * P)) for m in range(4)],
                                 c.tok, xw, *pfree[i])
                    c.free = tok
                    pfree[i] = [cp(A, d[:, 4 * half:4 * half + 4, :], p.rearrange("p (k s) -> p k s", k=4), tok)]
                return tok

            xk, xw, xa = mix(1, xa_), mix(3, xb_), mix(4, xc_)
            tk_ = proj(1, xk, xa_, kT)
            c = load((cols(288), T["lora1"].rearrange("(k p) n -> p k n", p=P)))
            lv = c.ap[:, 0:KT * 288].rearrange("p (k n) -> p k n", k=KT)
            c2 = load((lambda s: s[:, 0:1024], T["lora2"]), (lambda s: s[:, 1024:2048], T["rw_g2_2"][0, 0:128]),
                      (lambda s: s[0:32, 2048:3072], T["rw_g2_2"][0, 128:160]))
            lora2, g2a, g2b = c2.ap[:, 0:1024], c2.ap[:, 1024:2048], c2.ap[0:32, 2048:3072]
            i, p = ps()
            tw = mm([(p[0:64, 0:256], lv[:, k, 0:64], xb_[:, k, :], k == 0, k == 7) for k in range(KT)], c.tok, xw, *pfree[i])
            ta = mm([(p[64:128, 512:768], lv[:, k, 64:128], xc_[:, k, :], k == 0, k == 7) for k in range(KT)], xa)
            act(loT[0:64], p[0:64, 0:256], ACT.Tanh, tw)
            e = cp(A, loT[64:128], p[64:128, 512:768], ta)
            pfree[i] = [e]
            for k in range(KT):
                tkk = act(kk[:, k, :], kT[:, k, :], ACT.Copy, scale=vcol("kk", k))
            xr = mix(0, xa_, tk_)
            for base, dst, bias in ((0, lw, "w0"), (64, aT, "a0")):
                for half in range(2):
                    i, p = ps()
                    tok = mm([(p[:, n * 256:(n + 1) * 256], lora2[base:base + 64, (4 * half + n) * P:(4 * half + n + 1) * P],
                               loT[base:base + 64, :], True, True) for n in range(4)], e, c2.tok, *pfree[i])
                    for n in range(4):
                        t_ = act(dst[:, 4 * half + n, :], p[:, n * 256:(n + 1) * 256], ACT.Sigmoid, tok,
                                 bias=vcol(bias, 4 * half + n))
                    pfree[i] = [t_]
            g_, v_ = gt.rearrange("p t n -> p (t n)"), vt.rearrange("p t n -> p (t n)")
            sq3, ka3 = (a.rearrange("p (k s) -> p k s", k=KT) for a in (g_, v_))
            tq = tt(V, g_, flat(kk), flat(kk), MUL, tkk)
            xg = mix(5, xb_, tw)
            xv = mix(2, xc_, ta)
            ts(V, om, vec[:, VO["ka"]:VO["ka"] + 8], -1.0, 1.0, MUL, ADD)
            for k in range(KT):
                ts(V, ka3[:, k, :], aT[:, k, :], vcol("ka", k), om[:, k:k + 1], MUL, ADD, t_)
            tt(V, flat(kT), v_, flat(kT), MUL)
            for k in range(KT):
                V.add(lambda e, k=k: e.tensor_tensor_scan(Lc[:, k, :], tab["rst"], lw[:, k, :], 0.0, MUL, ADD))
            dec = -math.exp(-0.5)
            t1 = tt(V, flat(lw), flat(Lc), flat(lw), SUB)
            tr_ = proj(0, xr, xa_, rT)
            tr_e = A.last()
            i, p = ps()
            tok = mm([(p[32 * (k % 4):32 * (k % 4) + 32, 512 * (k // 4):512 * (k // 4) + 256], tab["hnd32"], sq3[:, k, :], True, True)
                      for k in range(KT)], tq, *pfree[i])
            ln = xx[:, 0:2, :]
            ts(V, ln, two(p, 256), 1e-24, None, MAX, None, tok)
            pfree[i] = [V.last()]
            act(ln, ln, ACT.Sqrt, V.last())
            tl = rec(ln, ln, A.last())
            i, p = ps()
            lst = [(p[:, 0:256], lv[:, k, 128:256], xb_[:, k, :], k == 0, k == 7) for k in range(KT)]
            lst += [(p[0:32, 256:512], lv[:, k, 256:288], xb_[:, k, :], k == 0, k == 7) for k in range(KT)]
            tg = tok = mm(lst, xg, *pfree[i])
            c.free = M.last()
            sg = xx[:, 2:4, :]
            act(sg[:, 0, :], p[:, 0:256], ACT.Sigmoid, tok, xv)
            e = act(sg[0:32, 1, :], p[0:32, 256:512], ACT.Sigmoid)
            pfree[i] = [e]
            e1 = act(v_, flat(Lc), ACT.Exp, t1, scale=dec)
            e3 = act(flat(xb_), flat(Lc), ACT.Exp, tg, scale=-dec)
            e2 = act(flat(lw), flat(lw), ACT.Exp, scale=dec)
            kk4 = kk.rearrange("p (h n) s -> p n h s", h=2)
            for n0 in range(0, 4, 2):
                i, p = ps()
                tok = mm([(p[:, n * 512 + half * 256:n * 512 + half * 256 + 256], tab["dnh"][32 * (n0 + n):32 * (n0 + n) + 32, :],
                           ln[32 * (n0 + n):32 * (n0 + n) + 32, half, :], True, True) for half in range(2) for n in range(2)],
                         tl, *pfree[i])
                pfree[i] = [tt(V, kk4[:, n0:n0 + 2], kk4[:, n0:n0 + 2], p.rearrange("p (n h s) -> p n h s", n=2, h=2), MUL, tok)]
            for k in range(KT):
                stt(xa_[:, k, :], rT[:, k, :], vcol("rk", k), kT[:, k, :], MUL, MUL, tr_, tr_e)
            tbon = V.last()
            tt(V, flat(rT), flat(rT), v_, MUL, e1)
            t_v = cp(V, pc, ka3.rearrange("p k (c s) -> p k c s", c=4)[:, :, :, 63])
            tt(V, flat(aT), flat(aT), flat(kk), MUL)
            tt(V, flat(kT), flat(kT), flat(xb_), MUL, e3)
            tt(V, flat(aT), flat(aT), flat(xb_), MUL)
            stt(flat(kk), flat(kk), -1.0, flat(lw), MUL, MUL, e2)
            for t in range(NT):
                i, p = ps()
                tok = mm([(p[:, n * 512:(n + 1) * 512], a[:, t * P:(t + 1) * P], b[:, n * 512:(n + 1) * 512], a is not sgb, a is sgb)
                          for n in range(2) for sgb in (sg[0:32, 1, :],) for a, b in ((sg[:, 0, :], g2a), (sgb, g2b))],
                         e, *pfree[i])
                pfree[i] = [cp(A, gt[:, t, :], p, tok)]
            c2.free = M.last()
            i, p = ps()
            tok = mm([(p[:, t * 512 + 2 * k:t * 512 + 2 * k + 2], xa_[:, k, t * P:(t + 1) * P], tab["hnd"], True, True)
                      for t in range(NT) for k in range(KT)], tbon, *pfree[i])
            pfree[i] = [cp(V, bon, two(p, 16), tok)]
            for half in range(2):
                c = load_cols(T["rw_w_rkv_2"][0, 2], 512 * half, 512)
                i, p = ps()
                o3 = p.rearrange("p (t n) -> p t n", t=NT)
                tok = proj_tok(xc_, c.v, KT, [o3[:, t, :] for t in range(NT)], slice(0, 512), c.tok, xv, *pfree[i])
                c.free = M.last()
                pfree[i] = [cp(A, vt[:, :, 512 * half:512 * half + 512], o3, tok, t_v)]
            spare_k = [order.pop(0) for _ in range(3)]
            spare = [ring[k] for k in spare_k]
            for k in spare_k[0:2]:
                zero = ms(G, ring[k], 0.0, lambda old=rwait[k]: old.free)
            barrier()
            bT, aa = aT, kk
            apos[0] = mark

            def u3(a):
                return a.rearrange("p (u n) -> p u n", n=64)

            def half_of(a, c):
                return a.rearrange("p (u c n) -> p c u n", c=2, n=64)[64 * c:64 * c + 64, c]

            def rows_of(a, c):
                return u3(a)[64 * c:64 * c + 64]

            hbf = hb.rearrange("p t d -> p (t d)")
            own = carve(5120)
            lf, hf, mf = flat(Lc), flat(hT), flat(mT)
            ones = [own[:, 1024 * m:1024 * m + 1024] for m in range(5)]
            ones.append(lnr[0][:, 0, :])
            stb = carve(1024)
            B = []
            for t in range(NT):
                d = {"nd": (hbf if t else spare[2][:, 0:2048]), "P": (hf if t else spare[2][:, 2048:4096]), "Q": (mf if t else lf)}
                for two_, names in (("nd", "ND"), ("P", "nY"), ("Q", "dX")):
                    for m in range(2):
                        d[names[m]] = d[two_][:, 1024 * m:1024 * m + 1024]
                for k in ("rb", "rk", "ak"):
                    d[k] = ones.pop(0)
                B.append(d)
            bd = [spare[m // 2][:, 2048 * (m % 2):2048 * (m % 2) + 2048] for m in range(4)]
            ms(V, st.rearrange("p k n -> p (k n)"), 0.0)
            ms(V, stb, 0.0)

            def mask(k, parts=slice(0, P)):
                return bc(tab[k][parts].unsqueeze(1), [parts.stop - parts.start, 16, 64])

            def spread(q, dst, src, t, *w):
                d5 = dst.rearrange("p (k c a n) -> p a k c n", k=KT, c=2, a=2)
                for hh in range(2):
                    h = slice(64 * hh, 64 * hh + 64)
                    tok = cp(q, d5[h, hh], src[h, :, t * P:(t + 1) * P].rearrange("p k (c n) -> p k c n", c=2), *w)
                return tok

            def pair(dst, lhs, rhs, t, m, *w):
                i, p = ps()
                r4 = rhs.rearrange("p (k c n) -> p k c n", k=KT, c=2)
                tok = mm([(p[64 * c:64 * c + 64, k * P:(k + 1) * P], lhs[:, k, t * P + 64 * c:t * P + 64 * c + 64],
                           r4[:, k, c, :], True, True) for k in range(KT) for c in range(2)], *w, *pfree[i])
                pfree[i] = [tt(V, u3(dst), u3(p), mask(m), MUL, tok)]
                return tok

            free = [zero] * 4
            place = (dict(a=0, b=2, r=1), dict(a=3, b=0, r=2))
            for t in range(NT):
                d, pl = B[t], place[t]
                ta = spread(A, bd[pl["a"]], aa, t, free[pl["a"]])
                tb = spread(A, bd[pl["b"]], bT, t, free[pl["b"]])
                t_r = spread(V, bd[pl["r"]], rT, t, free[pl["r"]])
                pair(d["N"], bT, bd[pl["a"]], t, "mlt", ta)
                free[pl["a"]] = pair(d["ak"], kT, bd[pl["a"]], t, "mlt")
                free[pl["b"]] = pair(d["D"], aa, bd[pl["b"]], t, "mgt", tb)
                pair(d["rb"], bT, bd[pl["r"]], t, "mle", t_r)
                free[pl["r"]] = pair(d["rk"], kT, bd[pl["r"]], t, "mle")
            for t in range(NT):
                d = B[t]
                d["nb"], d["db"] = (bd[1], bd[3]) if t == 0 else (bd[0], bd[2])
                fr = (free[1], free[3]) if t == 0 else (free[0], free[2])
                for src, dst, one, m, big_, f in ((d["N"], d["n"], d["Y"], "m16", d["nb"], fr[0]),
                                                  (d["D"], d["d"], d["X"], "n16", d["db"], fr[1])):
                    tok = tt(V, u3(dst), u3(src), mask(m), MUL)
                    for c in range(2):
                        tok2 = cp(A, half_of(big_, c), rows_of(dst, c), tok, f)
                    tt(V, u3(one), u3(dst), mask("i64"), ADD)
                d["bd"] = tok2
                d["st"] = V.last()

            def prod(lhs, rhs, g, *w):
                i, p = ps()
                r4 = rhs.rearrange("p (m u n) -> p u m n", m=2, n=64)
                o4 = p.rearrange("p (u m n) -> p u m n", m=2, n=64)
                tok = mm([(o4[:, u - 8 * g], lhs[:, u * P:(u + 1) * P], r4[:, u], True, True)
                          for u in range(8 * g, 8 * g + 8)], *w, *pfree[i])
                return i, p.rearrange("p (u m n) -> p m u n", m=2, n=64), tok

            for step in range(4):
                for t in range(NT):
                    d = B[t]
                    w = [d["bd"], d["st"]]
                    for g in range(2):
                        us = slice(8 * g, 8 * g + 8)
                        got = [prod(d["db"], d["P"], g, *w), prod(d["nb"], d["Q"], g)]
                        both = got[1][2]
                        for (i, p, tok), pw, inv, big_ in zip(got, "nd", "YX", ("nb", "db")):
                            if step < 3:
                                tn = cp(V, u3(d[pw])[:, us], p[:, 0], tok)
                            if step:
                                tn_ = tt(V, u3(d[inv])[:, us], u3(d[inv])[:, us], p[:, 1], ADD, tok)
                            d["st"] = V.last()
                            pfree[i] = [V.last()]
                            if step < 3:
                                for c in range(2):
                                    d["bd"] = cp(A, half_of(d[big_], c)[:, us], rows_of(d[pw], c)[:, us], tn, both)
                            else:
                                d["bd"] = both
            for mn, md in (("m32", "n32"), (None, "n64")):
                for t in range(NT):
                    d = B[t]
                    for c in range(2):
                        h = slice(64 * c, 64 * c + 64)
                        tt(V, half_of(d["db"], c), rows_of(d["D"], c), mask(md, h), MUL, d["bd"])
                        if mn:
                            tt(V, half_of(d["nb"], c), rows_of(d["N"], c), mask(mn, h), MUL)
                    d["m"] = V.last()
                for t in range(NT):
                    d = B[t]
                    w = [d["m"], d["st"]]
                    for g in range(2):
                        us = slice(8 * g, 8 * g + 8)
                        i, p, tok = prod(d["db"], d["P"], g, *w)
                        pfree[i] = [cp(V, u3(d["n"])[:, us], p[:, 1], tok)]
                        for c in range(2):
                            d["b"] = cp(A, half_of(d["db"], c)[:, us], rows_of(d["X"], c)[:, us], tok)
                        if mn:
                            i, p, tok = prod(d["nb"], d["Q"], g)
                            pfree[i] = [cp(V, u3(d["d"])[:, us], p[:, 1], tok)]
                            for c in range(2):
                                d["b"] = cp(A, half_of(d["nb"], c)[:, us], rows_of(d["Y"], c)[:, us], tok)
                        d["c"] = V.last()
                for t in range(NT):
                    d = B[t]
                    got = []
                    for g in range(2):
                        us = slice(8 * g, 8 * g + 8)
                        got = [("Y",) + prod(d["db"], d["P"], g, d["b"], d["c"])]
                        if mn:
                            got.append(("X",) + prod(d["nb"], d["Q"], g))
                        for inv, i, p, tok in got:
                            pfree[i] = [tt(V, u3(d[inv])[:, us], u3(d[inv])[:, us], p[:, 0], ADD, tok)]
                    d["st"], d["bd"] = V.last(), M.last()
            for t in range(NT):
                d = B[t]
                d["mv"], d["U"], d["btok"], d["ktok"] = d["n"], d["X"], d["d"], bd[t][:, 0:1024]
                for src, dst in ((bT, d["btok"]), (kT, d["ktok"])):
                    i, p = ps()
                    tok = tr([(p[:, k * P:(k + 1) * P], src[:, k, t * P:(t + 1) * P], idn) for k in range(KT)],
                             V.last(), A.last(), *pfree[i])
                    pfree[i] = [cp(A, dst, p, tok)]

            def blk_(a, c, u):
                return a[64 * c:64 * c + 64, u * 64:(u + 1) * 64]

            for t in range(NT):
                d = B[t]
                i, p = ps()
                tok = mm([(blk_(p, c, u), blk_(d["ak"], c, u), blk_(vt[:, t, :], c, u), True, True)
                          for u in range(16) for c in range(2)], V.last(), *pfree[i])
                pfree[i] = [cp(V, d["mv"], p, tok)]
            lnfree[0] = V.last()
            barrier()
            s3 = stb.rearrange("p (k a n) -> p k a n", k=KT, a=2)
            r, rtok = rows_in(4)

            def norm_ops(t):
                y = hb[:, t, :]
                h16 = y.rearrange("p (h n) -> p h n", h=16)
                sq = B[0]["ak"]
                s16 = sq.rearrange("p (h n) -> p h n", h=16)
                mu, va = carve(16), carve(16)

                def wide(a):
                    return bc(a.unsqueeze(2), [P, 16, 64])

                def last():
                    lnfree[0] = tt(V, y, y, r[:, 1, :], ADD)

                return [lambda: red(mu, h16, ADD), lambda: ts(V, mu, mu, 1.0 / 64, None, MUL, None),
                        lambda: tt(V, h16, h16, wide(mu), SUB), lambda: tt(V, sq, y, y, MUL), lambda: red(va, s16, ADD),
                        lambda: rms_scale(va, 64, 64e-5), lambda: tt(V, h16, h16, wide(va), MUL),
                        lambda: tt(V, y, y, r[:, 0, :], MUL, rtok), last,
                        lambda: tt(V, s16, vt[:, t, :].rearrange("p (h n) -> p h n", h=16), wide(bon[:, t, :]), MUL),
                        lambda: tt(V, y, y, sq, ADD), lambda: tt(V, y, y, gt[:, t, :], MUL)]

            norms = [norm_ops(t) for t in range(NT)]

            def some(t, n):
                for _ in range(n if t else 0):
                    if norms[0]:
                        norms[0].pop(0)()

            v_s = a_s = None
            for t in range(NT):
                d, v_, y = B[t], vt[:, t, :], hb[:, t, :]
                mv, U = d["mv"], d["U"]
                for c in range(2):
                    rows = slice(64 * c, 64 * c + 64)
                    tk = slice(t * P + 64 * c, t * P + 64 * c + 64)
                    i, p = ps()
                    tok = mm([(p[rows, k * P:(k + 1) * P], aa[:, k, tk], stb[:, k * P:(k + 1) * P], True, True)
                              for k in range(KT)], v_s, a_s, *pfree[i])
                    i2, p2 = ps()
                    tok2 = mm([(p2[rows, k * P:(k + 1) * P], rT[:, k, tk], stb[:, k * P:(k + 1) * P], True, True)
                               for k in range(KT)], *pfree[i2])
                    pfree[i] = [tt(V, mv[rows], mv[rows], p[rows], ADD, tok)]
                    v_mv = V.last()
                    pfree[i2] = [cp(A, y[rows], p2[rows], tok2)]
                    a_y = A.last()
                    some(t, 1)
                    i2, p2 = ps()
                    so = [(p2[64 * (u % 2):64 * (u % 2) + 64, (u // 2) * 64:(u // 2 + 1) * 64], u) for u in range(16)]
                    mm([(o, blk_(d["ktok"], c, u), blk_(v_, c, u), u < 2, False) for o, u in so], *pfree[i2])
                    i, p = ps()
                    tok = mm([(blk_(p, c, u), blk_(d["Y"], c, u), blk_(mv, c, u), True, True) for u in range(16)],
                             v_mv, *pfree[i])
                    pfree[i] = [cp(V, U[rows], p[rows], tok)]
                    v_u = V.last()
                    some(t, 3)
                    i, p = ps()
                    mm([(blk_(p, c, u), blk_(d["rk"], c, u), blk_(v_, c, u), u % 8 == 0, False) for u in range(16)], *pfree[i])
                    tok2 = mm([(o, blk_(d["btok"], c, u), blk_(U, c, u), False, True) for o, u in so], v_u)
                    s2 = st.rearrange("p k n -> p (k n)")
                    tt(V, s2, s2, p2[:, 0:512], ADD, tok2)
                    pfree[i2] = [V.last()]
                    e = tt(V, st, st, bc(pc[:, :, 2 * t + c:2 * t + c + 1], [P, 8, 64]), MUL)
                    cp(A, s3[64:128, :, 1], st[64:128], e)
                    v_s = cp(V, s3[0:64, :, 0], st[0:64])
                    a_s = A.last()
                    some(t, 2)
                    tok = mm([(blk_(p, c, u), blk_(d["rb"], c, u), blk_(U, c, u), False, True) for u in range(16)])
                    pfree[i] = [tt(V, y[rows], y[rows], p[rows], ADD, tok, a_y)]
                for k in spare_k[:2] if t else spare_k[2:]:
                    rwait[k] = [V.last(), A.last(), M.last()]
                    order.append(k)
            dmp("wkv", hb)
            def part(t):
                def go():
                    for f in norms[t]:
                        f()
                    return tile_T(t, hb, kT, V.last())
                return go

            out_proj(T["rw_w_o_2"][0], kT, 3, [(t, part(t)) for t in range(NT)])

        s_o = sem("s_o")
        if stop is None or stop[0] != "l":
            dmp("x1", x)
            if stop != "fn":
                diff_attention()
                dmp("xa", x)
                if stop != "da":
                    if stop != "rw":
                        moe(0, 2)
                        dmp("xm0", x)
                    if stop != "m0":
                        rwkv()
                        dmp("xr", x)
                        if stop != "rw":
                            moe(1, 5)
        A.dma(out.rearrange("b (t p) d -> p (b t) d", p=P), x, s_o, [V.last()])
        A.items.append((lambda e: None, [(s_o, 16)], None, 0))
        for d in dumps:
            A.items.append((lambda e: None, [d], None, 0))

        block = ctx.enter_context(nc.Block())

        @block.sync
        def _(eng):
            W.emit(eng)

        @block.gpsimd
        def _(eng):
            G.emit(eng)

        @block.scalar
        def _(eng):
            A.emit(eng)

        @block.tensor
        def _(eng):
            M.emit(eng)

        @block.vector
        def _(eng):
            V.emit(eng)


_VECS = (("norm_g", 16), ("qn", 4), ("kvn", 2), ("nb1", 4), ("nb2", 2), ("bm", 64), ("mu", 48), ("w0", 8), ("a0", 8),
         ("kk", 8), ("ka", 8), ("rk", 8))
_ROWS = (("subln", 128), ("lam", 256), ("mb", 72), ("nb2v", 128))


def vec_layout():
    o, out = 0, {}
    for n, w in _VECS:
        out[n] = o
        o += w
    return out


def row_layout():
    o, out = 0, {}
    for n, w in _ROWS:
        out[n] = o
        o += w
    return out


def layout(i):
    def colmaj(a):
        return np.ascontiguousarray(a.reshape(-1, P).T)

    tabs = tables()
    qn = np.zeros((L1, 256), np.float32)
    qn[:, :192] = i["mla_q_norm"]
    v = {
        "norm_g": colmaj(i["norm_g"]), "qn": colmaj(qn), "kvn": colmaj(i["mla_kv_norm"]), "nb1": colmaj(i["nsa_b1"]),
        "nb2": colmaj(np.concatenate([i["nsa_b2"][:, 0], i["nsa_b2"][:, 0]], axis=1)), "bm": colmaj(i["b_merge"]),
        "mu": colmaj(i["rw_mu_2"]), "w0": colmaj(i["rw_w0_2"]), "a0": colmaj(i["rw_a0_2"]), "kk": colmaj(i["rw_k_k_2"]),
        "ka": colmaj(i["rw_k_a_2"]), "rk": colmaj(i["rw_r_k_2"]),
    }
    r = {
        "subln": i["attn_subln_g_2"].reshape(-1), "lam": i["attn_lambda_2"].reshape(-1),
        "mb": np.concatenate([i["moe_rg_b_2"], i["moe_re_b_2"]], axis=1).reshape(-1), "nb2v": i["nsa_b2"][:, 1].reshape(-1),
    }
    vecs = np.concatenate([v[n] for n, _ in _VECS], axis=1)
    rows = np.tile(np.concatenate([r[n] for n, _ in _ROWS])[None], (P, 1))
    pairs = [(i["final_norm_g"], i["final_norm_g"])]
    pairs += [(i["ln1_g_2"][0], i["ln1_b_2"][0]), (i["ln2_g_2"][0], i["ln2_b_2"][0]), (i["ln1_g_2"][1], i["ln1_b_2"][1]),
              (i["rw_lnx_g_2"][0], i["rw_lnx_b_2"][0]), (i["ln2_g_2"][1], i["ln2_b_2"][1])]
    lrows = np.stack([np.tile(np.stack(p)[None], (P, 1, 1)) for p in pairs])
    common = [k for k in tabs if k not in FIRST_TABLES and k[0:2] != "cz"]
    arrays = {
        "x": i["x"], "vecs": vecs, "rows": rows, "lrows": lrows,
        "tcom": np.concatenate([tabs[k] for k in common], axis=1),
        "tfirst": np.concatenate([tabs[k] for k in FIRST_TABLES], axis=1),
        "cz0": tabs["cz0"], "cz1": tabs["cz1"],
        "pos": i["nsa_pos"].transpose(0, 1, 3, 2).reshape(L1, P, 32),
        "wr": np.concatenate([i["moe_rg_w_2"], i["moe_re_w_2"]], axis=2),
        "lora1": np.concatenate([i["rw_w1_2"][0], i["rw_a1_2"][0], i["rw_g1_2"][0]], axis=1),
        "lora2": np.concatenate([i["rw_w2_2"][0], i["rw_a2_2"][0]], axis=0),
    }
    for n in ("w_in", "mla_w_uq", "mla_w_ukv", "nsa_w1", "nsa_w2", "w_branch", "w_merge", "w_out", "attn_w_qkv_2",
              "attn_w_o_2", "rw_w_rkv_2", "rw_w_o_2", "rw_g2_2", "moe_w_gu_2", "moe_w_down_2"):
        arrays[n] = i[n]
    return {k: np.ascontiguousarray(a) for k, a in arrays.items()}


def kernel(**inputs):
    import concourse.bacc as bacc
    from concourse.bass_utils import run_bass_kernel_spmd

    arrays = layout({k: np.asarray(a) for k, a in inputs.items()})
    nc = bacc.Bacc("TRN2", target_bir_lowering=False, num_devices=1)
    T = {k: nc.dram_tensor(f"in_{k}", a.shape, mybir.dt.from_np(a.dtype), kind="ExternalInput").ap() for k, a in arrays.items()}
    out = nc.dram_tensor("out", (1, S, D), F, kind="ExternalOutput").ap()
    program(nc, T, out)
    r = run_bass_kernel_spmd(nc, [{f"in_{k}": a for k, a in arrays.items()}], core_ids=[0])
    return r.results[0]["out"]
```
